# Optimizing a Trainium2 kernel written in Bass

```python
import jax, jax.numpy as jnp
from jax import lax
import numpy as np

D_MODEL = 1024
BATCH = 1
SEQ = 256
DEPTH = 1

NORM_EPS = 1e-5
GLA_HEADS = 4
GLA_DK = 128
GLA_DV = 256
GLA_GATE_RANK = 16
GLA_TAU = 16.0
GLA_CHUNK = 64
SWA_Q_HEADS = 16
SWA_KV_HEADS = 2
SWA_GROUP = SWA_Q_HEADS // SWA_KV_HEADS
SWA_HEAD_DIM = 64
SWA_WINDOW = 128
ROPE_THETA = 10000.0
N_EXPERTS = 32
TOP_K = 4
D_FF = D_MODEL
SWIGLU_LIMIT = 7.0
SWIGLU_ALPHA = 1.702
MOE_BLOCK = 256

SPLIT_SIZES = (
    GLA_HEADS * GLA_DK,
    GLA_HEADS * GLA_DK,
    GLA_HEADS * GLA_DV,
    GLA_HEADS * GLA_DV,
    GLA_GATE_RANK,
    SWA_Q_HEADS * SWA_HEAD_DIM,
    SWA_KV_HEADS * SWA_HEAD_DIM,
    SWA_KV_HEADS * SWA_HEAD_DIM,
    D_MODEL,
    D_MODEL,
)
D_IN = sum(SPLIT_SIZES)

kernel_name = "hybrid_gla_swa_sink_moe"

def rms_norm(x, g):
    xf = x.astype(jnp.float32)
    y = xf * lax.rsqrt(jnp.mean(xf * xf, axis=-1, keepdims=True) + NORM_EPS)
    return (y * g.astype(jnp.float32)).astype(x.dtype)

def rope(x, pos):
    half = x.shape[-1] // 2
    inv_freq = ROPE_THETA ** (-jnp.arange(half, dtype=jnp.float32) / half)
    ang = pos.astype(jnp.float32)[:, None] * inv_freq[None, :]
    cos = jnp.cos(ang)[None, :, None, :]
    sin = jnp.sin(ang)[None, :, None, :]
    xf = x.astype(jnp.float32)
    x1, x2 = xf[..., :half], xf[..., half:]
    return jnp.concatenate([x1 * cos - x2 * sin, x2 * cos + x1 * sin], axis=-1).astype(x.dtype)

def gla_chunked(q, k, v, log_g):
    bsz, s, h, dk = q.shape
    dv = v.shape[-1]
    c = GLA_CHUNK
    n = s // c

    def to_chunks(t):
        return t.astype(jnp.float32).reshape(bsz, n, c, h, t.shape[-1]).transpose(1, 0, 3, 2, 4)

    qc = to_chunks(q) * (GLA_DK ** -0.5)
    kc, vc, gc = to_chunks(k), to_chunks(v), to_chunks(log_g)
    causal = jnp.tril(jnp.ones((c, c), dtype=bool))

    def step(state, inp):
        q_c, k_c, v_c, g_c = inp
        b = jnp.cumsum(g_c, axis=-2)
        diff = b[..., :, None, :] - b[..., None, :, :]
        decay = jnp.exp(jnp.where(causal[:, :, None], diff, -jnp.inf))
        scores = jnp.einsum('bhtsd,bhsd->bhts', q_c[..., :, None, :] * decay, k_c)
        o = (jnp.einsum('bhts,bhsv->bhtv', scores, v_c)
             + jnp.einsum('bhtd,bhdv->bhtv', q_c * jnp.exp(b), state))
        b_last = b[..., -1:, :]
        state = (jnp.exp(b_last[..., 0, :])[..., None] * state
                 + jnp.einsum('bhsd,bhsv->bhdv', k_c * jnp.exp(b_last - b), v_c))
        return state, o

    state0 = jnp.zeros((bsz, h, dk, dv), jnp.float32)
    _, o = lax.scan(step, state0, (qc, kc, vc, gc))
    return o.transpose(1, 0, 3, 2, 4).reshape(bsz, s, h, dv)

def swa_with_sinks(q, k, v, sinks):
    bsz, s, _, d = q.shape
    w = SWA_WINDOW
    nb = s // w
    qb = q.reshape(bsz, nb, w, SWA_KV_HEADS, SWA_GROUP, d)

    def band(t):
        tb = t.reshape(bsz, nb, w, SWA_KV_HEADS, d)
        prev = jnp.pad(tb[:, :-1], ((0, 0), (1, 0), (0, 0), (0, 0), (0, 0)))
        return jnp.concatenate([prev, tb], axis=2)

    kband, vband = band(k), band(v)
    scores = jnp.einsum('bnqhgd,bnkhd->bnhgqk', qb, kband).astype(jnp.float32) * (d ** -0.5)
    blk = jnp.arange(nb)[:, None, None]
    q_pos = blk * w + jnp.arange(w)[None, :, None]
    k_pos = (blk - 1) * w + jnp.arange(2 * w)[None, None, :]
    valid = (k_pos >= 0) & (k_pos <= q_pos) & (q_pos - k_pos < w)
    scores = jnp.where(valid[None, :, None, None], scores, -jnp.inf)
    sink = sinks.astype(jnp.float32).reshape(SWA_KV_HEADS, SWA_GROUP)[None, None, :, :, None, None]
    m = jnp.maximum(jnp.max(scores, axis=-1, keepdims=True), sink)
    p = jnp.exp(scores - m)
    denom = jnp.sum(p, axis=-1, keepdims=True) + jnp.exp(sink - m)
    probs = (p / denom).astype(v.dtype)
    out = jnp.einsum('bnhgqk,bnkhd->bnqhgd', probs, vband)
    return out.reshape(bsz, s, SWA_Q_HEADS * d)

def moe_ffn(h, w_router, b_router, w_e1, b_e1, w_e2, b_e2):
    bsz, s, d = h.shape
    t = bsz * s
    hf = h.reshape(t, d)
    logits = (hf @ w_router + b_router).astype(jnp.float32)
    top_v, top_i = lax.top_k(logits, TOP_K)
    gates = jax.nn.softmax(top_v, axis=-1)

    a = t * TOP_K
    flat_e = top_i.reshape(a)
    flat_tok = jnp.repeat(jnp.arange(t, dtype=jnp.int32), TOP_K)
    flat_w = gates.reshape(a)
    order = jnp.argsort(flat_e)
    se, stok, sw = flat_e[order], flat_tok[order], flat_w[order]
    counts = jnp.bincount(flat_e, length=N_EXPERTS)
    padded = ((counts + MOE_BLOCK - 1) // MOE_BLOCK) * MOE_BLOCK
    start = jnp.cumsum(counts) - counts
    pend = jnp.cumsum(padded)
    pstart = pend - padded
    dest = pstart[se] + (jnp.arange(a, dtype=jnp.int32) - start[se])

    n_blocks = -(-a // MOE_BLOCK) + N_EXPERTS
    rows = n_blocks * MOE_BLOCK
    ptok = jnp.zeros((rows,), jnp.int32).at[dest].set(stok)
    pw = jnp.zeros((rows,), jnp.float32).at[dest].set(sw)
    block_e = jnp.minimum(
        jnp.searchsorted(pend, jnp.arange(n_blocks) * MOE_BLOCK, side='right'), N_EXPERTS - 1)

    def expert_block(args):
        tok, e = args
        xb = hf[tok]
        u = xb @ w_e1[e] + b_e1[e]
        x_glu = jnp.minimum(u[..., ::2], SWIGLU_LIMIT)
        x_lin = jnp.clip(u[..., 1::2], -SWIGLU_LIMIT, SWIGLU_LIMIT)
        act = x_glu * jax.nn.sigmoid(SWIGLU_ALPHA * x_glu) * (x_lin + 1.0)
        return act @ w_e2[e] + b_e2[e]

    ys = lax.map(expert_block, (ptok.reshape(n_blocks, MOE_BLOCK), block_e))
    ys = ys.reshape(rows, d) * pw[:, None].astype(ys.dtype)
    y = jax.ops.segment_sum(ys, ptok, num_segments=t)
    return y.reshape(bsz, s, d)

def setup_inputs(seed: int = 0) -> dict:
    key = jax.random.key(seed)
    ks = jax.random.split(key, 20)
    f32 = jnp.float32
    L = DEPTH

    def nrm(k, shape, scale):
        return jax.random.normal(k, shape, f32) * scale

    return {
        "x": nrm(ks[0], (BATCH, SEQ, D_MODEL), 1.0),
        "g_mix": 1.0 + nrm(ks[1], (L, D_MODEL), 0.02),
        "w_in": nrm(ks[2], (L, D_MODEL, D_IN), D_MODEL ** -0.5),
        "b_in": nrm(ks[3], (L, D_IN), 0.02),
        "w_gla_gate": nrm(ks[4], (L, GLA_GATE_RANK, GLA_HEADS * GLA_DK), GLA_GATE_RANK ** -0.5),
        "b_gla_gate": nrm(ks[5], (L, GLA_HEADS * GLA_DK), 0.5),
        "g_gla_head": 1.0 + nrm(ks[6], (L, GLA_DV), 0.02),
        "w_gla_out": nrm(ks[7], (L, GLA_HEADS * GLA_DV, D_MODEL), (GLA_HEADS * GLA_DV) ** -0.5),
        "sinks": nrm(ks[8], (L, SWA_Q_HEADS), 1.0),
        "w_swa_out": nrm(ks[9], (L, SWA_Q_HEADS * SWA_HEAD_DIM, D_MODEL), (SWA_Q_HEADS * SWA_HEAD_DIM) ** -0.5),
        "w_out": nrm(ks[10], (L, D_MODEL, D_MODEL), D_MODEL ** -0.5),
        "g_ffn": 1.0 + nrm(ks[11], (L, D_MODEL), 0.02),
        "w_router": nrm(ks[12], (L, D_MODEL, N_EXPERTS), D_MODEL ** -0.5),
        "b_router": nrm(ks[13], (L, N_EXPERTS), 0.01),
        "w_e1": nrm(ks[14], (L, N_EXPERTS, D_MODEL, 2 * D_FF), D_MODEL ** -0.5),
        "b_e1": nrm(ks[15], (L, N_EXPERTS, 2 * D_FF), 0.01),
        "w_e2": nrm(ks[16], (L, N_EXPERTS, D_FF, D_MODEL), D_FF ** -0.5),
        "b_e2": nrm(ks[17], (L, N_EXPERTS, D_MODEL), 0.01),
        "g_final": 1.0 + nrm(ks[18], (D_MODEL,), 0.02),
    }

def reference(x, g_mix, w_in, b_in, w_gla_gate, b_gla_gate, g_gla_head, w_gla_out, sinks,
              w_swa_out, w_out, g_ffn, w_router, b_router, w_e1, b_e1, w_e2, b_e2, g_final):
    bsz, s, _ = x.shape
    pos = jnp.arange(s, dtype=jnp.int32)
    for l in range(DEPTH):
        h = rms_norm(x, g_mix[l])
        proj = h @ w_in[l] + b_in[l]
        parts = []
        off = 0
        for size in SPLIT_SIZES:
            parts.append(proj[..., off:off + size])
            off += size
        gq, gk, gv, gr, g_lr, sq, sk, sv, gate_a, gate_b = parts

        log_g = jax.nn.log_sigmoid((g_lr @ w_gla_gate[l] + b_gla_gate[l]).astype(jnp.float32)) / GLA_TAU
        o_a = gla_chunked(gq.reshape(bsz, s, GLA_HEADS, GLA_DK),
                          gk.reshape(bsz, s, GLA_HEADS, GLA_DK),
                          gv.reshape(bsz, s, GLA_HEADS, GLA_DV),
                          log_g.reshape(bsz, s, GLA_HEADS, GLA_DK))
        o_a = o_a * lax.rsqrt(jnp.mean(o_a * o_a, axis=-1, keepdims=True) + NORM_EPS) \
            * g_gla_head[l].astype(jnp.float32)
        o_a = o_a.reshape(bsz, s, GLA_HEADS * GLA_DV).astype(x.dtype) * jax.nn.silu(gr)
        y_a = o_a @ w_gla_out[l]

        q = rope(sq.reshape(bsz, s, SWA_Q_HEADS, SWA_HEAD_DIM), pos)
        k = rope(sk.reshape(bsz, s, SWA_KV_HEADS, SWA_HEAD_DIM), pos)
        v = sv.reshape(bsz, s, SWA_KV_HEADS, SWA_HEAD_DIM)
        y_b = swa_with_sinks(q, k, v, sinks[l]) @ w_swa_out[l]

        mixed = jax.nn.sigmoid(gate_a) * y_a + jax.nn.sigmoid(gate_b) * y_b
        x = x + mixed @ w_out[l]

        x = x + moe_ffn(rms_norm(x, g_ffn[l]), w_router[l], b_router[l],
                        w_e1[l], b_e1[l], w_e2[l], b_e2[l])
    return rms_norm(x, g_final)


_drawn_inputs = setup_inputs


def setup_inputs(seed=0):
    import zlib

    import numpy as np

    out = dict(_drawn_inputs(seed))
    spreads = {}
    factors = {'g_gla_head': 3.36, 'sinks': 3.502, 'b_e1': 8.0, 'b_e2': 8.0, 'g_final': 2.907}
    for name, (base, spread) in spreads.items():
        noise = np.random.default_rng([zlib.crc32(name.encode()), seed]).standard_normal(out[name].shape)
        drawn = base * np.exp(spread * noise) if base else spread * noise
        out[name] = __import__('jax').numpy.asarray(drawn.astype(out[name].dtype))
    for name, factor in factors.items():
        out[name] = (out[name] * factor).astype(out[name].dtype)
    return out
```

```python
from contextlib import ExitStack

import numpy as np

import concourse.bass as bass
from concourse import mybir

ALU = mybir.AluOpType
ACT = mybir.ActivationFunctionType
F32 = mybir.dt.float32
BF16 = mybir.dt.bfloat16
U32 = mybir.dt.uint32
I32 = mybir.dt.int32
AX_X = mybir.AxisListType.X

P = 128
D = 1024
SEQ = 256
TT = SEQ // P
KT = D // P
EPS = 1e-5
GH, GDK, GDV = 4, 128, 256
TAU = 16.0
GSCALE = GDK ** -0.5
CLAMP = 38.0
RANK = 16
QH, HD = 16, 64
KVW = 256
HALF = HD // 2
QSCALE = HD ** -0.5
HG = 4
NGRP = QH // HG * TT
NEG = -1e30
NE = 32
TOPK = 4
SLOTS = 64
PASSES = SEQ // SLOTS
LIMIT = 7.0
ALPHA = 1.702
FT = D // P
BW = 512
NSLOT = 16
SLOTW = 2048
DPAIRS = 5
RING0 = 2 * DPAIRS
CH1, CH2 = 8, 4
CH = CH1 + CH2
UNROLL = 4

BLOCKS = ["sq0", "sq1", "skv", "gq", "gk", "gv0", "gv1", "gr0", "gr1", "ga0", "glao0", "ga1", "glao1",
          "gb0", "swao0", "gb1", "swao1", "wo0", "wo1"]
NB = len(BLOCKS)
TOKEN_MAJOR = {"sq0", "sq1", "skv", "gv0", "gv1", "gr0", "gr1", "wo0", "wo1"}
BIAS_ROWS = ["sq0", "sq1", "skv", "gv0", "gv1", "gr0", "gr1"]
NPJ = 3

C_GMIX, C_BQ, C_BK, C_BGA, C_BGB, C_BGATE, C_GFFN, C_BLR = 0, 8, 12, 16, 24, 32, 36, 44
NCV = 45
R_SINK, R_HEAD, R_ROUTER = 0, 16, 272
NROW = 304
T_ID = 0
T_SWA = T_ID + P
T_DIAG = T_SWA + SEQ
T_COS = T_DIAG + 32
T_SIN = T_COS + TT * HALF
T_TRI = T_SIN + TT * HALF
T_ONE = T_TRI + P
T_IOTA = T_ONE + P
T_THR = T_IOTA + SLOTS
T_HOT = T_THR + PASSES
NTAB = T_HOT + NE


def tables():
    t = np.zeros((P, NTAB), np.float32)
    p = np.arange(P)[:, None]
    t[:, T_ID:T_ID + P] = np.eye(P)
    s = np.arange(SEQ)[None, :]
    t[:, T_SWA:T_SWA + SEQ] = np.where((s > p) & (s <= p + P), 0.0, NEG)
    t[:, T_DIAG:T_DIAG + 32] = np.arange(32)[None, :] >= p % 32
    inv = np.float32(10000.0) ** (-np.arange(HALF, dtype=np.float32) / np.float32(HALF))
    for i in range(TT):
        ang = (np.arange(P, dtype=np.float32) + np.float32(P * i))[:, None] * inv[None, :]
        t[:, T_COS + i * HALF:T_COS + (i + 1) * HALF] = np.cos(ang)
        t[:, T_SIN + i * HALF:T_SIN + (i + 1) * HALF] = np.sin(ang)
    t[:, T_TRI:T_TRI + P] = p < np.arange(P)[None, :]
    t[:, T_ONE:T_ONE + P] = 1.0
    t[:, T_IOTA:T_IOTA + SLOTS] = np.arange(SLOTS)[None, :]
    t[:, T_THR:T_THR + PASSES] = np.arange(PASSES)[None, :] * SLOTS
    t[:, T_THR] = -1.0
    t[:, T_HOT:T_HOT + NE] = np.arange(NE)[None, :] == p % NE
    return t


def program(nc, x, wblk, wskv, wgate, cv, rows, brow, tab, wrout, be1, be2, gfin, wexp, out):
    with ExitStack() as ctx:
        def sb(name, shape, dt=F32):
            return ctx.enter_context(nc.sbuf_tensor(name, shape, dt))

        def sem(name):
            return ctx.enter_context(nc.semaphore(name))

        ring = sb("ring", [P, NSLOT * SLOTW])
        X = sb("X", [P, TT, D])
        HT = sb("HT", [P, KT, SEQ])
        GV = sb("GV", [P, TT, D])
        GR = sb("GR", [P, TT, D])
        SQ = sb("SQ", [P, TT, D])
        SQR = sb("SQR", [P, TT, D])
        SIG = sb("SIG", [P, D])
        KVRAW = sb("KVRAW", [P, TT, KVW])
        KD = sb("KD", [P, TT, 4 * HD])
        KTT = sb("KTT", [P, 2, SEQ])
        PTG = sb("PTG", [P, GH, 3, P])
        BRW = sb("BRW", [P, 2, BW])
        CV = sb("CV", [P, NCV])
        ROW = sb("ROW", [P, NROW])
        TAB = sb("TAB", [P, NTAB])
        WR = sb("WR", [P, KT, NE])
        BE1 = sb("BE1", [3 * NE, 2 * D], BF16)
        SM = sb("SM", [P, 160])
        NBI = sb("NBI", [P, 1], I32)

        tail = [RING0 * SLOTW]

        def in_tail(n):
            tail[0] += n
            assert tail[0] <= NSLOT * SLOTW
            return ring[:, tail[0] - n:tail[0]]

        GQT, GKT, B, W0, W1, W2, TMP = [in_tail(GH * SEQ) for _ in range(7)]
        SS = in_tail(2 * HG * SEQ).rearrange("p (b h s) -> p b h s", b=2, h=HG)
        PTS = in_tail(2 * HG * SEQ).rearrange("p (b h s) -> p b h s", b=2, h=HG)
        WG = in_tail(GH * GDK)
        LRT = in_tail(SEQ)

        ident = TAB[:, T_ID:T_ID + P]

        def col(c, n=1, p=P):
            return CV[0:p, c:c + n]

        def small(a, n):
            return SM[:, a:a + n]
        S_SS, S_VAR, S_SD, S_RS = small(0, 2), small(2, 2), small(4, 2), small(6, 2)
        S_MX = [small(10 + 4 * b, 4) for b in range(2)]
        S_NM = [small(18 + 4 * b, 4) for b in range(2)]
        S_SUM = [small(26 + 4 * b, 4) for b in range(2)]
        S_DS = [small(34 + 4 * b, 4) for b in range(2)]
        S_ES = [small(42 + 4 * b, 4) for b in range(2)]
        S_DEN = [small(50 + 4 * b, 4) for b in range(2)]
        S_RD = [small(58 + 4 * b, 4) for b in range(2)]
        S_GS, S_GVAR, S_GSD, S_GRS = small(66, 8), small(74, 8), small(82, 8), small(90, 8)
        S_V8 = [small(98 + 8 * i, 8) for i in range(TT)]
        S_IF = [small(114 + 8 * i, 8) for i in range(TT)]
        S_NV = [small(130 + i, 1) for i in range(TT)]
        S_EG = [small(132 + 4 * i, 4) for i in range(TT)]
        S_ES4 = [small(140 + i, 1) for i in range(TT)]
        S_RG = [small(142 + i, 1) for i in range(TT)]
        S_GT = [small(144 + 4 * i, 4) for i in range(TT)]
        S_CNT, S_CMP, S_NP = small(152, 1), small(153, PASSES), small(157, 1)
        IDX = [sb(f"IDX{i}", [P, 8], U32) for i in range(TT)]

        mixT = SQR[:].rearrange("p i d -> p (i d)").rearrange("p (k t) -> p k t", k=KT)
        qT = SQ[:].rearrange("p i d -> p (i d)").rearrange("p (k t) -> p k t", k=KT)
        obT = qT
        oaT = GV[:].rearrange("p i d -> p (i d)").rearrange("p (k t) -> p k t", k=KT)
        HTf = HT[:].rearrange("p k t -> p (k t)")
        xn = HTf.rearrange("p (i d) -> p i d", i=TT)
        xnT = oaT
        GRf = GR[:].rearrange("p i d -> p (i d)")
        RK = GRf[:, 0:TT * 129].rearrange("p (i e) -> p i e", i=TT)
        GT_ = GRf[:, 264:264 + TT * NE].rearrange("p (i e) -> p i e", i=TT)
        LG = GRf[:, 328:328 + TT * NE].rearrange("p (i e) -> p i e", i=TT)
        MK = GRf[:, 392:392 + TT * NE].rearrange("p (i e) -> p i e", i=TT)
        OH = GRf[:, 456:456 + TT * TOPK * NE].rearrange("p (i k e) -> p i k e", i=TT, k=TOPK)
        BIG = GRf[:, 712:712 + TT * NE].rearrange("p (i e) -> p i e", i=TT)
        KVf = KVRAW[:].rearrange("p i d -> p (i d)")
        OG = KVf[:, 0:TT * TOPK * NE].rearrange("p (i k e) -> p i k e", i=TT, k=TOPK)
        GATT = KVf[0:NE, 256:256 + SEQ]
        BE2 = [KD[0:NE].rearrange("p i d -> p (i d)"), KTT[0:NE].rearrange("p g t -> p (g t)")]
        BE1R = GRf[0:NE, :]
        SQRf = SQR[:].rearrange("p i d -> p (i d)")
        SQf = SQ[:].rearrange("p i d -> p (i d)")
        XP = [a.bitcast(BF16).rearrange("p (i d) -> p i d", i=TT)
              for a in (SQRf[:, 0:D], SQRf[:, D:2 * D], GRf[:, D:2 * D])]
        REST = SQf.rearrange("p (i d) -> p i d", i=TT)
        XT = SQf[:, 0:512].rearrange("p (k c) -> p k c", k=KT)
        GLU, LIN, SGM = SQf[:, 512:1024], SQf[:, 1024:1536], SQf[:, 1536:2048]
        PTf = PTG[:].rearrange("p h b t -> p (h b t)")
        AT = PTf[:, 0:512]
        Y = PTf[:, 512:1024]
        SELG = PTf[:, 1024:1280].rearrange("p (i r c) -> p i r c", i=TT, r=2)
        SEL = PTf[:, 1280:1344].bitcast(BF16).rearrange("p (i c) -> p i c", i=TT)
        SELE = PTf[0:3 * NE, 1344:1376].bitcast(BF16)
        SELT = BRW
        OUTB = GV

        PS = ctx.enter_context(nc.psum_tensor("PS", [P, 8, 512], F32))

        def bk(b, w=512, p=P):
            return PS[0:p, b, 0:w]

        x_in, tab_in, cv_in, row_in = sem("x_in"), sem("tab_in"), sem("cv_in"), sem("row_in")
        wg_in, wr_in, be1_in, be2_in, gfin_in = sem("wg_in"), sem("wr_in"), sem("be1_in"), sem("be2_in"), sem("gfin_in")
        blk_in = [sem(f"blk_in{q}") for q in range(DPAIRS)]
        bias_in = [sem(f"bias_in{q}") for q in range(2)]
        pj_full = [sem(f"pj_full{b}") for b in range(NPJ)]
        pj_free = [sem(f"pj_free{b}") for b in range(NPJ)]
        ssq0, var0, sd0, rs0 = sem("ssq0"), sem("var0"), sem("sd0"), sem("rs0")
        xs_ready, xt_full, ht_ready = sem("xs_ready"), sem("xt_full"), sem("ht_ready")
        lr_full, lr_ready, z_full, z_ready = sem("lr_full"), sem("lr_ready"), sem("z_full"), sem("z_ready")
        qrot_ready, qt_full, qt_ready = sem("qrot_ready"), sem("qt_full"), sem("qt_ready")
        krot_ready, kt_full, kt_ready = sem("krot_ready"), sem("kt_full"), sem("kt_ready")
        gate_neg, gate_sp, decay_in, decay_out = sem("gate_neg"), sem("gate_sp"), sem("decay_in"), sem("decay_out")
        gla_ops, gla_sc, gla_pt, gla_o, gla_sq, gla_var, gla_sd, gla_oa = (
            sem("gla_ops"), sem("gla_sc"), sem("gla_pt"), sem("gla_o"), sem("gla_sq"), sem("gla_var"), sem("gla_sd"), sem("gla_oa"))
        gla_zero = sem("gla_zero")
        gr_sig, gr_ready = sem("gr_sig"), sem("gr_ready")
        oat_full, oat_ready, obt_full, obt_ready = sem("oat_full"), sem("oat_ready"), sem("obt_full"), sem("obt_ready")
        oat_cp, obt_cp = sem("oat_cp"), sem("obt_cp")
        sw_s, sw_masked, sw_max, sw_exp = sem("sw_s"), sem("sw_masked"), sem("sw_max"), sem("sw_exp")
        sw_t, sw_ptA, sw_ptV, sw_o, sw_out = sem("sw_t"), sem("sw_ptA"), sem("sw_ptV"), sem("sw_o"), sem("sw_out")
        mix_ready = sem("mix_ready")
        ssq1, var1, sd1, xn_ready, xnT_full, xnT_ready, lg_full = (
            sem("ssq1"), sem("var1"), sem("sd1"), sem("xn_ready"), sem("xnT_full"), sem("xnT_ready"), sem("lg_full"))
        top_ready, eg_ready, mask_ready, rank_full, gat_ready, gatT_full, gatT_ready, np_ready = (
            sem("top_ready"), sem("eg_ready"), sem("mask_ready"), sem("rank_full"), sem("gat_ready"), sem("gatT_full"), sem("gatT_ready"), sem("np_ready"))
        slot_in = [sem(f"slot_in{s}") for s in range(NSLOT)]
        chunk_used = sem("chunk_used")
        sel_ready, xg_full, xt_ready = sem("sel_ready"), sem("xg_full"), sem("xt_ready")
        u_read, glu_ready, sgm_ready, act_ready = sem("u_read"), sem("glu_ready"), sem("sgm_ready"), sem("act_ready")
        y_ready, at_full, at_ready = sem("y_ready"), sem("at_full"), sem("at_ready")
        selg_ready, selT_full, selT_a, selT_b = sem("selg_ready"), sem("selT_full"), sem("selT_a"), sem("selT_b")
        sele_ready, xp1, rest1, xp2, xp3, be1_ready = (
            sem("sele_ready"), sem("xp1"), sem("rest1"), sem("xp2"), sem("xp3"), sem("be1_ready"))
        moe_done, xf_ready, ssqf, varf, sdf, out_ready, out_done = (
            sem("moe_done"), sem("xf_ready"), sem("ssqf"), sem("varf"), sem("sdf"), sem("out_ready"), sem("out_done"))
        qt_cp, selg_raw, lin_ready = sem("qt_cp"), sem("selg_raw"), sem("lin_ready")
        dve_step, act_step = sem("dve_step"), sem("act_step")

        block = ctx.enter_context(nc.Block())

        def pair(i):
            return (i + DPAIRS - NB % DPAIRS) % DPAIRS

        def fills(i):
            return sum(pair(n) == pair(i) for n in range(i + 1))

        def wslice(i, k, a, b):
            width = KVW + RANK if BLOCKS[i] == "skv" else BW
            base = pair(i) * 2 * SLOTW + k * width
            return ring[:, base + a:base + b]

        def slot_of(c):
            s = (RING0 + c) % NSLOT
            return s, ring[:, s * SLOTW:(s + 1) * SLOTW]

        def block_multiplied(eng, i):
            u = 2 * i + 1
            eng.wait_ge(pj_full[u % NPJ], u // NPJ + 1)
            if BLOCKS[i] == "skv":
                eng.wait_ge(lr_full, 1)

        def evacuated(eng, u):
            eng.wait_ge(pj_free[u % NPJ], u // NPJ + 1)

        @block.sync
        def _(sp):
            sp.dma_start(X[:], x.rearrange("(i p) d -> p i d", p=P)).then_inc(x_in, 16)
            for i in range(NB):
                if i >= DPAIRS:
                    block_multiplied(sp, i - DPAIRS)
                q = pair(i)
                if BLOCKS[i] == "skv":
                    n = KT * (KVW + RANK)
                    sp.dma_start(ring[:, q * 2 * SLOTW:q * 2 * SLOTW + n], wskv).then_inc(blk_in[q], 16)
                else:
                    sp.dma_start(ring[:, q * 2 * SLOTW:(q + 1) * 2 * SLOTW],
                                 wblk[i - (i > 2)]).then_inc(blk_in[q], 16)

            def load_body(turn, e0):
                for c in range(UNROLL * CH):
                    s, dst = slot_of(c)
                    sp.wait_ge(chunk_used, turn * (UNROLL * CH) + c - NSLOT + 1)
                    sp.dma_start(dst, wexp[e0 * CH + c]).then_inc(slot_in[s], 16)

            for c in range(UNROLL * CH):
                s, dst = slot_of(c)
                if c == 0:
                    sp.wait_ge(gla_o, GH)
                    sp.wait_ge(sw_out, NGRP)
                if RING0 + c >= NSLOT and c < NSLOT and s % 2 == 0:
                    block_multiplied(sp, NB - DPAIRS + s // 2)
                if c >= NSLOT:
                    sp.wait_ge(chunk_used, c - NSLOT + 1)
                sp.dma_start(dst, wexp[c]).then_inc(slot_in[s], 16)
            with sp.Fori(1, NE // UNROLL) as i:
                load_body(i, i * UNROLL)
            sp.wait_ge(np_ready, 1)
            passes = sp.value_load(NBI[0:1, 0:1], min_val=1, max_val=PASSES)
            with sp.If(passes > 1):
                with sp.Fori(1, passes) as b:
                    with sp.Fori(0, NE // UNROLL) as i:
                        load_body(b * (NE // UNROLL) + i, i * UNROLL)
            for i in range(TT):
                sp.wait_ge(out_ready, i + 1)
                sp.dma_start(out[i * P:(i + 1) * P, :], OUTB[:, i, :]).then_inc(out_done, 16)
            sp.wait_ge(out_done, 16 * TT)

        @block.gpsimd
        def _(pool):
            nc.gpsimd.memset(PTG[:], 0.0).then_inc(gla_zero, 1)
            pool.dma_start(CV[:], cv).then_inc(cv_in, 16)

            def bias(n):
                if n >= 2:
                    block = BLOCKS.index(BIAS_ROWS[n - 2])
                    evacuated(pool, 2 * block)
                    evacuated(pool, 2 * block + 1)
                pool.dma_start(BRW[:, n % 2, :], brow[n:n + 1, :].partition_broadcast(P)).then_inc(bias_in[n % 2], 16)

            bias(0)
            bias(1)
            pool.dma_start(ROW[:], rows.partition_broadcast(P)).then_inc(row_in, 16)
            pool.dma_start(WG[0:RANK, :], wgate).then_inc(wg_in, 16)
            pool.dma_start(WR[:], wrout).then_inc(wr_in, 16)
            for n in range(2, len(BIAS_ROWS)):
                bias(n)
            pool.wait_ge(oat_full, 4)
            pool.dma_start(BE1R, be1).then_inc(be1_in, 16)
            pool.wait_ge(mix_ready, 4)
            pool.dma_start(SIG[:], gfin.partition_broadcast(P)).then_inc(gfin_in, 16)
            for n in range(2):
                pool.dma_start(BE2[n], be2[:, n * 512:(n + 1) * 512]).then_inc(be2_in, 16)

        @block.tensor
        def _(pe):
            mm = nc.tensor.matmul

            pe.wait_ge(tab_in, 16)
            for a in range(4):
                pe.wait_ge(xs_ready, TT)
                for q in range(4):
                    k, i = 2 * a + q // 2, q % 2
                    last = nc.tensor.transpose(PS[:, 4 + a, q * P:(q + 1) * P], SQ[:, i, k * P:(k + 1) * P], ident)
                last.then_inc(xt_full, 1)

            usage = [0]

            def pj_bank():
                b, n = usage[0] % NPJ, usage[0] // NPJ
                usage[0] += 1
                if n:
                    pe.wait_ge(pj_free[b], n)
                return b

            def dense(i, between=()):
                name = BLOCKS[i]
                pe.wait_ge(blk_in[pair(i)], 16 * fills(i))
                for half in range(2):
                    b = pj_bank()
                    if name in TOKEN_MAJOR:
                        src = mixT if name[:2] == "wo" else HT
                        w = KVW if name == "skv" else BW
                        for k in range(KT):
                            last = mm(bk(b, w), src[:, k, half * P:(half + 1) * P], wslice(i, k, 0, w),
                                      start=(k == 0), stop=(k == KT - 1))
                    else:
                        src = {"gl": oaT, "sw": obT}.get(name[:2], HT)
                        for f in range(2):
                            c = (2 * half + f) * P
                            for k in range(KT):
                                last = mm(PS[:, b, f * SEQ:(f + 1) * SEQ], wslice(i, k, c, c + P), src[:, k, :],
                                          start=(k == 0), stop=(k == KT - 1))
                    last.then_inc(pj_full[b], 1)
                    if half == 0:
                        for step in between[:1]:
                            step()
                if name == "skv":
                    for k in range(KT):
                        last = mm(PS[0:RANK, 3, 0:SEQ], wslice(i, k, KVW, KVW + RANK), HT[:, k, :],
                                  start=(k == 0), stop=(k == KT - 1))
                    last.then_inc(lr_full, 1)
                for step in between[1:]:
                    step()

            def transpose16(get_src, full):
                for a in range(4):
                    for q in range(4):
                        k, i = 2 * a + q // 2, q % 2
                        last = nc.tensor.transpose(PS[:, 4 + a, q * P:(q + 1) * P], get_src(i, k), ident)
                    last.then_inc(full, 1)

            pe.wait_ge(ht_ready, 4)
            dense(0)
            dense(1)
            dense(2)
            dense(3)
            pe.wait_ge(lr_ready, 1)
            pe.wait_ge(wg_in, 16)
            for h in range(GH):
                last = mm(PS[:, 6 + h // 2, (h % 2) * SEQ:(h % 2 + 1) * SEQ], WG[0:RANK, h * GDK:(h + 1) * GDK],
                          LRT[0:RANK, :], start=True, stop=True)
            last.then_inc(z_full, 1)
            dense(4)
            pe.wait_ge(krot_ready, TT)
            for g in range(2):
                for i in range(TT):
                    last = nc.tensor.transpose(PS[:, 3, (2 * g + i) * P:(2 * g + i + 1) * P],
                                               KD[:, i, g * P:(g + 1) * P], ident)
            last.then_inc(kt_full, 1)
            pe.wait_ge(qrot_ready, TT)
            pe.wait_ge(z_ready, GH)
            transpose16(lambda i, k: SQR[:, i, k * P:(k + 1) * P], qt_full)

            def scores(n):
                i, g4 = n // (NGRP // TT), n % (NGRP // TT)
                if n == 0:
                    pe.wait_ge(qt_ready, 2)
                    pe.wait_ge(qt_cp, 2)
                    pe.wait_ge(kt_ready, 1)
                else:
                    pe.wait_ge(sw_masked, 2 * n)
                ns = (i + 1) * P
                for hh in range(HG):
                    h = HG * g4 + hh
                    p0 = (h % 2) * HD
                    last = mm(PS[:, 4 + hh % 2, (hh // 2) * SEQ:(hh // 2) * SEQ + ns],
                              qT[p0:p0 + HD, h // 2, i * P:(i + 1) * P],
                              KTT[p0:p0 + HD, h // (QH // 2), 0:ns], start=True, stop=True)
                last.then_inc(sw_s, 1)

            def probs_t(n):
                i = n // (NGRP // TT)
                pe.wait_ge(sw_exp, n + 1)
                if n:
                    pe.wait_ge(sw_ptA, n)
                    pe.wait_ge(sw_ptV, n)
                for hh in range(HG):
                    for st in range(i + 1):
                        last = nc.tensor.transpose(PS[:, 6 + hh // 2, (2 * (hh % 2) + st) * P:(2 * (hh % 2) + st + 1) * P],
                                                   SS[:, n % 2, hh, st * P:(st + 1) * P], ident)
                last.then_inc(sw_t, 1)

            def values(n):
                i, g4 = n // (NGRP // TT), n % (NGRP // TT)
                pe.wait_ge(sw_ptA, n + 1)
                pe.wait_ge(sw_ptV, n + 1)
                if n:
                    pe.wait_ge(sw_out, n)
                kv = g4 // 2
                for hh in range(HG):
                    for st in range(i + 1):
                        last = mm(PS[:, 3, hh * HD:(hh + 1) * HD], PTS[:, n % 2, hh, st * P:(st + 1) * P],
                                  KVRAW[:, st, P + kv * HD:P + (kv + 1) * HD], start=(st == 0), stop=(st == i))
                last.then_inc(sw_o, 1)

            def swa_slot(n):
                def run():
                    if 0 <= n - 2 < NGRP:
                        values(n - 2)
                    if 0 <= n - 1 < NGRP:
                        probs_t(n - 1)
                    if n < NGRP:
                        scores(n)
                return run

            dense(5, [swa_slot(0), swa_slot(1)])
            dense(6, [swa_slot(2), swa_slot(3)])
            dense(7, [swa_slot(4), swa_slot(5)])
            dense(8, [swa_slot(6), swa_slot(7)])
            dense(9, [swa_slot(8), swa_slot(9)])

            pe.wait_ge(sw_out, NGRP)
            transpose16(lambda i, k: SQR[:, i, k * P:(k + 1) * P], obt_full)
            pe.wait_ge(obt_ready, 2)
            pe.wait_ge(obt_cp, 2)
            pe.wait_ge(gla_ops, 5)
            for h in range(GH):
                w0, w1, w2 = (w[:, h * SEQ:(h + 1) * SEQ] for w in (W0, W1, W2))
                gq, gk = GQT[:, h * SEQ:(h + 1) * SEQ], GKT[:, h * SEQ:(h + 1) * SEQ]
                mm(PS[:, 4 + h, 0:P], w0[:, 0:P], w0[:, P:SEQ], start=True, stop=True)
                for i in range(TT):
                    c = P + i * P
                    t0 = i * P
                    mm(PS[0:64, 4 + h, c:c + 64], w1[:, t0:t0 + 64], w1[:, t0 + 64:t0 + 128], start=True, stop=True)
                    for q in range(2):
                        s0 = t0 + 64 * q
                        mm(PS[64 * q:64 * q + 32, 4 + h, c + 64:c + 96], w2[:, s0:s0 + 32], w2[:, s0 + 32:s0 + 64],
                           start=True, stop=True)
                    for q in range(4):
                        s0 = t0 + 32 * q
                        last = mm(PS[32 * q:32 * q + 32, 4 + h, c + 96:c + 128], gk[:, s0:s0 + 32], gq[:, s0:s0 + 32],
                                  start=True, stop=True)
            last.then_inc(gla_sc, 1)
            pe.wait_ge(gla_pt, 1)
            for u in range(10, 14):
                evacuated(pe, u)
            for h in range(GH):
                v = slice(h * GDV, (h + 1) * GDV)
                mm(PS[:, 4 + h, 0:GDV], PTG[:, h, 1, :], GV[:, 0, v], start=True, stop=True)
                mm(PS[:, 4 + h, GDV:2 * GDV], PTG[:, h, 0, :], GV[:, 0, v], start=True, stop=False)
                last = mm(PS[:, 4 + h, GDV:2 * GDV], PTG[:, h, 2, :], GV[:, 1, v], start=False, stop=True)
                last.then_inc(gla_o, 1)
            pe.wait_ge(gla_oa, GH * TT)
            transpose16(lambda i, k: GR[:, i, k * P:(k + 1) * P], oat_full)
            pe.wait_ge(oat_ready, 2)
            pe.wait_ge(oat_cp, 2)
            for i in range(10, 17):
                dense(i)
            pe.wait_ge(mix_ready, 4)
            dense(17)
            dense(18)

            pe.wait_ge(xn_ready, TT)
            transpose16(lambda i, k: xn[:, i, k * P:(k + 1) * P], xnT_full)
            pe.wait_ge(xnT_ready, 4)
            pe.wait_ge(wr_in, 16)
            for i in range(TT):
                for k in range(KT):
                    last = mm(PS[:, 3, i * NE:(i + 1) * NE], xnT[:, k, i * P:(i + 1) * P], WR[:, k, :],
                              start=(k == 0), stop=(k == KT - 1))
            last.then_inc(lg_full, 1)
            tri, ones = TAB[:, T_TRI:T_TRI + P], TAB[:, T_ONE:T_ONE + P]
            pe.wait_ge(mask_ready, TT)
            mm(PS[:, 4, 0:NE], tri, MK[:, 0, :], start=True, stop=True)
            mm(PS[:, 4, NE:2 * NE], tri, MK[:, 1, :], start=True, stop=False)
            mm(PS[:, 4, NE:2 * NE], ones, MK[:, 0, :], start=False, stop=True)
            mm(PS[:, 4, 2 * NE:3 * NE], ones, MK[:, 0, :], start=True, stop=False)
            mm(PS[:, 4, 2 * NE:3 * NE], ones, MK[:, 1, :], start=False, stop=True).then_inc(rank_full, 1)
            pe.wait_ge(gat_ready, TT)
            for i in range(TT):
                last = nc.tensor.transpose(PS[0:NE, 5, i * P:(i + 1) * P], GT_[:, i, :], ident)
            last.then_inc(gatT_full, 1)
            pe.wait_ge(gatT_ready, 1)
            pe.wait_ge(be2_in, 32)
            for i in range(TT):
                for n in range(2):
                    mm(bk(2 * i + n), GATT[:, i * P:(i + 1) * P], BE2[n],
                       start=True, stop=True, skip_group_check=True)

            def gather():
                for k in range(KT):
                    for n in range(3 * TT):
                        last = mm(PS[:, 7, k * SLOTS:(k + 1) * SLOTS], XP[n // TT][:, n % TT, k * P:(k + 1) * P],
                                  SEL[:, n % TT, :], start=(n == 0), stop=(n == 3 * TT - 1))
                last.then_inc(xg_full, 1)

            def scatter():
                for i in range(TT):
                    for n in range(2):
                        last = mm(bk(2 * i + n), SELT[:, n, i * P:(i + 1) * P], Y,
                                  start=False, stop=True, skip_group_check=True)
                return last

            def both_halves(b, lhsT, rhs, start, stop):
                for g in range(2):
                    last = mm(PS[g * SLOTS:(g + 1) * SLOTS, b, :], lhsT, rhs[:, g * 512:(g + 1) * 512],
                              start=start, stop=stop)
                return last

            for n in range(TT):
                pe.wait_ge(xp3, n + 1)
            pe.wait_ge(sel_ready, 1)
            gather()
            pe.wait_ge(be1_ready, 1)
            pe.wait_ge(np_ready, 1)
            passes = pe.value_load(NBI[0:1, 0:1], min_val=1, max_val=PASSES)
            with pe.Fori(0, passes) as b:
                with pe.Fori(0, NE // UNROLL) as it:
                    turn = b * (NE // UNROLL) + it
                    for j in range(UNROLL):
                        e = turn * UNROLL + j

                        def chunk(c):
                            s, data = slot_of(j * CH + c)
                            pe.wait_ge(slot_in[s], turn * 48 + 16 * ((j * CH + c) // NSLOT + 1))
                            return data

                        pe.wait_ge(sele_ready, e + 1)
                        pe.wait_ge(selT_a, e + 1)
                        pe.wait_ge(selT_b, e + 1)
                        for n in range(2):
                            both_halves(4 + n, SELE, BE1[:, n * D:(n + 1) * D], True, False)
                        pe.wait_ge(xt_ready, e + 1)
                        for c in range(CH1):
                            w = chunk(c)
                            for n in range(2):
                                last = both_halves(4 + n, XT[:, c, :], w[:, n * D:(n + 1) * D], False, c == CH1 - 1)
                            last.then_inc(chunk_used, 1)
                        pe.wait_ge(sel_ready, e + 2)
                        gather()
                        pe.wait_ge(y_ready, e + 1)
                        scatter()
                        pe.wait_ge(selg_ready, e + 1)
                        pe.wait_ge(u_read, e + 1)
                        for i in range(TT):
                            last = nc.tensor.transpose(PS[:, 5, i * P:(i + 1) * P], SELG[:, i], ident)
                        last.then_inc(selT_full, 1)
                        pe.wait_ge(act_ready, e + 2)
                        for q in range(4):
                            last = nc.tensor.transpose(PS[:, 4, q * P:(q + 1) * P], LIN[:, q * P:(q + 1) * P], ident)
                        last.then_inc(at_full, 1)
                        pe.wait_ge(at_ready, e + 1)
                        for c in range(CH2):
                            w = chunk(CH1 + c)
                            for kk in range(2):
                                f = 2 * c + kk
                                o = (2 * (f % 4) + f // 4) * SLOTS
                                last = both_halves(6, AT[:, o:o + SLOTS], w[:, kk * D:(kk + 1) * D],
                                                   f == 0, f == FT - 1)
                            last.then_inc(chunk_used, 1)
            total = passes * NE
            pe.wait_ge(y_ready, total + 1)
            pe.wait_ge(selT_a, total + 1)
            pe.wait_ge(selT_b, total + 1)
            scatter().then_inc(moe_done, 1)

        @block.scalar
        def _(act):
            fn = nc.scalar.activation
            steps = [0]

            def link(ins):
                steps[0] += 1
                ins.then_inc(act_step, 1)
                act.wait_ge(act_step, steps[0])

            act.dma_start(TAB[:], tab).then_inc(tab_in, 16)
            act.wait_ge(x_in, 16)
            for i in range(TT):
                fn(HTf[:, i * D:(i + 1) * D], X[:, i, :], ACT.Square, accum_out=S_SS[:, i:i + 1]).then_inc(ssq0, 1)
            act.wait_ge(var0, 1)
            fn(S_SD, S_VAR, ACT.Sqrt).then_inc(sd0, 1)
            act.wait_ge(lr_full, 1)
            act.wait_ge(cv_in, 16)
            fn(LRT[0:RANK, :], PS[0:RANK, 3, 0:SEQ], ACT.Identity, bias=col(C_BLR, p=RANK)).then_inc(lr_ready, 1)

            def feature_major(i, dst, c, func):
                for half in range(2):
                    u = 2 * i + half
                    act.wait_ge(pj_full[u % NPJ], u // NPJ + 1)
                    for f in range(2):
                        n = 2 * half + f
                        last = fn(dst[:, n * SEQ:(n + 1) * SEQ], PS[:, u % NPJ, f * SEQ:(f + 1) * SEQ], func,
                                  bias=col(c + n))
                    last.then_inc(pj_free[u % NPJ], 1)

            feature_major(3, GQT, C_BQ, ACT.Identity)
            act.wait_ge(z_full, 1)
            for h in range(GH):
                fn(TMP[:, h * SEQ:(h + 1) * SEQ], PS[:, 6 + h // 2, (h % 2) * SEQ:(h % 2 + 1) * SEQ], ACT.Identity,
                   bias=col(C_BGATE + h)).then_inc(z_ready, 1)
            feature_major(4, GKT, C_BK, ACT.Identity)
            act.wait_ge(gate_neg, 1)
            link(fn(W1, W0, ACT.Exp))
            fn(W1, W1, ACT.Ln, bias=1.0).then_inc(gate_sp, 1)
            for a in range(2):
                act.wait_ge(qt_full, a + 1)
                fn(qT[:, 2 * a:2 * a + 2, :], PS[:, 4 + a, :].rearrange("p (k t) -> p k t", k=2), ACT.Copy).then_inc(qt_cp, 1)

            def swa_exp(n):
                ns = (n // (NGRP // TT) + 1) * P
                q = n % 2
                act.wait_ge(sw_max, n + 1)
                for hh in range(HG):
                    fn(SS[:, q, hh, 0:ns], SS[:, q, hh, 0:ns], ACT.Exp, bias=S_NM[q][:, hh:hh + 1],
                       accum_out=S_SUM[q][:, hh:hh + 1])
                fn(S_ES[q], S_DS[q], ACT.Exp).then_inc(sw_exp, 1)

            def swa_pt(n):
                i = n // (NGRP // TT)
                act.wait_ge(sw_t, n + 1)
                fn(PTS[:, n % 2, 0:2, 0:(i + 1) * P],
                   PS[:, 6, :].rearrange("p (h s) -> p h s", h=2)[:, :, 0:(i + 1) * P], ACT.Copy).then_inc(sw_ptA, 1)

            def gr_sigmoid(u):
                n, m = (u - 14) // 2, u % 2
                evacuated(act, u)
                if u >= 16:
                    act.wait_ge(gr_ready, u - 15)
                fn(SIG[:, m * BW:(m + 1) * BW], GR[:, m, n * BW:(n + 1) * BW], ACT.Sigmoid).then_inc(gr_sig, 1)

            def decays():
                v0 = W0.rearrange("p (h t) -> p h t", h=GH)
                b0 = B.rearrange("p (h t) -> p h t", h=GH)
                act.wait_ge(decay_in, 1)
                fn(v0[:, :, 0:P], v0[:, :, 0:P], ACT.Exp, scale=1.0 / TAU)
                fn(v0[:, :, P:SEQ], b0[:, :, P:SEQ], ACT.Exp, scale=1.0 / TAU).then_inc(decay_out, 1)
                for n, w in ((2, W1), (3, W2)):
                    act.wait_ge(decay_in, n)
                    fn(w, w, ACT.Exp, scale=1.0 / TAU).then_inc(decay_out, 1)
                act.wait_ge(decay_in, 4)
                act.wait_ge(decay_out, 1)
                fn(B, TMP, ACT.Exp, scale=1.0 / TAU).then_inc(decay_out, 1)
                act.wait_ge(decay_out, 4)
                fn(TMP, TMP, ACT.Exp, scale=-1.0 / TAU).then_inc(decay_out, 1)

            for n in range(NGRP + 1):
                if 0 <= n - 1:
                    swa_pt(n - 1)
                if n < NGRP:
                    swa_exp(n)
                if n == 2:
                    decays()
                if n >= 5:
                    gr_sigmoid(n + 9)

            act.wait_ge(gr_ready, 4)
            feature_major(9, SIG, C_BGA, ACT.Sigmoid)
            for a in range(2):
                act.wait_ge(obt_full, a + 1)
                fn(obT[:, 2 * a:2 * a + 2, :], PS[:, 4 + a, :].rearrange("p (k t) -> p k t", k=2), ACT.Copy).then_inc(obt_cp, 1)
            for h in range(GH):
                act.wait_ge(gla_o, h + 1)
                act.wait_ge(gla_sq, TT * h)
                for i in range(TT):
                    fn(PS[:, 3, i * GDV:(i + 1) * GDV], PS[:, 4 + h, i * GDV:(i + 1) * GDV], ACT.Square,
                       accum_out=S_GS[:, TT * h + i:TT * h + i + 1]).then_inc(gla_sq, 1)
            act.wait_ge(gla_var, 1)
            fn(S_GSD, S_GVAR, ACT.Sqrt).then_inc(gla_sd, 1)
            for a in range(2):
                act.wait_ge(oat_full, a + 1)
                fn(oaT[:, 2 * a:2 * a + 2, :], PS[:, 4 + a, :].rearrange("p (k t) -> p k t", k=2), ACT.Copy).then_inc(oat_cp, 1)
            for i, c in ((11, C_BGA + 4), (13, C_BGB), (15, C_BGB + 4)):
                if i == 15:
                    act.wait_ge(mix_ready, 2)
                else:
                    evacuated(act, 2 * i - 2)
                    evacuated(act, 2 * i - 1)
                feature_major(i, SIG, c, ACT.Sigmoid)
            for u in range(2 * NB - 4, 2 * NB):
                evacuated(act, u)
            for i in range(TT):
                fn(HTf[:, i * D:(i + 1) * D], X[:, i, :], ACT.Square, accum_out=S_SS[:, i:i + 1]).then_inc(ssq1, 1)
            act.wait_ge(var1, 1)
            fn(S_SD, S_VAR, ACT.Sqrt).then_inc(sd1, 1)
            for i in range(TT):
                act.wait_ge(xn_ready, i + 1)
                fn(XP[0][:, i, :], xn[:, i, :], ACT.Copy).then_inc(xp1, 1)
            for i in range(TT):
                act.wait_ge(rest1, i + 1)
                fn(XP[1][:, i, :], REST[:, i, :], ACT.Copy).then_inc(xp2, 1)
            for i in range(TT):
                act.wait_ge(top_ready, i + 1)
                fn(S_EG[i], S_V8[i][:, 0:TOPK], ACT.Exp, bias=S_NV[i], accum_out=S_ES4[i]).then_inc(eg_ready, 1)
            act.wait_ge(np_ready, 1)
            passes = act.value_load(NBI[0:1, 0:1], min_val=1, max_val=PASSES)
            with act.Fori(0, passes) as b:
                with act.Fori(0, NE) as e:
                    done = b * NE + e
                    act.wait_ge(glu_ready, done + 1)
                    fn(SGM, GLU, ACT.Sigmoid, scale=ALPHA).then_inc(sgm_ready, 1)
                    act.wait_ge(selT_full, done + 1)
                    fn(SELT[0:SLOTS, 0, 0:SEQ], PS[0:SLOTS, 5, 0:SEQ], ACT.Copy).then_inc(selT_a, 1)
                    act.wait_ge(at_full, done + 1)
                    fn(AT, bk(4), ACT.Copy).then_inc(at_ready, 1)
                    act.wait_ge(chunk_used, done * CH + CH)
                    fn(Y, bk(6), ACT.Copy).then_inc(y_ready, 1)
            for i in range(TT):
                act.wait_ge(xf_ready, 2 * (i + 1))
                fn(OUTB[:, i, :], X[:, i, :], ACT.Square, accum_out=S_SS[:, i:i + 1]).then_inc(ssqf, 1)
            act.wait_ge(varf, 1)
            fn(S_SD, S_VAR, ACT.Sqrt).then_inc(sdf, 1)

        @block.vector
        def _(dve):
            v = nc.vector
            steps = [0]

            def link(ins):
                steps[0] += 1
                ins.then_inc(dve_step, 1)
                dve.wait_ge(dve_step, steps[0])

            def mean_eps(ssq, var, n, count_sem, count, done):
                dve.wait_ge(count_sem, count)
                v.tensor_scalar(var, ssq, 1.0 / n, EPS, ALU.mult, ALU.add).then_inc(done, 1)

            mean_eps(S_SS, S_VAR, D, ssq0, TT, var0)
            dve.wait_ge(sd0, 1)
            link(v.reciprocal(S_RS, S_SD))
            for i in range(TT):
                v.tensor_scalar(SQ[:, i, :], X[:, i, :], S_RS[:, i:i + 1], None, ALU.mult).then_inc(xs_ready, 1)
            dve.wait_ge(cv_in, 16)
            for a in range(4):
                dve.wait_ge(xt_full, a + 1)
                v.tensor_tensor(HT[:, 2 * a:2 * a + 2, :], PS[:, 4 + a, :].rearrange("p (k t) -> p k t", k=2),
                                col(C_GMIX + 2 * a, 2).unsqueeze(2).broadcast_to([P, 2, SEQ]), ALU.mult).then_inc(ht_ready, 1)

            def token_major(u, dst, w, done=None):
                i = u // 2
                n = BIAS_ROWS.index(BLOCKS[i])
                dve.wait_ge(bias_in[n % 2], 16 * (n // 2 + 1))
                dve.wait_ge(pj_full[u % NPJ], u // NPJ + 1)
                v.tensor_tensor(dst, bk(u % NPJ, w), BRW[:, n % 2, 0:w], ALU.add).then_inc(pj_free[u % NPJ], 1)

            for u in range(6):
                i, m = u // 2, u % 2
                if i < 2:
                    token_major(u, SQ[:, m, i * BW:(i + 1) * BW], BW)
                else:
                    token_major(u, KVRAW[:, m, :], KVW)

            cos = TAB[:, T_COS:T_COS + TT * HALF].rearrange("p (i d) -> p i d", i=TT)
            sin = TAB[:, T_SIN:T_SIN + TT * HALF].rearrange("p (i d) -> p i d", i=TT)

            def rotate(src, dst, n, i, done):
                t1 = SIG[:, 0:n * HALF].rearrange("p (h d) -> p h d", h=n)
                t2 = SIG[:, BW:BW + n * HALF].rearrange("p (h d) -> p h d", h=n)
                c = cos[:, i, :].unsqueeze(1).broadcast_to([P, n, HALF])
                s = sin[:, i, :].unsqueeze(1).broadcast_to([P, n, HALF])
                v.tensor_tensor(t1, src[:, :, 0, :], c, ALU.mult)
                link(v.tensor_tensor(t2, src[:, :, 1, :], s, ALU.mult))
                for d in dst:
                    last = v.tensor_tensor(d[:, :, 0, :], t1, t2, ALU.subtract)
                link(last)
                v.tensor_tensor(t1, src[:, :, 1, :], c, ALU.mult)
                link(v.tensor_tensor(t2, src[:, :, 0, :], s, ALU.mult))
                for d in dst:
                    last = v.tensor_tensor(d[:, :, 1, :], t1, t2, ALU.add)
                last.then_inc(done, 1)
                dve.wait_ge(done, i + 1)

            dve.wait_ge(tab_in, 16)
            for i in range(TT):
                evacuated(dve, 4 + i)
                kd = KD[:, i, :].rearrange("p (h c x d) -> p h c x d", h=2, c=2, x=2)
                rotate(KVRAW[:, i, 0:P].rearrange("p (h x d) -> p h x d", h=2, x=2),
                       [kd[:, :, c] for c in range(2)], 2, i, krot_ready)
            dve.wait_ge(z_ready, GH)
            v.scalar_tensor_tensor(W0, TMP, -1.0, TMP, ALU.mult, ALU.min).then_inc(gate_neg, 1)
            for i in range(TT):
                evacuated(dve, i)
                evacuated(dve, 2 + i)
                rotate(SQ[:, i, :].rearrange("p (h x d) -> p h x d", h=QH, x=2),
                       [SQR[:, i, :].rearrange("p (h x d) -> p h x d", h=QH, x=2)], QH, i, qrot_ready)
            dve.wait_ge(kt_full, 1)
            v.tensor_copy(KTT[:].rearrange("p g t -> p (g t)"), bk(3)).then_inc(kt_ready, 1)
            for a in range(2, 4):
                dve.wait_ge(qt_full, a + 1)
                v.tensor_copy(qT[:, 2 * a:2 * a + 2, :], PS[:, 4 + a, :].rearrange("p (k t) -> p k t", k=2)).then_inc(qt_ready, 1)

            def decay_exponents():
                dve.wait_ge(gate_sp, 1)
                link(v.scalar_tensor_tensor(W2, TMP, 0.0, W1, ALU.min, ALU.subtract))
                link(v.memset(W0, 1.0))
                link(v.memset(W0.rearrange("p (n t) -> p n t", t=P)[:, :, 0:1], 0.0))
                link(v.tensor_tensor_scan(B, W0, W2, 0.0, ALU.mult, ALU.add))
                bh = B.rearrange("p (h t) -> p h t", h=GH)
                v.tensor_tensor(W0.rearrange("p (h t) -> p h t", h=GH)[:, :, 0:P],
                                bh[:, :, P - 1:P].broadcast_to([P, GH, P]), bh[:, :, 0:P], ALU.subtract).then_inc(decay_in, 1)
                for w, half in ((W1, 64), (W2, 32)):
                    n = GH * SEQ // (2 * half)
                    wv = w.rearrange("p (n s t) -> p n s t", s=2, t=half)
                    bv = B.rearrange("p (n s t) -> p n s t", s=2, t=half)
                    ref = bv[:, :, 0, half - 1:half].broadcast_to([P, n, half])
                    v.tensor_tensor(wv[:, :, 0, :], ref, bv[:, :, 0, :], ALU.subtract)
                    v.tensor_tensor(wv[:, :, 1, :], bv[:, :, 1, :], ref, ALU.subtract).then_inc(decay_in, 1)
                tv = TMP.rearrange("p (n t) -> p n t", t=32)
                bv = B.rearrange("p (n t) -> p n t", t=32)
                link(v.tensor_tensor(tv, bv, bv[:, :, 15:16].broadcast_to([P, GH * SEQ // 32, 32]), ALU.subtract))
                v.tensor_scalar(TMP, TMP, -CLAMP * TAU, CLAMP * TAU, ALU.max, ALU.min).then_inc(decay_in, 1)

            def decay_products():
                for u in range(6, 10):
                    evacuated(dve, u)
                dve.wait_ge(decay_out, 1)
                a, q, k = (t.rearrange("p (h t) -> p h t", h=GH) for t in (W0, GQT, GKT))
                v.tensor_tensor(a[:, :, 0:P], a[:, :, 0:P], k[:, :, 0:P], ALU.mult)
                v.scalar_tensor_tensor(a[:, :, P:SEQ], a[:, :, P:SEQ], GSCALE, q[:, :, P:SEQ], ALU.mult, ALU.mult).then_inc(gla_ops, 1)
                for n, (w, half) in enumerate(((W1, 64), (W2, 32))):
                    dve.wait_ge(decay_out, n + 2)
                    a, q, k = (t.rearrange("p (n s t) -> p n s t", s=2, t=half) for t in (w, GQT, GKT))
                    v.tensor_tensor(a[:, :, 0, :], a[:, :, 0, :], k[:, :, 0, :], ALU.mult)
                    v.scalar_tensor_tensor(a[:, :, 1, :], a[:, :, 1, :], GSCALE, q[:, :, 1, :], ALU.mult, ALU.mult).then_inc(gla_ops, 1)
                dve.wait_ge(decay_out, 5)
                dve.wait_ge(gla_ops, 3)
                v.scalar_tensor_tensor(GQT, B, GSCALE, GQT, ALU.mult, ALU.mult).then_inc(gla_ops, 1)
                v.tensor_tensor(GKT, TMP, GKT, ALU.mult).then_inc(gla_ops, 1)

            mask = TAB[:, T_SWA:T_SWA + SEQ]

            def swa_mask(n):
                i, g4 = n // (NGRP // TT), n % (NGRP // TT)
                q, ns = n % 2, (i + 1) * P
                dve.wait_ge(sw_s, n + 1)
                m = (mask[:, P:SEQ] if i == 0 else mask).unsqueeze(1).broadcast_to([P, 2, ns])
                for a in range(2):
                    last = v.scalar_tensor_tensor(SS[:, q, 2 * a:2 * a + 2, 0:ns],
                                                  PS[:, 4 + a, :].rearrange("p (h s) -> p h s", h=2)[:, :, 0:ns],
                                                  QSCALE, m, ALU.mult, ALU.add)
                    last.then_inc(sw_masked, 1)
                dve.wait_ge(sw_masked, 2 * (n + 1))
                link(v.tensor_reduce(S_MX[q], SS[:, q, :, 0:ns], AX_X, ALU.max))
                sink = ROW[:, R_SINK + HG * g4:R_SINK + HG * (g4 + 1)]
                link(v.tensor_tensor(S_MX[q], S_MX[q], sink, ALU.max))
                v.tensor_scalar(S_NM[q], S_MX[q], -1.0, None, ALU.mult)
                v.tensor_tensor(S_DS[q], sink, S_MX[q], ALU.subtract).then_inc(sw_max, 1)

            def swa_pt(n):
                i = n // (NGRP // TT)
                dve.wait_ge(sw_t, n + 1)
                v.tensor_copy(PTS[:, n % 2, 2:4, 0:(i + 1) * P],
                              PS[:, 7, :].rearrange("p (h s) -> p h s", h=2)[:, :, 0:(i + 1) * P]).then_inc(sw_ptV, 1)

            def swa_out(n):
                i, g4 = n // (NGRP // TT), n % (NGRP // TT)
                q = n % 2
                dve.wait_ge(sw_exp, n + 1)
                if n >= 2:
                    dve.wait_ge(sw_out, n - 1)
                link(v.tensor_tensor(S_DEN[q], S_SUM[q], S_ES[q], ALU.add))
                link(v.reciprocal(S_RD[q], S_DEN[q]))
                dve.wait_ge(sw_o, n + 1)
                v.tensor_tensor(SQR[:, i, g4 * HG * HD:(g4 + 1) * HG * HD].rearrange("p (a b d) -> p b a d", a=2, b=2),
                                PS[:, 3, 0:HG * HD].rearrange("p (b a d) -> p b a d", a=2, b=2),
                                S_RD[q].rearrange("p (b a) -> p b a", a=2).unsqueeze(3).broadcast_to([P, 2, 2, HD]),
                                ALU.mult).then_inc(sw_out, 1)

            def gr_finish(u):
                n, m = (u - 14) // 2, u % 2
                part = GR[:, m, n * BW:(n + 1) * BW]
                dve.wait_ge(gr_sig, u - 13)
                link(v.tensor_tensor(part, part, SIG[:, m * BW:(m + 1) * BW], ALU.mult))
                pv = part.rearrange("p (h d) -> p h d", h=2)
                v.tensor_tensor(pv, pv, ROW[:, R_HEAD:R_HEAD + GDV].unsqueeze(1).broadcast_to([P, 2, GDV]),
                                ALU.mult).then_inc(gr_ready, 1)

            dve.wait_ge(row_in, 16)
            for n in range(NGRP + 2):
                u = 10 + n
                if u < 14:
                    token_major(u, GV[:, u % 2, (u - 10) // 2 * BW:((u - 10) // 2 + 1) * BW], BW)
                elif u < 18:
                    token_major(u, GR[:, u % 2, (u - 14) // 2 * BW:((u - 14) // 2 + 1) * BW], BW)
                if n - 2 >= 0:
                    swa_out(n - 2)
                if 0 <= n - 1 < NGRP:
                    swa_pt(n - 1)
                if n < NGRP:
                    swa_mask(n)
                if n == 1:
                    decay_exponents()
                if n == 4:
                    decay_products()
                if n >= 6:
                    gr_finish(n + 8)

            def copy_t(dst, full, done):
                for a in range(2, 4):
                    dve.wait_ge(full, a + 1)
                    v.tensor_copy(dst[:, 2 * a:2 * a + 2, :], PS[:, 4 + a, :].rearrange("p (k t) -> p k t", k=2)).then_inc(done, 1)

            copy_t(obT, obt_full, obt_ready)

            dve.wait_ge(gla_zero, 1)
            dve.wait_ge(gla_sc, 1)
            sc = PS[:, 4:8, :]
            v.tensor_copy(PTG[:, :, 0, :], sc[:, :, 0:P])
            tiles = sc[:, :, P:P + SEQ].rearrange("p h (i c) -> p h i c", i=TT)
            v.tensor_copy(PTG[0:64, :, 1:3, 64:128], tiles[0:64, :, :, 0:64])
            for q in range(2):
                s = slice(64 * q, 64 * q + 32)
                v.tensor_copy(PTG[s, :, 1:3, 64 * q + 32:64 * q + 64], tiles[s, :, :, 64:96])
            for q in range(4):
                s = slice(32 * q, 32 * q + 32)
                last = v.tensor_tensor(PTG[s, :, 1:3, 32 * q:32 * q + 32], tiles[s, :, :, 96:128],
                                       TAB[s, T_DIAG:T_DIAG + 32].unsqueeze(1).unsqueeze(1).broadcast_to([32, GH, TT, 32]), ALU.mult)
            last.then_inc(gla_pt, 1)
            mean_eps(S_GS, S_GVAR, GDV, gla_sq, GH * TT, gla_var)
            dve.wait_ge(gla_sd, 1)
            link(v.reciprocal(S_GRS, S_GSD))
            dve.wait_ge(gr_ready, 4)
            for h in range(GH):
                for i in range(TT):
                    g = GR[:, i, h * GDV:(h + 1) * GDV]
                    n = TT * h + i
                    v.scalar_tensor_tensor(g, PS[:, 4 + h, i * GDV:(i + 1) * GDV], S_GRS[:, n:n + 1], g,
                                           ALU.mult, ALU.mult).then_inc(gla_oa, 1)
            copy_t(oaT, oat_full, oat_ready)
            dve.wait_ge(be1_in, 16)
            for part in range(2):
                link(v.tensor_copy(BE1[0:NE], BE1R))
                link(v.tensor_copy(BE1[(2 - part) * NE:(3 - part) * NE], BE1[0:NE]))
                link(v.tensor_tensor(BE1R, BE1R, BE1[0:NE], ALU.subtract))
            v.tensor_copy(BE1[0:NE], BE1R).then_inc(be1_ready, 1)

            mixf = SQRf
            for i in (10, 12, 14, 16):
                for half in range(2):
                    u = 2 * i + half
                    c = (i in (12, 16)) * 2 * BW + half * BW
                    part, sg = mixf[:, c:c + BW], SIG[:, half * BW:(half + 1) * BW]
                    evacuated(dve, u - 2)
                    dve.wait_ge(pj_full[u % NPJ], u // NPJ + 1)
                    if i < 14:
                        v.tensor_tensor(part, bk(u % NPJ), sg, ALU.mult).then_inc(pj_free[u % NPJ], 1)
                    else:
                        v.tensor_tensor(sg, bk(u % NPJ), sg, ALU.mult).then_inc(pj_free[u % NPJ], 1)
                        evacuated(dve, u)
                        v.tensor_tensor(part, part, sg, ALU.add).then_inc(mix_ready, 1)
            for i in (17, 18):
                for m in range(TT):
                    u = 2 * i + m
                    xs = X[:, m, (i - 17) * BW:(i - 16) * BW]
                    dve.wait_ge(pj_full[u % NPJ], u // NPJ + 1)
                    v.tensor_tensor(xs, bk(u % NPJ), xs, ALU.add).then_inc(pj_free[u % NPJ], 1)

            mean_eps(S_SS, S_VAR, D, ssq1, TT, var1)
            dve.wait_ge(sd1, 1)
            link(v.reciprocal(S_RS, S_SD))
            for i in range(TT):
                v.tensor_scalar(xn[:, i, :], X[:, i, :], S_RS[:, i:i + 1], None, ALU.mult).then_inc(xn_ready, 1)
            for i in range(TT):
                dve.wait_ge(xp1, i + 1)
                v.tensor_tensor(REST[:, i, :], xn[:, i, :], XP[0][:, i, :], ALU.subtract).then_inc(rest1, 1)
            gffn = col(C_GFFN, KT)
            for a in range(4):
                dve.wait_ge(xnT_full, a + 1)
                v.tensor_tensor(xnT[:, 2 * a:2 * a + 2, :], PS[:, 4 + a, :].rearrange("p (k t) -> p k t", k=2),
                                gffn[:, 2 * a:2 * a + 2].unsqueeze(2).broadcast_to([P, 2, SEQ]), ALU.mult).then_inc(xnT_ready, 1)
            for i in range(TT):
                dve.wait_ge(xp2, i + 1)
                v.tensor_tensor(XP[2][:, i, :], REST[:, i, :], XP[1][:, i, :], ALU.subtract).then_inc(xp3, 1)
            dve.wait_ge(lg_full, 1)
            link(v.tensor_tensor(LG, PS[:, 3, 0:TT * NE].rearrange("p (i e) -> p i e", i=TT),
                                 ROW[:, R_ROUTER:R_ROUTER + NE].unsqueeze(1).broadcast_to([P, TT, NE]), ALU.add))
            for i in range(TT):
                link(v.max(S_V8[i], LG[:, i, :]))
                v.tensor_scalar(S_NV[i], S_V8[i][:, 0:1], -1.0, None, ALU.mult).then_inc(top_ready, 1)
                link(v.max_index(IDX[i][:], S_V8[i], LG[:, i, :]))
                link(v.tensor_copy(S_IF[i], IDX[i][:]))
            experts = TAB[:, T_IOTA:T_IOTA + NE]
            for i in range(TT):
                for k in range(TOPK):
                    last = v.tensor_scalar(OH[:, i, k, :], experts, S_IF[i][:, k:k + 1], None, ALU.is_equal)
                link(last)
                v.tensor_reduce(MK[:, i, :], OH[:, i].rearrange("p k e -> p e k"), AX_X, ALU.add).then_inc(mask_ready, 1)
            for i in range(TT):
                dve.wait_ge(eg_ready, i + 1)
                link(v.reciprocal(S_RG[i], S_ES4[i]))
                link(v.tensor_scalar(S_GT[i], S_EG[i], S_RG[i], None, ALU.mult))
                for k in range(TOPK):
                    last = v.tensor_scalar(OG[:, i, k, :], OH[:, i, k, :], S_GT[i][:, k:k + 1], None, ALU.mult)
                link(last)
                v.tensor_reduce(GT_[:, i, :], OG[:, i].rearrange("p k e -> p e k"), AX_X, ALU.add).then_inc(gat_ready, 1)
            dve.wait_ge(mask_ready, TT)
            dve.wait_ge(rank_full, 1)
            link(v.tensor_scalar(BIG, MK, -1e6, 1e6, ALU.mult, ALU.add))
            link(v.tensor_tensor(BIG, BIG, PS[:, 4, 0:TT * NE].rearrange("p (i e) -> p i e", i=TT), ALU.add))
            v.memset(RK[:, :, PASSES * NE:PASSES * NE + 1], 1e6)
            for b in range(PASSES):
                v.tensor_scalar(RK[:, :, b * NE:(b + 1) * NE], BIG, float(-b * SLOTS), None, ALU.add)
            link(v.tensor_reduce(S_CNT, PS[:, 4, 2 * NE:3 * NE], AX_X, ALU.max))
            link(v.tensor_scalar(S_CMP, TAB[:, T_THR:T_THR + PASSES], S_CNT, None, ALU.is_lt))
            link(v.tensor_reduce(S_NP, S_CMP, AX_X, ALU.add))
            v.tensor_copy(NBI[:], S_NP).then_inc(np_ready, 1)
            dve.wait_ge(gatT_full, 1)
            v.tensor_copy(GATT, PS[0:NE, 5, 0:SEQ]).then_inc(gatT_ready, 1)
            v.memset(Y, 0.0).then_inc(y_ready, 1)
            v.memset(SELT[:, 0, :], 0.0).then_inc(selT_a, 1)
            dve.wait_ge(gatT_ready, 1)
            v.memset(SELT[:, 1, :], 0.0).then_inc(selT_b, 1)
            dve.wait_ge(xp3, TT)
            v.memset(LIN, 0.0).then_inc(act_ready, 1)

            iota = TAB[:, T_IOTA:T_IOTA + SLOTS].unsqueeze(1).broadcast_to([P, TT, SLOTS])
            iota2 = TAB[:, T_IOTA:T_IOTA + SLOTS].unsqueeze(1).unsqueeze(1).broadcast_to([P, TT, 2, SLOTS])

            def spread(a):
                return a.broadcast_to([P, a.shape[1], SLOTS])

            def spread2(a):
                return a.unsqueeze(3).broadcast_to([P, TT, 2, SLOTS])

            def hot(a):
                return TAB[0:3 * NE, a].broadcast_to([3 * NE, SLOTS])

            v.tensor_tensor(SEL, iota, spread(RK[:, :, 0:1]), ALU.is_equal).then_inc(sel_ready, 1)
            v.tensor_copy(SELE, hot(slice(T_HOT, T_HOT + 1))).then_inc(sele_ready, 1)
            x_bank = PS[:, 7, :].rearrange("p (k c) -> p k c", k=KT)
            dve.wait_ge(xg_full, 1)
            v.tensor_tensor(XT, x_bank, spread(gffn.unsqueeze(2)), ALU.mult).then_inc(xt_ready, 1)
            dve.wait_ge(np_ready, 1)
            passes = dve.value_load(NBI[0:1, 0:1], min_val=1, max_val=PASSES)
            with dve.Fori(0, passes) as b:
                with dve.Fori(0, NE) as e:
                    done = b * NE + e
                    dve.wait_ge(chunk_used, done * CH + 1)
                    v.tensor_tensor(SEL, iota, spread(RK[:, :, bass.ds(done + 1, 1)]), ALU.is_equal).then_inc(sel_ready, 1)
                    v.tensor_tensor(SELG, iota2, spread2(RK[:, :, bass.ds(done, 1)]), ALU.is_equal).then_inc(selg_raw, 1)
                    v.tensor_copy(SELE, hot(bass.ds(T_HOT + (e + 1) % NE, 1))).then_inc(sele_ready, 1)
                    dve.wait_ge(selg_raw, done + 1)
                    v.tensor_tensor(SELG, SELG, spread2(GT_[:, :, bass.ds(e, 1)]), ALU.mult).then_inc(selg_ready, 1)
                    dve.wait_ge(chunk_used, done * CH + CH1)
                    dve.wait_ge(act_ready, done + 1)
                    v.tensor_scalar(GLU, bk(4), LIMIT, None, ALU.min).then_inc(glu_ready, 1)
                    v.tensor_scalar(LIN, bk(5), -LIMIT, LIMIT, ALU.max, ALU.min).then_inc(u_read, 1)
                    dve.wait_ge(glu_ready, done + 1)
                    dve.wait_ge(u_read, done + 1)
                    v.scalar_tensor_tensor(LIN, LIN, 1.0, GLU, ALU.add, ALU.mult).then_inc(lin_ready, 1)
                    dve.wait_ge(lin_ready, done + 1)
                    dve.wait_ge(sgm_ready, done + 1)
                    v.tensor_tensor(LIN, LIN, SGM, ALU.mult).then_inc(act_ready, 1)
                    dve.wait_ge(xg_full, done + 2)
                    v.tensor_tensor(XT, x_bank, spread(gffn.unsqueeze(2)), ALU.mult).then_inc(xt_ready, 1)
                    dve.wait_ge(selT_full, done + 1)
                    v.tensor_copy(SELT[SLOTS:P, 1, 0:SEQ], PS[SLOTS:P, 5, 0:SEQ]).then_inc(selT_b, 1)
            dve.wait_ge(moe_done, 1)
            for i in range(TT):
                for n in range(2):
                    xs = X[:, i, n * 512:(n + 1) * 512]
                    v.tensor_tensor(xs, bk(2 * i + n), xs, ALU.add).then_inc(xf_ready, 1)
            mean_eps(S_SS, S_VAR, D, ssqf, TT, varf)
            dve.wait_ge(sdf, 1)
            link(v.reciprocal(S_RS, S_SD))
            dve.wait_ge(gfin_in, 16)
            for i in range(TT):
                v.scalar_tensor_tensor(OUTB[:, i, :], X[:, i, :], S_RS[:, i:i + 1], SIG[:], ALU.mult, ALU.mult).then_inc(out_ready, 1)


def kernel(**inputs):
    import concourse.bacc as bacc
    from concourse.bass_utils import run_bass_kernel_spmd

    f = {k: np.asarray(a) for k, a in inputs.items()}
    x = f["x"].reshape(SEQ, D)
    w_in, b_in = f["w_in"][0], f["b_in"][0]
    at = {}
    off = 0
    for name, size in (("gq", 512), ("gk", 512), ("gv", 1024), ("gr", 1024), ("lr", 16), ("sq", 1024),
                       ("sk", 128), ("sv", 128), ("ga", 1024), ("gb", 1024)):
        at[name] = off
        off += size

    def ktiles(w):
        return w.reshape(KT, P, -1).transpose(1, 0, 2).reshape(P, -1)

    def columns(name):
        if name[:2] in ("gl", "sw", "wo"):
            w = f[{"gl": "w_gla_out", "sw": "w_swa_out", "wo": "w_out"}[name[:2]]][0]
            n = int(name[-1]) * BW
            return w[:, n:n + BW]
        n = at[name[:2]] + (int(name[2]) * BW if len(name) > 2 else 0)
        return w_in[:, n:n + BW]

    def feature_columns(a):
        return a.reshape(-1, P).T

    s0 = at["sk"]
    lr0 = at["lr"]
    cv = np.zeros((P, NCV), np.float32)
    for c, a in ((C_GMIX, f["g_mix"][0]), (C_BQ, b_in[at["gq"]:at["gq"] + 512]), (C_BK, b_in[at["gk"]:at["gk"] + 512]),
                 (C_BGA, b_in[at["ga"]:at["ga"] + D]), (C_BGB, b_in[at["gb"]:at["gb"] + D]),
                 (C_BGATE, f["b_gla_gate"][0]), (C_GFFN, f["g_ffn"][0])):
        cv[:, c:c + a.size // P] = feature_columns(a)
    cv[0:RANK, C_BLR] = b_in[lr0:lr0 + RANK]
    brow = np.zeros((len(BIAS_ROWS), BW), np.float32)
    for n, name in enumerate(BIAS_ROWS):
        if name == "skv":
            brow[n, 0:KVW] = b_in[s0:s0 + KVW]
        else:
            c = at[name[:2]] + int(name[2]) * BW
            brow[n] = b_in[c:c + BW]
    sinks = f["sinks"][0].reshape(QH // HG, 2, 2).transpose(0, 2, 1).reshape(-1)
    rows = np.concatenate([sinks, f["g_gla_head"][0], f["b_router"][0]])[None, :]
    w1 = f["w_e1"][0].reshape(NE, KT, P, D, 2).transpose(0, 1, 2, 4, 3).reshape(NE, CH1, P, SLOTW)
    w2 = f["w_e2"][0].reshape(NE, CH2, 2, P, D).transpose(0, 1, 3, 2, 4).reshape(NE, CH2, P, SLOTW)
    arrays = {
        "x": x,
        "wblk": np.stack([ktiles(columns(n)) for n in BLOCKS if n != "skv"]),
        "wskv": ktiles(np.concatenate([w_in[:, s0:s0 + KVW], w_in[:, lr0:lr0 + RANK]], axis=1)),
        "wgate": f["w_gla_gate"][0],
        "cv": cv,
        "rows": rows,
        "brow": brow,
        "tab": tables(),
        "wrout": f["w_router"][0].reshape(KT, P, NE).transpose(1, 0, 2),
        "be1": f["b_e1"][0].reshape(NE, D, 2).transpose(0, 2, 1).reshape(NE, 2 * D),
        "be2": f["b_e2"][0],
        "gfin": f["g_final"][None, :],
        "wexp": np.concatenate([w1, w2], axis=1).reshape(NE * CH, P, SLOTW),
    }
    arrays = {k: np.ascontiguousarray(a) for k, a in arrays.items()}
    nc = bacc.Bacc("TRN2", target_bir_lowering=False, num_devices=1)
    args = [nc.dram_tensor(k, a.shape, F32, kind="ExternalInput").ap() for k, a in arrays.items()]
    out = nc.dram_tensor("out", (SEQ, D), F32, kind="ExternalOutput").ap()
    program(nc, *args, out)
    res = run_bass_kernel_spmd(nc, [arrays], core_ids=[0])
    return res.results[0]["out"].reshape(1, SEQ, D)
```

```python
from contextlib import ExitStack

import numpy as np

import concourse.bass as bass
from concourse import mybir

ALU = mybir.AluOpType
ACT = mybir.ActivationFunctionType
F32 = mybir.dt.float32
F32R = mybir.dt.float32r
BF16 = mybir.dt.bfloat16
U32 = mybir.dt.uint32
I32 = mybir.dt.int32
AX_X = mybir.AxisListType.X

P = 128
D = 1024
SEQ = 256
TT = SEQ // P
KT = D // P
EPS = 1e-5
GH, GDK, GDV = 4, 128, 256
TAU = 16.0
GSCALE = GDK ** -0.5
CLAMP = 38.0
RANK = 16
QH, HD = 16, 64
KVW = 256
HALF = HD // 2
QSCALE = HD ** -0.5
HG = 4
NGRP = QH // HG * TT
NEG = -1e30
NE = 32
TOPK = 4
SLOTS = 64
PASSES = SEQ // SLOTS
LIMIT = 7.0
ALPHA = 1.702
FT = D // P
BW = 512
NSLOT = 16
SLOTW = 2048
RING0 = 10
W_SLOTS = [1, 2, 4, 6, 8]
H_SLOTS = [3, 5, 7, 9]
HTL_SLOT = 0
CH1, CH2 = 8, 4
CH = CH1 + CH2
UNROLL = 4

BLOCKS = ["sq0", "sq1", "skv", "gq", "gk", "gv0", "gv1", "gr0", "gr1", "ga0", "ga1", "gb0", "gb1",
          "glao0", "glao1", "swao0", "swao1", "wo0", "wo1"]
NB = len(BLOCKS)
NU = 2 * NB
KH = KT // 2
GATES_DONE = 2 * (BLOCKS.index("gb1") + 1)
SKVW = 384
TOKEN_MAJOR = {"sq0", "sq1", "skv", "gv0", "gv1", "gr0", "gr1", "wo0", "wo1"}
BIAS_ROWS = ["sq0", "sq1", "skv", "gv0", "gv1", "gr0", "gr1"]
NPJ = 3

C_GMIX, C_BQ, C_BK, C_BGA, C_BGB, C_BGATE, C_GFFN, C_BLR = 0, 8, 12, 16, 24, 32, 36, 44
NCV = 45
R_SINK, R_HEAD, R_ROUTER = 0, 16, 272
NROW = 304
T_ID = 0
T_SWA = T_ID + P
T_DIAG = T_SWA + SEQ
T_COS = T_DIAG + 32
T_SIN = T_COS + TT * HALF
T_TRI = T_SIN + TT * HALF
T_ONE = T_TRI + P
T_IOTA = T_ONE + P
T_THR = T_IOTA + SLOTS
T_HOT = T_THR + PASSES
NTAB = T_HOT + NE


def tables():
    t = np.zeros((P, NTAB), np.float32)
    p = np.arange(P)[:, None]
    t[:, T_ID:T_ID + P] = np.eye(P)
    s = np.arange(SEQ)[None, :]
    t[:, T_SWA:T_SWA + SEQ] = np.where((s > p) & (s <= p + P), 0.0, NEG)
    t[:, T_DIAG:T_DIAG + 32] = np.arange(32)[None, :] >= p % 32
    inv = np.float32(10000.0) ** (-np.arange(HALF, dtype=np.float32) / np.float32(HALF))
    for i in range(TT):
        ang = (np.arange(P, dtype=np.float32) + np.float32(P * i))[:, None] * inv[None, :]
        t[:, T_COS + i * HALF:T_COS + (i + 1) * HALF] = np.cos(ang)
        t[:, T_SIN + i * HALF:T_SIN + (i + 1) * HALF] = np.sin(ang)
    t[:, T_TRI:T_TRI + P] = p < np.arange(P)[None, :]
    t[:, T_ONE:T_ONE + P] = 1.0
    t[:, T_IOTA:T_IOTA + SLOTS] = np.arange(SLOTS)[None, :]
    t[:, T_THR:T_THR + PASSES] = np.arange(PASSES)[None, :] * SLOTS
    t[:, T_THR] = -1.0
    t[:, T_HOT:T_HOT + NE] = np.arange(NE)[None, :] == p % NE
    return t


def program(nc, x, wblk, wskv, wgate, cv, rows, brow, tab, wrout, be1, be2, gfin, wexp, out):
    with ExitStack() as ctx:
        def sb(name, shape, dt=F32):
            return ctx.enter_context(nc.sbuf_tensor(name, shape, dt))

        def sem(name):
            return ctx.enter_context(nc.semaphore(name))

        shapes = {"HT": [P, KT, SEQ], "GV": [P, TT, D], "GR": [P, TT, D], "SQ": [P, TT, D], "SQR": [P, TT, D]}
        with ExitStack() as rounded:
            slots_R = [rounded.enter_context(nc.sbuf_tensor(f"slot{n}_R", [P, SLOTW], F32R)) for n in range(NSLOT)]
            HT_R, GV_R, GR_R, SQ_R, SQR_R = [
                rounded.enter_context(nc.sbuf_tensor(name + "_R", shape, F32R)) for name, shape in shapes.items()]
        ring = sb("ring", [P, NSLOT * SLOTW])
        HT = sb("HT", shapes["HT"])
        GV = sb("GV", shapes["GV"])
        GR = sb("GR", shapes["GR"])
        SQ = sb("SQ", shapes["SQ"])
        SQR = sb("SQR", shapes["SQR"])
        X = sb("X", [P, TT, D])
        SIG = sb("SIG", [P, D])
        KVRAW = sb("KVRAW", [P, TT, KVW])
        KD = sb("KD", [P, TT, 4 * HD])
        KTT = sb("KTT", [P, 2, SEQ])
        PTG = sb("PTG", [P, GH, 3, P])
        BRW = sb("BRW", [P, 2, BW])
        CV = sb("CV", [P, NCV])
        ROW = sb("ROW", [P, NROW])
        TAB = sb("TAB", [P, NTAB])
        WR = sb("WR", [P, KT, NE])
        BE1 = sb("BE1", [3 * NE, 2 * D], BF16)
        SM = sb("SM", [P, 160])
        NBI = sb("NBI", [P, 1], I32)

        tail = [RING0 * SLOTW]

        def in_tail(n):
            tail[0] += n
            assert tail[0] <= NSLOT * SLOTW
            return ring[:, tail[0] - n:tail[0]]

        GQT, GKT, B, W0, W1, W2, TMP = [in_tail(GH * SEQ) for _ in range(7)]
        SS = in_tail(2 * HG * SEQ).rearrange("p (b h s) -> p b h s", b=2, h=HG)
        PTS = in_tail(2 * HG * SEQ).rearrange("p (b h s) -> p b h s", b=2, h=HG)
        WG = in_tail(GH * GDK)
        LRT = in_tail(SEQ)

        ident = TAB[:, T_ID:T_ID + P]

        def col(c, n=1, p=P):
            return CV[0:p, c:c + n]

        def small(a, n):
            return SM[:, a:a + n]
        S_SS, S_VAR, S_SD, S_RS = small(0, 2), small(2, 2), small(4, 2), small(6, 2)
        S_MX = [small(10 + 4 * b, 4) for b in range(2)]
        S_NM = [small(18 + 4 * b, 4) for b in range(2)]
        S_SUM = [small(26 + 4 * b, 4) for b in range(2)]
        S_DS = [small(34 + 4 * b, 4) for b in range(2)]
        S_ES = [small(42 + 4 * b, 4) for b in range(2)]
        S_DEN = [small(50 + 4 * b, 4) for b in range(2)]
        S_RD = [small(58 + 4 * b, 4) for b in range(2)]
        S_GS, S_GVAR, S_GSD, S_GRS = small(66, 8), small(74, 8), small(82, 8), small(90, 8)
        S_V8 = [small(98 + 8 * i, 8) for i in range(TT)]
        S_IF = [small(114 + 8 * i, 8) for i in range(TT)]
        S_NV = [small(130 + i, 1) for i in range(TT)]
        S_EG = [small(132 + 4 * i, 4) for i in range(TT)]
        S_ES4 = [small(140 + i, 1) for i in range(TT)]
        S_RG = [small(142 + i, 1) for i in range(TT)]
        S_GT = [small(144 + 4 * i, 4) for i in range(TT)]
        S_CNT, S_CMP, S_NP = small(152, 1), small(153, PASSES), small(157, 1)
        IDX = [sb(f"IDX{i}", [P, 8], U32) for i in range(TT)]

        RSR, DIAG = SIG[:, 0:SEQ], SIG[:, BW:BW + SEQ]

        def feature(t):
            return t[:].rearrange("p i d -> p (i d)").rearrange("p (k t) -> p k t", k=KT)

        def slot(s, rounded=False):
            return slots_R[s][:] if rounded else ring[:, s * SLOTW:(s + 1) * SLOTW]

        HTL, HTL_R = (slot(HTL_SLOT, r).rearrange("p (k t) -> p k t", k=KT) for r in (False, True))
        qT = feature(SQ)
        HT2 = (HT_R[:], HTL_R)
        OB2 = (feature(SQ_R), feature(SQR_R))
        OA2 = (feature(GV_R), feature(GR_R))
        MIX2 = OA2
        HTf = HT[:].rearrange("p k t -> p (k t)")
        xn = HTf.rearrange("p (i d) -> p i d", i=TT)
        xnT = feature(GV)
        GRf = GR[:].rearrange("p i d -> p (i d)")
        RK = GRf[:, 0:TT * 129].rearrange("p (i e) -> p i e", i=TT)
        GT_ = GRf[:, 264:264 + TT * NE].rearrange("p (i e) -> p i e", i=TT)
        LG = GRf[:, 328:328 + TT * NE].rearrange("p (i e) -> p i e", i=TT)
        MK = GRf[:, 392:392 + TT * NE].rearrange("p (i e) -> p i e", i=TT)
        OH = GRf[:, 456:456 + TT * TOPK * NE].rearrange("p (i k e) -> p i k e", i=TT, k=TOPK)
        BIG = GRf[:, 712:712 + TT * NE].rearrange("p (i e) -> p i e", i=TT)
        KVf = KVRAW[:].rearrange("p i d -> p (i d)")
        OG = KVf[:, 0:TT * TOPK * NE].rearrange("p (i k e) -> p i k e", i=TT, k=TOPK)
        GATT = KVf[0:NE, 256:256 + SEQ]
        BE2 = [KD[0:NE].rearrange("p i d -> p (i d)"), KTT[0:NE].rearrange("p g t -> p (g t)")]
        BE1R = GRf[0:NE, :]
        SQRf = SQR[:].rearrange("p i d -> p (i d)")
        SQf = SQ[:].rearrange("p i d -> p (i d)")
        XP = [a.bitcast(BF16).rearrange("p (i d) -> p i d", i=TT)
              for a in (SQRf[:, 0:D], SQRf[:, D:2 * D], GRf[:, D:2 * D])]
        REST = SQf.rearrange("p (i d) -> p i d", i=TT)
        XT = SQf[:, 0:512].rearrange("p (k c) -> p k c", k=KT)
        GLU, LIN, SGM = SQf[:, 512:1024], SQf[:, 1024:1536], SQf[:, 1536:2048]
        PTf = PTG[:].rearrange("p h b t -> p (h b t)")
        AT = PTf[:, 0:512]
        Y = PTf[:, 512:1024]
        SELG = PTf[:, 1024:1280].rearrange("p (i r c) -> p i r c", i=TT, r=2)
        SEL = PTf[:, 1280:1344].bitcast(BF16).rearrange("p (i c) -> p i c", i=TT)
        SELE = PTf[0:3 * NE, 1344:1376].bitcast(BF16)
        KDf = KD[:].rearrange("p i d -> p (i d)")
        KTf = KTT[:].rearrange("p g t -> p (g t)")
        MIX = [SIG[:, 0:BW], SIG[:, BW:D], KVf, KDf]
        GB = [PTf[:, 0:BW], PTf[:, BW:D], PTf[:, D:D + BW], KTf]
        SELT = BRW
        OUTB = GV

        PS = ctx.enter_context(nc.psum_tensor("PS", [P, 8, 512], F32))

        def bk(b, w=512, p=P):
            return PS[0:p, b, 0:w]

        x_in, ident_in, tab_in, cv_in, row_in = sem("x_in"), sem("ident_in"), sem("tab_in"), sem("cv_in"), sem("row_in")
        wg_in, wr_in, be1_in, be2_in, gfin_in = sem("wg_in"), sem("wr_in"), sem("be1_in"), sem("be2_in"), sem("gfin_in")
        unit_in = [sem(f"unit_in{q}") for q in range(len(W_SLOTS))]
        hi_ready = sem("hi_ready")
        lo_v, lo_p = sem("lo_v"), sem("lo_p")
        first_used = sem("first_used")
        bias_in = [sem(f"bias_in{q}") for q in range(2)]
        pj_full = [sem(f"pj_full{b}") for b in range(NPJ)]
        pj_free = [sem(f"pj_free{b}") for b in range(NPJ)]
        ssq0, var0, sd0 = sem("ssq0"), sem("var0"), sem("sd0")
        diag_ready, rsr_full, xt_full, ht_raw, ht_hi, ht_ready = (
            sem("diag_ready"), sem("rsr_full"), sem("xt_full"), sem("ht_raw"), sem("ht_hi"), sem("ht_ready"))
        lr_full, lr_ready, z_full, z_ready = sem("lr_full"), sem("lr_ready"), sem("z_full"), sem("z_ready")
        qrot_ready, qt_full, qt_ready = sem("qrot_ready"), sem("qt_full"), sem("qt_ready")
        krot_ready, kt_full, kt_ready = sem("krot_ready"), sem("kt_full"), sem("kt_ready")
        gate_neg, gate_sp, decay_in, decay_out = sem("gate_neg"), sem("gate_sp"), sem("decay_in"), sem("decay_out")
        gla_ops, gla_sc, gla_pt, gla_o, gla_sq, gla_var, gla_sd, gla_oa = (
            sem("gla_ops"), sem("gla_sc"), sem("gla_pt"), sem("gla_o"), sem("gla_sq"), sem("gla_var"), sem("gla_sd"), sem("gla_oa"))
        gla_zero = sem("gla_zero")
        gr_sig, gr_ready = sem("gr_sig"), sem("gr_ready")
        oat_full, oat_hi, oat_lo = sem("oat_full"), sem("oat_hi"), sem("oat_lo")
        obt_full, obt_hi, obt_lo = sem("obt_full"), sem("obt_hi"), sem("obt_lo")
        sw_s, sw_masked, sw_max, sw_exp = sem("sw_s"), sem("sw_masked"), sem("sw_max"), sem("sw_exp")
        sw_t, sw_ptA, sw_ptV, sw_o, sw_out = sem("sw_t"), sem("sw_ptA"), sem("sw_ptV"), sem("sw_o"), sem("sw_out")
        mix_ready, mix_hi, mix_lo = sem("mix_ready"), sem("mix_hi"), sem("mix_lo")
        ssq1, var1, sd1, xn_ready, xnT_full, xnT_ready, lg_full = (
            sem("ssq1"), sem("var1"), sem("sd1"), sem("xn_ready"), sem("xnT_full"), sem("xnT_ready"), sem("lg_full"))
        top_ready, eg_ready, mask_ready, rank_full, gat_ready, gatT_full, gatT_ready, np_ready = (
            sem("top_ready"), sem("eg_ready"), sem("mask_ready"), sem("rank_full"), sem("gat_ready"), sem("gatT_full"), sem("gatT_ready"), sem("np_ready"))
        slot_in = [sem(f"slot_in{s}") for s in range(NSLOT)]
        chunk_used = sem("chunk_used")
        sel_ready, xg_full, xt_ready = sem("sel_ready"), sem("xg_full"), sem("xt_ready")
        u_read, glu_ready, sgm_ready, act_ready = sem("u_read"), sem("glu_ready"), sem("sgm_ready"), sem("act_ready")
        y_ready, at_full, at_ready = sem("y_ready"), sem("at_full"), sem("at_ready")
        selg_ready, selT_full, selT_a, selT_b = sem("selg_ready"), sem("selT_full"), sem("selT_a"), sem("selT_b")
        sele_ready, xp1, rest1, xp2, xp3, be1_ready = (
            sem("sele_ready"), sem("xp1"), sem("rest1"), sem("xp2"), sem("xp3"), sem("be1_ready"))
        moe_done, xf_ready, ssqf, varf, sdf, out_ready, out_done = (
            sem("moe_done"), sem("xf_ready"), sem("ssqf"), sem("varf"), sem("sdf"), sem("out_ready"), sem("out_done"))
        qt_cp, selg_raw, lin_ready = sem("qt_cp"), sem("selg_raw"), sem("lin_ready")
        dve_step, act_step = sem("dve_step"), sem("act_step")

        block = ctx.enter_context(nc.Block())

        def w_slot(u):
            return (u - (NU - len(W_SLOTS))) % len(W_SLOTS)

        def w_unit(u, rounded=False):
            return slot(W_SLOTS[w_slot(u)], rounded)[:, 0:unit_width(u)]

        def h_unit(u, rounded=False):
            return slot(H_SLOTS[(u - (NU - len(H_SLOTS))) % len(H_SLOTS)], rounded)[:, 0:unit_width(u)]

        def unit_width(u):
            return KH * (SKVW if BLOCKS[u // 2] == "skv" else BW)

        def landed(eng, u):
            fills = sum(w_slot(n) == w_slot(u) for n in range(u + 1))
            eng.wait_ge(unit_in[w_slot(u)], 16 * fills)

        def slot_of(c):
            s = (RING0 + c) % NSLOT
            return s, ring[:, s * SLOTW:(s + 1) * SLOTW]

        def multiplied(eng, u):
            if u % 2 == 0:
                eng.wait_ge(first_used, u // 2 + 1)
            elif BLOCKS[u // 2] == "skv":
                eng.wait_ge(lr_full, 1)
            else:
                eng.wait_ge(pj_full[u % NPJ], u // NPJ + 1)

        def evacuated(eng, u):
            eng.wait_ge(pj_free[u % NPJ], u // NPJ + 1)

        @block.sync
        def _(sp):
            for i in range(TT):
                sp.dma_start(X[:, i, :], x[i * P:(i + 1) * P, :]).then_inc(x_in, 16)

            def bias(n):
                sp.dma_start(BRW[:, n % 2, :], brow[n:n + 1, :].partition_broadcast(P)).then_inc(bias_in[n % 2], 16)

            for u in range(NU):
                if u >= len(W_SLOTS):
                    multiplied(sp, u - len(W_SLOTS))
                if BLOCKS[u // 2] == "skv":
                    sp.dma_start(w_unit(u), wskv[u % 2]).then_inc(unit_in[w_slot(u)], 16)
                else:
                    sp.dma_start(w_unit(u), wblk[u - 2 * (u >= 6)]).then_inc(unit_in[w_slot(u)], 16)
                if u in (1, 2):
                    bias(u - 1)
                for n in range(2, len(BIAS_ROWS)):
                    last = BLOCKS.index(BIAS_ROWS[n - 2])
                    if u == 2 * last + 7:
                        evacuated(sp, 2 * last)
                        evacuated(sp, 2 * last + 1)
                        bias(n)

            def load_body(turn, e0):
                for c in range(UNROLL * CH):
                    s, dst = slot_of(c)
                    sp.wait_ge(chunk_used, turn * (UNROLL * CH) + c - NSLOT + 1)
                    sp.dma_start(dst, wexp[e0 * CH + c]).then_inc(slot_in[s], 16)

            for c in range(UNROLL * CH):
                s, dst = slot_of(c)
                if c == 0:
                    sp.wait_ge(gla_o, GH)
                    sp.wait_ge(sw_out, NGRP)
                if RING0 + c >= NSLOT and c < NSLOT:
                    if s == HTL_SLOT:
                        multiplied(sp, GATES_DONE - 1)
                    elif s in W_SLOTS:
                        multiplied(sp, NU - len(W_SLOTS) + W_SLOTS.index(s))
                    else:
                        multiplied(sp, NU - len(H_SLOTS) + H_SLOTS.index(s))
                if c >= NSLOT:
                    sp.wait_ge(chunk_used, c - NSLOT + 1)
                sp.dma_start(dst, wexp[c]).then_inc(slot_in[s], 16)
            with sp.Fori(1, NE // UNROLL) as i:
                load_body(i, i * UNROLL)
            sp.wait_ge(np_ready, 1)
            passes = sp.value_load(NBI[0:1, 0:1], min_val=1, max_val=PASSES)
            with sp.If(passes > 1):
                with sp.Fori(1, passes) as b:
                    with sp.Fori(0, NE // UNROLL) as i:
                        load_body(b * (NE // UNROLL) + i, i * UNROLL)
            for i in range(TT):
                sp.wait_ge(out_ready, i + 1)
                sp.dma_start(out[i * P:(i + 1) * P, :], OUTB[:, i, :]).then_inc(out_done, 16)
            sp.wait_ge(out_done, 16 * TT)

        @block.gpsimd
        def _(pool):
            pool.dma_start(BE1R, be1).then_inc(be1_in, 16)
            nc.gpsimd.memset(PTG[:], 0.0).then_inc(gla_zero, 1)
            pool.dma_start(ROW[:], rows.partition_broadcast(P)).then_inc(row_in, 16)
            pool.dma_start(WG[0:RANK, :], wgate).then_inc(wg_in, 16)
            pool.dma_start(WR[:], wrout).then_inc(wr_in, 16)
            for u in range(1, NU, 2):
                pool.wait_ge(hi_ready, u + 1)
                nc.gpsimd.tensor_tensor(w_unit(u, True), w_unit(u), h_unit(u, True).bitcast(F32), ALU.subtract).then_inc(lo_p, 1)
            pool.wait_ge(mix_lo, 4)
            pool.dma_start(SIG[:], gfin.partition_broadcast(P)).then_inc(gfin_in, 16)
            for n in range(2):
                pool.dma_start(BE2[n], be2[:, n * 512:(n + 1) * 512]).then_inc(be2_in, 16)

        @block.tensor
        def _(pe):
            mm = nc.tensor.matmul

            pe.wait_ge(ident_in, 16)
            pe.wait_ge(x_in, 16 * TT)
            for a in range(4):
                for q in range(4):
                    k, i = 2 * a + q // 2, q % 2
                    last = nc.tensor.transpose(PS[:, 4 + a, q * P:(q + 1) * P], X[:, i, k * P:(k + 1) * P], ident)
                last.then_inc(xt_full, 1)
            pe.wait_ge(tab_in, 16)
            pe.wait_ge(diag_ready, TT)
            for i in range(TT):
                last = mm(PS[:, 3, i * P:(i + 1) * P], TAB[:, T_ONE:T_ONE + P], DIAG[:, i * P:(i + 1) * P],
                          start=True, stop=True)
            last.then_inc(rsr_full, 1)

            usage = [0]

            def pj_bank():
                b, n = usage[0] % NPJ, usage[0] // NPJ
                usage[0] += 1
                if n:
                    pe.wait_ge(pj_free[b], n)
                return b

            def dense(i, hooks={}):
                name = BLOCKS[i]
                token = name in TOKEN_MAJOR
                src = {"gl": OA2, "sw": OB2, "wo": MIX2}.get(name[:2], HT2)
                w = KVW if name == "skv" else BW
                width = SKVW if name == "skv" else BW
                banks = []
                for kh in range(2):
                    u = 2 * i + kh
                    pe.wait_ge((lo_v, lo_p)[kh], i + 1)
                    ws = (h_unit(u, True), w_unit(u, True))
                    if name[:2] == "wo":
                        pe.wait_ge(mix_lo, 2 * (kh + 1))
                    if i == 0:
                        pe.wait_ge(ht_ready, 2 * (kh + 1))

                    def chain(dst, left, right):
                        for k in range(KH):
                            for a, b in ((0, 0), (1, 0), (0, 1)):
                                last = mm(dst, left(k, a), right(k, b), start=(kh == 0 and k == 0 and a + b == 0 and first),
                                          stop=(kh == 1 and k == KH - 1 and b == 1), skip_group_check=True)
                        return last

                    for half in range(2):
                        if kh == 0:
                            banks.append(pj_bank())
                        b = banks[half]
                        first = True
                        if token:
                            last = chain(bk(b, w), lambda k, p: src[p][:, KH * kh + k, half * P:(half + 1) * P],
                                         lambda k, p: ws[p][:, k * width:k * width + w])
                        else:
                            for f in range(2):
                                first = f == 0
                                c = (2 * half + f) * P
                                last = chain(PS[:, b, f * SEQ:(f + 1) * SEQ], lambda k, p: ws[p][:, k * width + c:k * width + c + P],
                                             lambda k, p: src[p][:, KH * kh + k, :])
                        if kh == 1:
                            last.then_inc(pj_full[b], 1)
                        elif half == 1 and name != "skv":
                            last.then_inc(first_used, 1)
                        if half == 1 and name == "skv":
                            first = True
                            last = chain(PS[:, 3, 0:SEQ], lambda k, p: ws[p][:, k * width + KVW:(k + 1) * width],
                                         lambda k, p: src[p][:, KH * kh + k, :])
                            last.then_inc(lr_full if kh else first_used, 1)
                        for step in hooks.get((kh, half), ()):
                            step()

            def transpose16(get_src, full):
                for a in range(4):
                    for q in range(4):
                        k, i = 2 * a + q // 2, q % 2
                        last = nc.tensor.transpose(PS[:, 4 + a, q * P:(q + 1) * P], get_src(i, k), ident)
                    last.then_inc(full, 1)

            dense(0)
            dense(1)
            dense(2)
            dense(3)
            pe.wait_ge(lr_ready, 1)
            pe.wait_ge(wg_in, 16)
            for h in range(GH):
                last = mm(PS[:, 6 + h // 2, (h % 2) * SEQ:(h % 2 + 1) * SEQ], WG[0:RANK, h * GDK:(h + 1) * GDK],
                          LRT[0:RANK, :], start=True, stop=True)
            last.then_inc(z_full, 1)
            dense(4)
            pe.wait_ge(krot_ready, TT)
            for g in range(2):
                for i in range(TT):
                    last = nc.tensor.transpose(PS[:, 3, (2 * g + i) * P:(2 * g + i + 1) * P],
                                               KD[:, i, g * P:(g + 1) * P], ident)
            last.then_inc(kt_full, 1)
            pe.wait_ge(qrot_ready, TT)
            pe.wait_ge(z_ready, GH)
            transpose16(lambda i, k: SQR[:, i, k * P:(k + 1) * P], qt_full)

            def scores(n):
                i, g4 = n // (NGRP // TT), n % (NGRP // TT)
                if n == 0:
                    pe.wait_ge(qt_ready, 2)
                    pe.wait_ge(qt_cp, 2)
                    pe.wait_ge(kt_ready, 1)
                else:
                    pe.wait_ge(sw_masked, 2 * n)
                ns = (i + 1) * P
                for hh in range(HG):
                    h = HG * g4 + hh
                    p0 = (h % 2) * HD
                    last = mm(PS[:, 4 + hh % 2, (hh // 2) * SEQ:(hh // 2) * SEQ + ns],
                              qT[p0:p0 + HD, h // 2, i * P:(i + 1) * P],
                              KTT[p0:p0 + HD, h // (QH // 2), 0:ns], start=True, stop=True)
                last.then_inc(sw_s, 1)

            def probs_t(n):
                i = n // (NGRP // TT)
                pe.wait_ge(sw_exp, n + 1)
                if n:
                    pe.wait_ge(sw_ptA, n)
                    pe.wait_ge(sw_ptV, n)
                for hh in range(HG):
                    for st in range(i + 1):
                        last = nc.tensor.transpose(PS[:, 6 + hh // 2, (2 * (hh % 2) + st) * P:(2 * (hh % 2) + st + 1) * P],
                                                   SS[:, n % 2, hh, st * P:(st + 1) * P], ident)
                last.then_inc(sw_t, 1)

            def values(n):
                i, g4 = n // (NGRP // TT), n % (NGRP // TT)
                pe.wait_ge(sw_ptA, n + 1)
                pe.wait_ge(sw_ptV, n + 1)
                if n:
                    pe.wait_ge(sw_out, n)
                kv = g4 // 2
                for hh in range(HG):
                    for st in range(i + 1):
                        last = mm(PS[:, 3, hh * HD:(hh + 1) * HD], PTS[:, n % 2, hh, st * P:(st + 1) * P],
                                  KVRAW[:, st, P + kv * HD:P + (kv + 1) * HD], start=(st == 0), stop=(st == i))
                last.then_inc(sw_o, 1)

            def swa_slot(n):
                def run(n=n):
                    if 0 <= n - 2 < NGRP:
                        values(n - 2)
                    if 0 <= n - 1 < NGRP:
                        probs_t(n - 1)
                    if n < NGRP:
                        scores(n)
                return run

            def attention_slots(i):
                n = 2 * (i - 5)
                return {(0, 1): [swa_slot(n)], (1, 1): [swa_slot(n + 1)]}

            for i in range(5, 10):
                dense(i, attention_slots(i))

            def attention_t():
                pe.wait_ge(sw_out, NGRP)
                transpose16(lambda i, k: SQR[:, i, k * P:(k + 1) * P], obt_full)

            def gla_scores():
                pe.wait_ge(obt_hi, 4)
                pe.wait_ge(obt_lo, 4)
                pe.wait_ge(gla_ops, 5)
                for h in range(GH):
                    w0, w1, w2 = (w[:, h * SEQ:(h + 1) * SEQ] for w in (W0, W1, W2))
                    gq, gk = GQT[:, h * SEQ:(h + 1) * SEQ], GKT[:, h * SEQ:(h + 1) * SEQ]
                    mm(PS[:, 4 + h, 0:P], w0[:, 0:P], w0[:, P:SEQ], start=True, stop=True)
                    for i in range(TT):
                        c = P + i * P
                        t0 = i * P
                        mm(PS[0:64, 4 + h, c:c + 64], w1[:, t0:t0 + 64], w1[:, t0 + 64:t0 + 128], start=True, stop=True)
                        for q in range(2):
                            s0 = t0 + 64 * q
                            mm(PS[64 * q:64 * q + 32, 4 + h, c + 64:c + 96], w2[:, s0:s0 + 32], w2[:, s0 + 32:s0 + 64],
                               start=True, stop=True)
                        for q in range(4):
                            s0 = t0 + 32 * q
                            last = mm(PS[32 * q:32 * q + 32, 4 + h, c + 96:c + 128], gk[:, s0:s0 + 32], gq[:, s0:s0 + 32],
                                      start=True, stop=True)
                last.then_inc(gla_sc, 1)

            def gla_output():
                pe.wait_ge(gla_pt, 1)
                for u in range(10, 14):
                    evacuated(pe, u)
                for h in range(GH):
                    v = slice(h * GDV, (h + 1) * GDV)
                    mm(PS[:, 4 + h, 0:GDV], PTG[:, h, 1, :], GV[:, 0, v], start=True, stop=True)
                    mm(PS[:, 4 + h, GDV:2 * GDV], PTG[:, h, 0, :], GV[:, 0, v], start=True, stop=False)
                    last = mm(PS[:, 4 + h, GDV:2 * GDV], PTG[:, h, 2, :], GV[:, 1, v], start=False, stop=True)
                    last.then_inc(gla_o, 1)

            def gla_t():
                pe.wait_ge(gla_oa, GH * TT)
                transpose16(lambda i, k: GR[:, i, k * P:(k + 1) * P], oat_full)

            dense(10, {(0, 1): [attention_t]})
            gla_scores()
            dense(11, {(0, 1): [gla_output]})
            dense(12, {(1, 0): [gla_t]})
            pe.wait_ge(oat_hi, 4)
            pe.wait_ge(oat_lo, 4)
            for i in range(13, NB):
                dense(i)

            pe.wait_ge(xn_ready, TT)
            transpose16(lambda i, k: xn[:, i, k * P:(k + 1) * P], xnT_full)
            pe.wait_ge(xnT_ready, 4)
            pe.wait_ge(wr_in, 16)
            for i in range(TT):
                for k in range(KT):
                    last = mm(PS[:, 3, i * NE:(i + 1) * NE], xnT[:, k, i * P:(i + 1) * P], WR[:, k, :],
                              start=(k == 0), stop=(k == KT - 1))
            last.then_inc(lg_full, 1)
            tri, ones = TAB[:, T_TRI:T_TRI + P], TAB[:, T_ONE:T_ONE + P]
            pe.wait_ge(mask_ready, TT)
            mm(PS[:, 4, 0:NE], tri, MK[:, 0, :], start=True, stop=True)
            mm(PS[:, 4, NE:2 * NE], tri, MK[:, 1, :], start=True, stop=False)
            mm(PS[:, 4, NE:2 * NE], ones, MK[:, 0, :], start=False, stop=True)
            mm(PS[:, 4, 2 * NE:3 * NE], ones, MK[:, 0, :], start=True, stop=False)
            mm(PS[:, 4, 2 * NE:3 * NE], ones, MK[:, 1, :], start=False, stop=True).then_inc(rank_full, 1)
            pe.wait_ge(gat_ready, TT)
            for i in range(TT):
                last = nc.tensor.transpose(PS[0:NE, 5, i * P:(i + 1) * P], GT_[:, i, :], ident)
            last.then_inc(gatT_full, 1)
            pe.wait_ge(gatT_ready, 1)
            pe.wait_ge(be2_in, 32)
            for i in range(TT):
                for n in range(2):
                    mm(bk(2 * i + n), GATT[:, i * P:(i + 1) * P], BE2[n],
                       start=True, stop=True, skip_group_check=True)

            def gather():
                for k in range(KT):
                    for n in range(3 * TT):
                        last = mm(PS[:, 7, k * SLOTS:(k + 1) * SLOTS], XP[n // TT][:, n % TT, k * P:(k + 1) * P],
                                  SEL[:, n % TT, :], start=(n == 0), stop=(n == 3 * TT - 1))
                last.then_inc(xg_full, 1)

            def scatter():
                for i in range(TT):
                    for n in range(2):
                        last = mm(bk(2 * i + n), SELT[:, n, i * P:(i + 1) * P], Y,
                                  start=False, stop=True, skip_group_check=True)
                return last

            def both_halves(b, lhsT, rhs, start, stop):
                for g in range(2):
                    last = mm(PS[g * SLOTS:(g + 1) * SLOTS, b, :], lhsT, rhs[:, g * 512:(g + 1) * 512],
                              start=start, stop=stop)
                return last

            for n in range(TT):
                pe.wait_ge(xp3, n + 1)
            pe.wait_ge(sel_ready, 1)
            gather()
            pe.wait_ge(be1_ready, 1)
            pe.wait_ge(np_ready, 1)
            passes = pe.value_load(NBI[0:1, 0:1], min_val=1, max_val=PASSES)
            with pe.Fori(0, passes) as b:
                with pe.Fori(0, NE // UNROLL) as it:
                    turn = b * (NE // UNROLL) + it
                    for j in range(UNROLL):
                        e = turn * UNROLL + j

                        def chunk(c):
                            s, data = slot_of(j * CH + c)
                            pe.wait_ge(slot_in[s], turn * 48 + 16 * ((j * CH + c) // NSLOT + 1))
                            return data

                        pe.wait_ge(sele_ready, e + 1)
                        pe.wait_ge(selT_a, e + 1)
                        pe.wait_ge(selT_b, e + 1)
                        for n in range(2):
                            both_halves(4 + n, SELE, BE1[:, n * D:(n + 1) * D], True, False)
                        pe.wait_ge(xt_ready, e + 1)
                        for c in range(CH1):
                            w = chunk(c)
                            for n in range(2):
                                last = both_halves(4 + n, XT[:, c, :], w[:, n * D:(n + 1) * D], False, c == CH1 - 1)
                            last.then_inc(chunk_used, 1)
                        pe.wait_ge(sel_ready, e + 2)
                        gather()
                        pe.wait_ge(y_ready, e + 1)
                        scatter()
                        pe.wait_ge(selg_ready, e + 1)
                        pe.wait_ge(u_read, e + 1)
                        for i in range(TT):
                            last = nc.tensor.transpose(PS[:, 5, i * P:(i + 1) * P], SELG[:, i], ident)
                        last.then_inc(selT_full, 1)
                        pe.wait_ge(act_ready, e + 2)
                        for q in range(4):
                            last = nc.tensor.transpose(PS[:, 4, q * P:(q + 1) * P], LIN[:, q * P:(q + 1) * P], ident)
                        last.then_inc(at_full, 1)
                        pe.wait_ge(at_ready, e + 1)
                        for c in range(CH2):
                            w = chunk(CH1 + c)
                            for kk in range(2):
                                f = 2 * c + kk
                                o = (2 * (f % 4) + f // 4) * SLOTS
                                last = both_halves(6, AT[:, o:o + SLOTS], w[:, kk * D:(kk + 1) * D],
                                                   f == 0, f == FT - 1)
                            last.then_inc(chunk_used, 1)
            total = passes * NE
            pe.wait_ge(y_ready, total + 1)
            pe.wait_ge(selT_a, total + 1)
            pe.wait_ge(selT_b, total + 1)
            scatter().then_inc(moe_done, 1)

        @block.scalar
        def _(act):
            fn = nc.scalar.activation
            steps = [0]

            def link(ins):
                steps[0] += 1
                ins.then_inc(act_step, 1)
                act.wait_ge(act_step, steps[0])

            def split(u):
                landed(act, u)
                if u >= len(H_SLOTS):
                    multiplied(act, u - len(H_SLOTS))
                fn(h_unit(u, True), w_unit(u), ACT.Copy).then_inc(hi_ready, 1)

            act.dma_start(TAB[:, T_ID:T_ID + P], tab[:, T_ID:T_ID + P]).then_inc(ident_in, 16)
            act.dma_start(TAB[:, P:NTAB], tab[:, P:NTAB]).then_inc(tab_in, 16)
            act.dma_start(CV[:], cv).then_inc(cv_in, 16)
            for i in range(TT):
                act.wait_ge(x_in, 16 * TT)
                fn(SQ[:, i, :], X[:, i, :], ACT.Square, accum_out=S_SS[:, i:i + 1]).then_inc(ssq0, 1)
            act.wait_ge(var0, 1)
            fn(S_SD, S_VAR, ACT.Sqrt).then_inc(sd0, 1)
            split(0)
            for a in range(4):
                act.wait_ge(ht_raw, 2 * (a + 1))
                fn(HT_R[:, 2 * a:2 * a + 2, :], HTL[:, 2 * a:2 * a + 2, :], ACT.Copy).then_inc(ht_hi, 1)
                if a == 1:
                    split(1)
            for u in range(2, 10):
                split(u)
            act.wait_ge(lr_full, 1)
            act.wait_ge(cv_in, 16)
            fn(LRT[0:RANK, :], PS[0:RANK, 3, 0:SEQ], ACT.Identity, bias=col(C_BLR, p=RANK)).then_inc(lr_ready, 1)

            def feature_major(i, dst, c, func):
                for half in range(2):
                    u = 2 * i + half
                    act.wait_ge(pj_full[u % NPJ], u // NPJ + 1)
                    for f in range(2):
                        n = 2 * half + f
                        last = fn(dst[half][:, f * SEQ:(f + 1) * SEQ], PS[:, u % NPJ, f * SEQ:(f + 1) * SEQ], func,
                                  bias=col(c + n))
                    last.then_inc(pj_free[u % NPJ], 1)

            split(10)
            feature_major(3, [GQT[:, c * BW:(c + 1) * BW] for c in range(2)], C_BQ, ACT.Identity)
            act.wait_ge(z_full, 1)
            for h in range(GH):
                fn(TMP[:, h * SEQ:(h + 1) * SEQ], PS[:, 6 + h // 2, (h % 2) * SEQ:(h % 2 + 1) * SEQ], ACT.Identity,
                   bias=col(C_BGATE + h)).then_inc(z_ready, 1)
            split(11)
            split(12)
            feature_major(4, [GKT[:, c * BW:(c + 1) * BW] for c in range(2)], C_BK, ACT.Identity)
            act.wait_ge(gate_neg, 1)
            link(fn(W1, W0, ACT.Exp))
            fn(W1, W1, ACT.Ln, bias=1.0).then_inc(gate_sp, 1)
            for a in range(2):
                act.wait_ge(qt_full, a + 1)
                fn(qT[:, 2 * a:2 * a + 2, :], PS[:, 4 + a, :].rearrange("p (k t) -> p k t", k=2), ACT.Copy).then_inc(qt_cp, 1)

            split(13)

            def swa_exp(n):
                ns = (n // (NGRP // TT) + 1) * P
                q = n % 2
                act.wait_ge(sw_max, n + 1)
                for hh in range(HG):
                    fn(SS[:, q, hh, 0:ns], SS[:, q, hh, 0:ns], ACT.Exp, bias=S_NM[q][:, hh:hh + 1],
                       accum_out=S_SUM[q][:, hh:hh + 1])
                fn(S_ES[q], S_DS[q], ACT.Exp).then_inc(sw_exp, 1)

            def swa_pt(n):
                i = n // (NGRP // TT)
                act.wait_ge(sw_t, n + 1)
                fn(PTS[:, n % 2, 0:2, 0:(i + 1) * P],
                   PS[:, 6, :].rearrange("p (h s) -> p h s", h=2)[:, :, 0:(i + 1) * P], ACT.Copy).then_inc(sw_ptA, 1)

            def gr_sigmoid(u):
                n, m = (u - 14) // 2, u % 2
                evacuated(act, u)
                if u >= 16:
                    act.wait_ge(gr_ready, u - 15)
                fn(SIG[:, m * BW:(m + 1) * BW], GR[:, m, n * BW:(n + 1) * BW], ACT.Sigmoid).then_inc(gr_sig, 1)

            def decays():
                v0 = W0.rearrange("p (h t) -> p h t", h=GH)
                b0 = B.rearrange("p (h t) -> p h t", h=GH)
                act.wait_ge(decay_in, 1)
                fn(v0[:, :, 0:P], v0[:, :, 0:P], ACT.Exp, scale=1.0 / TAU)
                fn(v0[:, :, P:SEQ], b0[:, :, P:SEQ], ACT.Exp, scale=1.0 / TAU).then_inc(decay_out, 1)
                for n, w in ((2, W1), (3, W2)):
                    act.wait_ge(decay_in, n)
                    fn(w, w, ACT.Exp, scale=1.0 / TAU).then_inc(decay_out, 1)
                act.wait_ge(decay_in, 4)
                act.wait_ge(decay_out, 1)
                fn(B, TMP, ACT.Exp, scale=1.0 / TAU).then_inc(decay_out, 1)
                act.wait_ge(decay_out, 4)
                fn(TMP, TMP, ACT.Exp, scale=-1.0 / TAU).then_inc(decay_out, 1)

            for n in range(NGRP + 1):
                if 0 <= n - 1:
                    swa_pt(n - 1)
                if n < NGRP:
                    swa_exp(n)
                split(n + 14)
                if n == 2:
                    decays()
                if n >= 5:
                    gr_sigmoid(n + 9)

            def high_t(dst, full, done):
                for a in range(4):
                    act.wait_ge(full, a + 1)
                    fn(dst[:, 2 * a:2 * a + 2, :], PS[:, 4 + a, :].rearrange("p (k t) -> p k t", k=2), ACT.Copy).then_inc(done, 1)

            act.wait_ge(gr_ready, 4)
            feature_major(9, MIX[0:2], C_BGA, ACT.Sigmoid)
            split(23)
            high_t(OB2[0], obt_full, obt_hi)
            split(24)
            feature_major(10, MIX[2:4], C_BGA + 4, ACT.Sigmoid)
            split(25)
            for h in range(GH):
                act.wait_ge(gla_o, h + 1)
                act.wait_ge(gla_sq, TT * h)
                for i in range(TT):
                    fn(PS[:, 3, i * GDV:(i + 1) * GDV], PS[:, 4 + h, i * GDV:(i + 1) * GDV], ACT.Square,
                       accum_out=S_GS[:, TT * h + i:TT * h + i + 1]).then_inc(gla_sq, 1)
            act.wait_ge(gla_var, 1)
            fn(S_GSD, S_GVAR, ACT.Sqrt).then_inc(gla_sd, 1)
            split(26)
            feature_major(11, GB[0:2], C_BGB, ACT.Sigmoid)
            split(27)
            split(28)
            high_t(OA2[0], oat_full, oat_hi)
            feature_major(12, GB[2:4], C_BGB + 4, ACT.Sigmoid)
            for u in range(29, NU - 3):
                split(u)
            for c in range(2):
                act.wait_ge(mix_ready, c + 1)
                fn(MIX2[0][:, 2 * c:2 * c + 2, :].rearrange("p k t -> p (k t)"), MIX[c], ACT.Copy).then_inc(mix_hi, 1)
            split(NU - 3)
            split(NU - 2)
            for c in range(2, 4):
                act.wait_ge(mix_ready, c + 1)
                fn(MIX2[0][:, 2 * c:2 * c + 2, :].rearrange("p k t -> p (k t)"), MIX[c], ACT.Copy).then_inc(mix_hi, 1)
            split(NU - 1)
            for u in range(2 * NB - 4, 2 * NB):
                evacuated(act, u)
            for i in range(TT):
                fn(HTf[:, i * D:(i + 1) * D], X[:, i, :], ACT.Square, accum_out=S_SS[:, i:i + 1]).then_inc(ssq1, 1)
            act.wait_ge(var1, 1)
            fn(S_SD, S_VAR, ACT.Sqrt).then_inc(sd1, 1)
            for i in range(TT):
                act.wait_ge(xn_ready, i + 1)
                fn(XP[0][:, i, :], xn[:, i, :], ACT.Copy).then_inc(xp1, 1)
            for i in range(TT):
                act.wait_ge(rest1, i + 1)
                fn(XP[1][:, i, :], REST[:, i, :], ACT.Copy).then_inc(xp2, 1)
            for i in range(TT):
                act.wait_ge(top_ready, i + 1)
                fn(S_EG[i], S_V8[i][:, 0:TOPK], ACT.Exp, bias=S_NV[i], accum_out=S_ES4[i]).then_inc(eg_ready, 1)
            act.wait_ge(np_ready, 1)
            passes = act.value_load(NBI[0:1, 0:1], min_val=1, max_val=PASSES)
            with act.Fori(0, passes) as b:
                with act.Fori(0, NE) as e:
                    done = b * NE + e
                    act.wait_ge(glu_ready, done + 1)
                    fn(SGM, GLU, ACT.Sigmoid, scale=ALPHA).then_inc(sgm_ready, 1)
                    act.wait_ge(selT_full, done + 1)
                    fn(SELT[0:SLOTS, 0, 0:SEQ], PS[0:SLOTS, 5, 0:SEQ], ACT.Copy).then_inc(selT_a, 1)
                    act.wait_ge(at_full, done + 1)
                    fn(AT, bk(4), ACT.Copy).then_inc(at_ready, 1)
                    act.wait_ge(chunk_used, done * CH + CH)
                    fn(Y, bk(6), ACT.Copy).then_inc(y_ready, 1)
            for i in range(TT):
                act.wait_ge(xf_ready, 2 * (i + 1))
                fn(OUTB[:, i, :], X[:, i, :], ACT.Square, accum_out=S_SS[:, i:i + 1]).then_inc(ssqf, 1)
            act.wait_ge(varf, 1)
            fn(S_SD, S_VAR, ACT.Sqrt).then_inc(sdf, 1)

        @block.vector
        def _(dve):
            v = nc.vector
            steps = [0]

            def link(ins):
                steps[0] += 1
                ins.then_inc(dve_step, 1)
                dve.wait_ge(dve_step, steps[0])

            def mean_eps(ssq, var, n, count_sem, count, done):
                dve.wait_ge(count_sem, count)
                v.tensor_scalar(var, ssq, 1.0 / n, EPS, ALU.mult, ALU.add).then_inc(done, 1)

            def rest(u):
                dve.wait_ge(hi_ready, u + 1)
                v.tensor_tensor(w_unit(u, True), w_unit(u), h_unit(u, True).bitcast(F32), ALU.subtract).then_inc(lo_v, 1)

            mean_eps(S_SS, S_VAR, D, ssq0, TT, var0)
            dve.wait_ge(sd0, 1)
            link(v.reciprocal(S_RS, S_SD))
            dve.wait_ge(ident_in, 16)
            for i in range(TT):
                v.tensor_scalar(DIAG[:, i * P:(i + 1) * P], ident, S_RS[:, i:i + 1], None, ALU.mult).then_inc(diag_ready, 1)
            dve.wait_ge(cv_in, 16)
            dve.wait_ge(rsr_full, 1)
            link(v.tensor_copy(RSR, PS[:, 3, 0:SEQ]))
            for a in range(4):
                dve.wait_ge(xt_full, a + 1)
                for k in range(2 * a, 2 * a + 2):
                    v.scalar_tensor_tensor(HTL[:, k, :], PS[:, 4 + a, (k % 2) * SEQ:(k % 2 + 1) * SEQ],
                                           col(C_GMIX + k), RSR, ALU.mult, ALU.mult).then_inc(ht_raw, 1)
                if a == 1 or a == 3:
                    for n in range(a - 1, a + 1):
                        dve.wait_ge(ht_hi, n + 1)
                        v.tensor_tensor(HT2[1][:, 2 * n:2 * n + 2, :], HTL[:, 2 * n:2 * n + 2, :],
                                        HT_R[:, 2 * n:2 * n + 2, :].bitcast(F32),
                                        ALU.subtract).then_inc(ht_ready, 1)
                if a == 1:
                    rest(0)
            rest(2)
            dve.wait_ge(be1_in, 16)
            for part in range(2):
                link(v.tensor_copy(BE1[0:NE], BE1R))
                link(v.tensor_copy(BE1[(2 - part) * NE:(3 - part) * NE], BE1[0:NE]))
                link(v.tensor_tensor(BE1R, BE1R, BE1[0:NE], ALU.subtract))
                if part == 0:
                    rest(4)
            v.tensor_copy(BE1[0:NE], BE1R).then_inc(be1_ready, 1)
            dve.wait_ge(be1_ready, 1)

            def token_major(u, dst, w, done=None):
                i = u // 2
                n = BIAS_ROWS.index(BLOCKS[i])
                dve.wait_ge(bias_in[n % 2], 16 * (n // 2 + 1))
                dve.wait_ge(pj_full[u % NPJ], u // NPJ + 1)
                v.tensor_tensor(dst, bk(u % NPJ, w), BRW[:, n % 2, 0:w], ALU.add).then_inc(pj_free[u % NPJ], 1)

            for u in range(6):
                i, m = u // 2, u % 2
                if i < 2:
                    token_major(u, SQ[:, m, i * BW:(i + 1) * BW], BW)
                else:
                    token_major(u, KVRAW[:, m, :], KVW)
                if m:
                    rest(u + 5)

            cos = TAB[:, T_COS:T_COS + TT * HALF].rearrange("p (i d) -> p i d", i=TT)
            sin = TAB[:, T_SIN:T_SIN + TT * HALF].rearrange("p (i d) -> p i d", i=TT)

            def rotate(src, dst, n, i, done):
                t1 = SIG[:, 0:n * HALF].rearrange("p (h d) -> p h d", h=n)
                t2 = SIG[:, BW:BW + n * HALF].rearrange("p (h d) -> p h d", h=n)
                c = cos[:, i, :].unsqueeze(1).broadcast_to([P, n, HALF])
                s = sin[:, i, :].unsqueeze(1).broadcast_to([P, n, HALF])
                v.tensor_tensor(t1, src[:, :, 0, :], c, ALU.mult)
                link(v.tensor_tensor(t2, src[:, :, 1, :], s, ALU.mult))
                for d in dst:
                    last = v.tensor_tensor(d[:, :, 0, :], t1, t2, ALU.subtract)
                link(last)
                v.tensor_tensor(t1, src[:, :, 1, :], c, ALU.mult)
                link(v.tensor_tensor(t2, src[:, :, 0, :], s, ALU.mult))
                for d in dst:
                    last = v.tensor_tensor(d[:, :, 1, :], t1, t2, ALU.add)
                last.then_inc(done, 1)
                dve.wait_ge(done, i + 1)

            dve.wait_ge(tab_in, 16)
            for i in range(TT):
                evacuated(dve, 4 + i)
                kd = KD[:, i, :].rearrange("p (h c x d) -> p h c x d", h=2, c=2, x=2)
                rotate(KVRAW[:, i, 0:P].rearrange("p (h x d) -> p h x d", h=2, x=2),
                       [kd[:, :, c] for c in range(2)], 2, i, krot_ready)
            for i in range(TT):
                evacuated(dve, i)
                evacuated(dve, 2 + i)
                rotate(SQ[:, i, :].rearrange("p (h x d) -> p h x d", h=QH, x=2),
                       [SQR[:, i, :].rearrange("p (h x d) -> p h x d", h=QH, x=2)], QH, i, qrot_ready)
            dve.wait_ge(z_ready, GH)
            v.scalar_tensor_tensor(W0, TMP, -1.0, TMP, ALU.mult, ALU.min).then_inc(gate_neg, 1)
            rest(12)
            dve.wait_ge(kt_full, 1)
            v.tensor_copy(KTT[:].rearrange("p g t -> p (g t)"), bk(3)).then_inc(kt_ready, 1)
            for a in range(2, 4):
                dve.wait_ge(qt_full, a + 1)
                v.tensor_copy(qT[:, 2 * a:2 * a + 2, :], PS[:, 4 + a, :].rearrange("p (k t) -> p k t", k=2)).then_inc(qt_ready, 1)

            def decay_exponents():
                dve.wait_ge(gate_sp, 1)
                link(v.scalar_tensor_tensor(W2, TMP, 0.0, W1, ALU.min, ALU.subtract))
                link(v.memset(W0, 1.0))
                link(v.memset(W0.rearrange("p (n t) -> p n t", t=P)[:, :, 0:1], 0.0))
                link(v.tensor_tensor_scan(B, W0, W2, 0.0, ALU.mult, ALU.add))
                bh = B.rearrange("p (h t) -> p h t", h=GH)
                v.tensor_tensor(W0.rearrange("p (h t) -> p h t", h=GH)[:, :, 0:P],
                                bh[:, :, P - 1:P].broadcast_to([P, GH, P]), bh[:, :, 0:P], ALU.subtract).then_inc(decay_in, 1)
                for w, half in ((W1, 64), (W2, 32)):
                    n = GH * SEQ // (2 * half)
                    wv = w.rearrange("p (n s t) -> p n s t", s=2, t=half)
                    bv = B.rearrange("p (n s t) -> p n s t", s=2, t=half)
                    ref = bv[:, :, 0, half - 1:half].broadcast_to([P, n, half])
                    v.tensor_tensor(wv[:, :, 0, :], ref, bv[:, :, 0, :], ALU.subtract)
                    v.tensor_tensor(wv[:, :, 1, :], bv[:, :, 1, :], ref, ALU.subtract).then_inc(decay_in, 1)
                tv = TMP.rearrange("p (n t) -> p n t", t=32)
                bv = B.rearrange("p (n t) -> p n t", t=32)
                link(v.tensor_tensor(tv, bv, bv[:, :, 15:16].broadcast_to([P, GH * SEQ // 32, 32]), ALU.subtract))
                v.tensor_scalar(TMP, TMP, -CLAMP * TAU, CLAMP * TAU, ALU.max, ALU.min).then_inc(decay_in, 1)

            def decay_products():
                for u in range(6, 10):
                    evacuated(dve, u)
                dve.wait_ge(decay_out, 1)
                a, q, k = (t.rearrange("p (h t) -> p h t", h=GH) for t in (W0, GQT, GKT))
                v.tensor_tensor(a[:, :, 0:P], a[:, :, 0:P], k[:, :, 0:P], ALU.mult)
                v.scalar_tensor_tensor(a[:, :, P:SEQ], a[:, :, P:SEQ], GSCALE, q[:, :, P:SEQ], ALU.mult, ALU.mult).then_inc(gla_ops, 1)
                for n, (w, half) in enumerate(((W1, 64), (W2, 32))):
                    dve.wait_ge(decay_out, n + 2)
                    a, q, k = (t.rearrange("p (n s t) -> p n s t", s=2, t=half) for t in (w, GQT, GKT))
                    v.tensor_tensor(a[:, :, 0, :], a[:, :, 0, :], k[:, :, 0, :], ALU.mult)
                    v.scalar_tensor_tensor(a[:, :, 1, :], a[:, :, 1, :], GSCALE, q[:, :, 1, :], ALU.mult, ALU.mult).then_inc(gla_ops, 1)
                dve.wait_ge(decay_out, 5)
                dve.wait_ge(gla_ops, 3)
                v.scalar_tensor_tensor(GQT, B, GSCALE, GQT, ALU.mult, ALU.mult).then_inc(gla_ops, 1)
                v.tensor_tensor(GKT, TMP, GKT, ALU.mult).then_inc(gla_ops, 1)

            mask = TAB[:, T_SWA:T_SWA + SEQ]

            def swa_mask(n):
                i, g4 = n // (NGRP // TT), n % (NGRP // TT)
                q, ns = n % 2, (i + 1) * P
                dve.wait_ge(sw_s, n + 1)
                m = (mask[:, P:SEQ] if i == 0 else mask).unsqueeze(1).broadcast_to([P, 2, ns])
                for a in range(2):
                    last = v.scalar_tensor_tensor(SS[:, q, 2 * a:2 * a + 2, 0:ns],
                                                  PS[:, 4 + a, :].rearrange("p (h s) -> p h s", h=2)[:, :, 0:ns],
                                                  QSCALE, m, ALU.mult, ALU.add)
                    last.then_inc(sw_masked, 1)
                dve.wait_ge(sw_masked, 2 * (n + 1))
                link(v.tensor_reduce(S_MX[q], SS[:, q, :, 0:ns], AX_X, ALU.max))
                sink = ROW[:, R_SINK + HG * g4:R_SINK + HG * (g4 + 1)]
                link(v.tensor_tensor(S_MX[q], S_MX[q], sink, ALU.max))
                v.tensor_scalar(S_NM[q], S_MX[q], -1.0, None, ALU.mult)
                v.tensor_tensor(S_DS[q], sink, S_MX[q], ALU.subtract).then_inc(sw_max, 1)

            def swa_pt(n):
                i = n // (NGRP // TT)
                dve.wait_ge(sw_t, n + 1)
                v.tensor_copy(PTS[:, n % 2, 2:4, 0:(i + 1) * P],
                              PS[:, 7, :].rearrange("p (h s) -> p h s", h=2)[:, :, 0:(i + 1) * P]).then_inc(sw_ptV, 1)

            def swa_out(n):
                i, g4 = n // (NGRP // TT), n % (NGRP // TT)
                q = n % 2
                dve.wait_ge(sw_exp, n + 1)
                if n >= 2:
                    dve.wait_ge(sw_out, n - 1)
                link(v.tensor_tensor(S_DEN[q], S_SUM[q], S_ES[q], ALU.add))
                link(v.reciprocal(S_RD[q], S_DEN[q]))
                dve.wait_ge(sw_o, n + 1)
                v.tensor_tensor(SQR[:, i, g4 * HG * HD:(g4 + 1) * HG * HD].rearrange("p (a b d) -> p b a d", a=2, b=2),
                                PS[:, 3, 0:HG * HD].rearrange("p (b a d) -> p b a d", a=2, b=2),
                                S_RD[q].rearrange("p (b a) -> p b a", a=2).unsqueeze(3).broadcast_to([P, 2, 2, HD]),
                                ALU.mult).then_inc(sw_out, 1)

            def gr_finish(u):
                n, m = (u - 14) // 2, u % 2
                part = GR[:, m, n * BW:(n + 1) * BW]
                dve.wait_ge(gr_sig, u - 13)
                link(v.tensor_tensor(part, part, SIG[:, m * BW:(m + 1) * BW], ALU.mult))
                pv = part.rearrange("p (h d) -> p h d", h=2)
                v.tensor_tensor(pv, pv, ROW[:, R_HEAD:R_HEAD + GDV].unsqueeze(1).broadcast_to([P, 2, GDV]),
                                ALU.mult).then_inc(gr_ready, 1)

            dve.wait_ge(row_in, 16)
            for n in range(NGRP + 2):
                u = 10 + n
                if u % 2 and u < 18:
                    dst, c = (GV, (u - 10) // 2 * BW) if u < 14 else (GR, (u - 14) // 2 * BW)
                    for m in range(TT):
                        token_major(u - 1 + m, dst[:, m, c:c + BW], BW)
                if n - 2 >= 0:
                    swa_out(n - 2)
                if 0 <= n - 1 < NGRP:
                    swa_pt(n - 1)
                if n < NGRP:
                    swa_mask(n)
                if n % 2 == 0 and n <= NGRP:
                    rest(n + 14)
                if n == 1:
                    decay_exponents()
                if n == 4:
                    decay_products()
                if n >= 6:
                    gr_finish(n + 8)

            def rest_t(pair, full, done):
                dve.wait_ge(full, 4)
                for a in range(4):
                    hi = pair[0][:, 2 * a:2 * a + 2, :].bitcast(F32)
                    if done is obt_lo:
                        dve.wait_ge(obt_hi, a + 1)
                    else:
                        dve.wait_ge(oat_hi, a + 1)
                    v.tensor_tensor(pair[1][:, 2 * a:2 * a + 2, :], PS[:, 4 + a, :].rearrange("p (k t) -> p k t", k=2), hi,
                                    ALU.subtract).then_inc(done, 1)

            rest_t(OB2, obt_full, obt_lo)
            rest(24)

            dve.wait_ge(gla_zero, 1)
            dve.wait_ge(gla_sc, 1)
            sc = PS[:, 4:8, :]
            v.tensor_copy(PTG[:, :, 0, :], sc[:, :, 0:P])
            tiles = sc[:, :, P:P + SEQ].rearrange("p h (i c) -> p h i c", i=TT)
            v.tensor_copy(PTG[0:64, :, 1:3, 64:128], tiles[0:64, :, :, 0:64])
            for q in range(2):
                s = slice(64 * q, 64 * q + 32)
                v.tensor_copy(PTG[s, :, 1:3, 64 * q + 32:64 * q + 64], tiles[s, :, :, 64:96])
            for q in range(4):
                s = slice(32 * q, 32 * q + 32)
                last = v.tensor_tensor(PTG[s, :, 1:3, 32 * q:32 * q + 32], tiles[s, :, :, 96:128],
                                       TAB[s, T_DIAG:T_DIAG + 32].unsqueeze(1).unsqueeze(1).broadcast_to([32, GH, TT, 32]), ALU.mult)
            last.then_inc(gla_pt, 1)
            mean_eps(S_GS, S_GVAR, GDV, gla_sq, GH * TT, gla_var)
            dve.wait_ge(gla_sd, 1)
            link(v.reciprocal(S_GRS, S_GSD))
            dve.wait_ge(gr_ready, 4)
            for h in range(GH):
                for i in range(TT):
                    g = GR[:, i, h * GDV:(h + 1) * GDV]
                    n = TT * h + i
                    v.scalar_tensor_tensor(g, PS[:, 4 + h, i * GDV:(i + 1) * GDV], S_GRS[:, n:n + 1], g,
                                           ALU.mult, ALU.mult).then_inc(gla_oa, 1)
            rest(26)
            rest(28)
            rest_t(OA2, oat_full, oat_lo)
            rest(30)

            for i in (13, 14):
                for half in range(2):
                    u, c = 2 * i + half, 2 * (i - 13) + half
                    evacuated(dve, 2 * (9 + c // 2) + half)
                    dve.wait_ge(pj_full[u % NPJ], u // NPJ + 1)
                    v.tensor_tensor(MIX[c], bk(u % NPJ), MIX[c], ALU.mult).then_inc(pj_free[u % NPJ], 1)
                rest(2 * i + 6)

            def mix_rest(c):
                dve.wait_ge(mix_hi, c + 1)
                v.tensor_tensor(MIX2[1][:, 2 * c:2 * c + 2, :].rearrange("p k t -> p (k t)"), MIX[c],
                                MIX2[0][:, 2 * c:2 * c + 2, :].bitcast(F32).rearrange("p k t -> p (k t)"),
                                ALU.subtract).then_inc(mix_lo, 1)

            for i in (15, 16):
                for half in range(2):
                    u, c = 2 * i + half, 2 * (i - 15) + half
                    evacuated(dve, 2 * (11 + c // 2) + half)
                    dve.wait_ge(pj_full[u % NPJ], u // NPJ + 1)
                    v.tensor_tensor(GB[c], bk(u % NPJ), GB[c], ALU.mult).then_inc(pj_free[u % NPJ], 1)
                    evacuated(dve, u)
                    v.tensor_tensor(MIX[c], MIX[c], GB[c], ALU.add).then_inc(mix_ready, 1)
                for half in range(2):
                    mix_rest(2 * (i - 15) + half)
                if i == 15:
                    rest(36)
            for i in (17, 18):
                for m in range(TT):
                    u = 2 * i + m
                    xs = X[:, m, (i - 17) * BW:(i - 16) * BW]
                    dve.wait_ge(pj_full[u % NPJ], u // NPJ + 1)
                    v.tensor_tensor(xs, bk(u % NPJ), xs, ALU.add).then_inc(pj_free[u % NPJ], 1)

            mean_eps(S_SS, S_VAR, D, ssq1, TT, var1)
            dve.wait_ge(sd1, 1)
            link(v.reciprocal(S_RS, S_SD))
            for i in range(TT):
                v.tensor_scalar(xn[:, i, :], X[:, i, :], S_RS[:, i:i + 1], None, ALU.mult).then_inc(xn_ready, 1)
            for i in range(TT):
                dve.wait_ge(xp1, i + 1)
                v.tensor_tensor(REST[:, i, :], xn[:, i, :], XP[0][:, i, :], ALU.subtract).then_inc(rest1, 1)
            gffn = col(C_GFFN, KT)
            for a in range(4):
                dve.wait_ge(xnT_full, a + 1)
                v.tensor_tensor(xnT[:, 2 * a:2 * a + 2, :], PS[:, 4 + a, :].rearrange("p (k t) -> p k t", k=2),
                                gffn[:, 2 * a:2 * a + 2].unsqueeze(2).broadcast_to([P, 2, SEQ]), ALU.mult).then_inc(xnT_ready, 1)
            for i in range(TT):
                dve.wait_ge(xp2, i + 1)
                v.tensor_tensor(XP[2][:, i, :], REST[:, i, :], XP[1][:, i, :], ALU.subtract).then_inc(xp3, 1)
            dve.wait_ge(lg_full, 1)
            link(v.tensor_tensor(LG, PS[:, 3, 0:TT * NE].rearrange("p (i e) -> p i e", i=TT),
                                 ROW[:, R_ROUTER:R_ROUTER + NE].unsqueeze(1).broadcast_to([P, TT, NE]), ALU.add))
            for i in range(TT):
                link(v.max(S_V8[i], LG[:, i, :]))
                v.tensor_scalar(S_NV[i], S_V8[i][:, 0:1], -1.0, None, ALU.mult).then_inc(top_ready, 1)
                link(v.max_index(IDX[i][:], S_V8[i], LG[:, i, :]))
                link(v.tensor_copy(S_IF[i], IDX[i][:]))
            experts = TAB[:, T_IOTA:T_IOTA + NE]
            for i in range(TT):
                for k in range(TOPK):
                    last = v.tensor_scalar(OH[:, i, k, :], experts, S_IF[i][:, k:k + 1], None, ALU.is_equal)
                link(last)
                v.tensor_reduce(MK[:, i, :], OH[:, i].rearrange("p k e -> p e k"), AX_X, ALU.add).then_inc(mask_ready, 1)
            for i in range(TT):
                dve.wait_ge(eg_ready, i + 1)
                link(v.reciprocal(S_RG[i], S_ES4[i]))
                link(v.tensor_scalar(S_GT[i], S_EG[i], S_RG[i], None, ALU.mult))
                for k in range(TOPK):
                    last = v.tensor_scalar(OG[:, i, k, :], OH[:, i, k, :], S_GT[i][:, k:k + 1], None, ALU.mult)
                link(last)
                v.tensor_reduce(GT_[:, i, :], OG[:, i].rearrange("p k e -> p e k"), AX_X, ALU.add).then_inc(gat_ready, 1)
            dve.wait_ge(mask_ready, TT)
            dve.wait_ge(rank_full, 1)
            link(v.tensor_scalar(BIG, MK, -1e6, 1e6, ALU.mult, ALU.add))
            link(v.tensor_tensor(BIG, BIG, PS[:, 4, 0:TT * NE].rearrange("p (i e) -> p i e", i=TT), ALU.add))
            v.memset(RK[:, :, PASSES * NE:PASSES * NE + 1], 1e6)
            for b in range(PASSES):
                v.tensor_scalar(RK[:, :, b * NE:(b + 1) * NE], BIG, float(-b * SLOTS), None, ALU.add)
            link(v.tensor_reduce(S_CNT, PS[:, 4, 2 * NE:3 * NE], AX_X, ALU.max))
            link(v.tensor_scalar(S_CMP, TAB[:, T_THR:T_THR + PASSES], S_CNT, None, ALU.is_lt))
            link(v.tensor_reduce(S_NP, S_CMP, AX_X, ALU.add))
            v.tensor_copy(NBI[:], S_NP).then_inc(np_ready, 1)
            dve.wait_ge(gatT_full, 1)
            v.tensor_copy(GATT, PS[0:NE, 5, 0:SEQ]).then_inc(gatT_ready, 1)
            v.memset(Y, 0.0).then_inc(y_ready, 1)
            v.memset(SELT[:, 0, :], 0.0).then_inc(selT_a, 1)
            dve.wait_ge(gatT_ready, 1)
            v.memset(SELT[:, 1, :], 0.0).then_inc(selT_b, 1)
            dve.wait_ge(xp3, TT)
            v.memset(LIN, 0.0).then_inc(act_ready, 1)

            iota = TAB[:, T_IOTA:T_IOTA + SLOTS].unsqueeze(1).broadcast_to([P, TT, SLOTS])
            iota2 = TAB[:, T_IOTA:T_IOTA + SLOTS].unsqueeze(1).unsqueeze(1).broadcast_to([P, TT, 2, SLOTS])

            def spread(a):
                return a.broadcast_to([P, a.shape[1], SLOTS])

            def spread2(a):
                return a.unsqueeze(3).broadcast_to([P, TT, 2, SLOTS])

            def hot(a):
                return TAB[0:3 * NE, a].broadcast_to([3 * NE, SLOTS])

            v.tensor_tensor(SEL, iota, spread(RK[:, :, 0:1]), ALU.is_equal).then_inc(sel_ready, 1)
            v.tensor_copy(SELE, hot(slice(T_HOT, T_HOT + 1))).then_inc(sele_ready, 1)
            x_bank = PS[:, 7, :].rearrange("p (k c) -> p k c", k=KT)
            dve.wait_ge(xg_full, 1)
            v.tensor_tensor(XT, x_bank, spread(gffn.unsqueeze(2)), ALU.mult).then_inc(xt_ready, 1)
            dve.wait_ge(np_ready, 1)
            passes = dve.value_load(NBI[0:1, 0:1], min_val=1, max_val=PASSES)
            with dve.Fori(0, passes) as b:
                with dve.Fori(0, NE) as e:
                    done = b * NE + e
                    dve.wait_ge(chunk_used, done * CH + 1)
                    v.tensor_tensor(SEL, iota, spread(RK[:, :, bass.ds(done + 1, 1)]), ALU.is_equal).then_inc(sel_ready, 1)
                    v.tensor_tensor(SELG, iota2, spread2(RK[:, :, bass.ds(done, 1)]), ALU.is_equal).then_inc(selg_raw, 1)
                    v.tensor_copy(SELE, hot(bass.ds(T_HOT + (e + 1) % NE, 1))).then_inc(sele_ready, 1)
                    dve.wait_ge(selg_raw, done + 1)
                    v.tensor_tensor(SELG, SELG, spread2(GT_[:, :, bass.ds(e, 1)]), ALU.mult).then_inc(selg_ready, 1)
                    dve.wait_ge(chunk_used, done * CH + CH1)
                    dve.wait_ge(act_ready, done + 1)
                    v.tensor_scalar(GLU, bk(4), LIMIT, None, ALU.min).then_inc(glu_ready, 1)
                    v.tensor_scalar(LIN, bk(5), -LIMIT, LIMIT, ALU.max, ALU.min).then_inc(u_read, 1)
                    dve.wait_ge(glu_ready, done + 1)
                    dve.wait_ge(u_read, done + 1)
                    v.scalar_tensor_tensor(LIN, LIN, 1.0, GLU, ALU.add, ALU.mult).then_inc(lin_ready, 1)
                    dve.wait_ge(lin_ready, done + 1)
                    dve.wait_ge(sgm_ready, done + 1)
                    v.tensor_tensor(LIN, LIN, SGM, ALU.mult).then_inc(act_ready, 1)
                    dve.wait_ge(xg_full, done + 2)
                    v.tensor_tensor(XT, x_bank, spread(gffn.unsqueeze(2)), ALU.mult).then_inc(xt_ready, 1)
                    dve.wait_ge(selT_full, done + 1)
                    v.tensor_copy(SELT[SLOTS:P, 1, 0:SEQ], PS[SLOTS:P, 5, 0:SEQ]).then_inc(selT_b, 1)
            dve.wait_ge(moe_done, 1)
            for i in range(TT):
                for n in range(2):
                    xs = X[:, i, n * 512:(n + 1) * 512]
                    v.tensor_tensor(xs, bk(2 * i + n), xs, ALU.add).then_inc(xf_ready, 1)
            mean_eps(S_SS, S_VAR, D, ssqf, TT, varf)
            dve.wait_ge(sdf, 1)
            link(v.reciprocal(S_RS, S_SD))
            dve.wait_ge(gfin_in, 16)
            for i in range(TT):
                v.scalar_tensor_tensor(OUTB[:, i, :], X[:, i, :], S_RS[:, i:i + 1], SIG[:], ALU.mult, ALU.mult).then_inc(out_ready, 1)


def kernel(**inputs):
    import concourse.bacc as bacc
    from concourse.bass_utils import run_bass_kernel_spmd

    f = {k: np.asarray(a) for k, a in inputs.items()}
    x = f["x"].reshape(SEQ, D)
    w_in, b_in = f["w_in"][0], f["b_in"][0]
    at = {}
    off = 0
    for name, size in (("gq", 512), ("gk", 512), ("gv", 1024), ("gr", 1024), ("lr", 16), ("sq", 1024),
                       ("sk", 128), ("sv", 128), ("ga", 1024), ("gb", 1024)):
        at[name] = off
        off += size

    def units(w):
        return w.reshape(2, KH, P, -1).transpose(0, 2, 1, 3).reshape(2, P, -1)

    def columns(name):
        if name[:2] in ("gl", "sw", "wo"):
            w = f[{"gl": "w_gla_out", "sw": "w_swa_out", "wo": "w_out"}[name[:2]]][0]
            n = int(name[-1]) * BW
            return w[:, n:n + BW]
        n = at[name[:2]] + (int(name[2]) * BW if len(name) > 2 else 0)
        return w_in[:, n:n + BW]

    def feature_columns(a):
        return a.reshape(-1, P).T

    s0 = at["sk"]
    lr0 = at["lr"]
    cv = np.zeros((P, NCV), np.float32)
    for c, a in ((C_GMIX, f["g_mix"][0]), (C_BQ, b_in[at["gq"]:at["gq"] + 512]), (C_BK, b_in[at["gk"]:at["gk"] + 512]),
                 (C_BGA, b_in[at["ga"]:at["ga"] + D]), (C_BGB, b_in[at["gb"]:at["gb"] + D]),
                 (C_BGATE, f["b_gla_gate"][0]), (C_GFFN, f["g_ffn"][0])):
        cv[:, c:c + a.size // P] = feature_columns(a)
    cv[0:RANK, C_BLR] = b_in[lr0:lr0 + RANK]
    brow = np.zeros((len(BIAS_ROWS), BW), np.float32)
    for n, name in enumerate(BIAS_ROWS):
        if name == "skv":
            brow[n, 0:KVW] = b_in[s0:s0 + KVW]
        else:
            c = at[name[:2]] + int(name[2]) * BW
            brow[n] = b_in[c:c + BW]
    sinks = f["sinks"][0].reshape(QH // HG, 2, 2).transpose(0, 2, 1).reshape(-1)
    rows = np.concatenate([sinks, f["g_gla_head"][0], f["b_router"][0]])[None, :]
    w1 = f["w_e1"][0].reshape(NE, KT, P, D, 2).transpose(0, 1, 2, 4, 3).reshape(NE, CH1, P, SLOTW)
    w2 = f["w_e2"][0].reshape(NE, CH2, 2, P, D).transpose(0, 1, 3, 2, 4).reshape(NE, CH2, P, SLOTW)
    arrays = {
        "x": x,
        "wblk": np.concatenate([units(columns(n)) for n in BLOCKS if n != "skv"]),
        "wskv": units(np.concatenate([w_in[:, s0:s0 + KVW], w_in[:, lr0:lr0 + RANK],
                                      np.zeros((D, SKVW - KVW - RANK), np.float32)], axis=1)),
        "wgate": f["w_gla_gate"][0],
        "cv": cv,
        "rows": rows,
        "brow": brow,
        "tab": tables(),
        "wrout": f["w_router"][0].reshape(KT, P, NE).transpose(1, 0, 2),
        "be1": f["b_e1"][0].reshape(NE, D, 2).transpose(0, 2, 1).reshape(NE, 2 * D),
        "be2": f["b_e2"][0],
        "gfin": f["g_final"][None, :],
        "wexp": np.concatenate([w1, w2], axis=1).reshape(NE * CH, P, SLOTW),
    }
    arrays = {k: np.ascontiguousarray(a) for k, a in arrays.items()}
    nc = bacc.Bacc("TRN2", target_bir_lowering=False, num_devices=1)
    args = [nc.dram_tensor(k, a.shape, F32, kind="ExternalInput").ap() for k, a in arrays.items()]
    out = nc.dram_tensor("out", (SEQ, D), F32, kind="ExternalOutput").ap()
    program(nc, *args, out)
    res = run_bass_kernel_spmd(nc, [arrays], core_ids=[0])
    return res.results[0]["out"].reshape(1, SEQ, D)
```

```python
from contextlib import ExitStack

import numpy as np

import concourse.bass as bass
from concourse import mybir

ALU = mybir.AluOpType
ACT = mybir.ActivationFunctionType
F32 = mybir.dt.float32
F32R = mybir.dt.float32r
BF16 = mybir.dt.bfloat16
U32 = mybir.dt.uint32
I32 = mybir.dt.int32
AX_X = mybir.AxisListType.X

P = 128
D = 1024
SEQ = 256
TT = SEQ // P
KT = D // P
EPS = 1e-5
GH, GDK, GDV = 4, 128, 256
TAU = 16.0
GSCALE = GDK ** -0.5
CLAMP = 38.0
RANK = 16
QH, HD = 16, 64
KVW = 256
HALF = HD // 2
QSCALE = HD ** -0.5
HG = 4
NGRP = QH // HG * TT
NEG = -1e30
NE = 32
TOPK = 4
SLOTS = 64
PASSES = SEQ // SLOTS
LIMIT = 7.0
ALPHA = 1.702
FT = D // P
BW = 512
NSLOT = 16
SLOTW = 2048
RING0 = 10
W_SLOTS = [1, 2, 4, 6, 8]
H_SLOTS = [3, 5, 7, 9]
HTL_SLOT = 0
CH1, CH2 = 8, 4
CH = CH1 + CH2
UNROLL = 4

EARLY = NSLOT - RING0 + 1

BLOCKS = ["sq0", "sq1", "skv", "gq", "gk", "gv0", "gv1", "gr0", "gr1", "ga0", "ga1", "gb0", "gb1",
          "glao0", "glao1", "swao0", "swao1", "wo0", "wo1"]
NB = len(BLOCKS)
NU = 2 * NB
KH = KT // 2
GATES_DONE = 2 * (BLOCKS.index("gb1") + 1)
SKVW = 384
TOKEN_MAJOR = {"sq0", "sq1", "skv", "gv0", "gv1", "gr0", "gr1", "wo0", "wo1"}
BIAS_ROWS = ["sq0", "sq1", "skv", "gv0", "gv1", "gr0", "gr1"]
NPJ = 3

C_GMIX, C_BQ, C_BK, C_BGA, C_BGB, C_BGATE, C_GFFN, C_BLR = 0, 8, 12, 16, 24, 32, 36, 44
NCV = 45
R_SINK, R_HEAD, R_ROUTER = 0, 16, 272
NROW = 304
T_ID = 0
T_SWA = T_ID + P
T_DIAG = T_SWA + SEQ
T_COS = T_DIAG + 32
T_SIN = T_COS + TT * HALF
T_TRI = T_SIN + TT * HALF
T_ONE = T_TRI + P
T_IOTA = T_ONE + P
T_THR = T_IOTA + SLOTS
T_HOT = T_THR + PASSES
NTAB = T_HOT + NE


def tables():
    t = np.zeros((P, NTAB), np.float32)
    p = np.arange(P)[:, None]
    t[:, T_ID:T_ID + P] = np.eye(P)
    s = np.arange(SEQ)[None, :]
    t[:, T_SWA:T_SWA + SEQ] = np.where((s > p) & (s <= p + P), 0.0, NEG)
    t[:, T_DIAG:T_DIAG + 32] = np.arange(32)[None, :] >= p % 32
    inv = np.float32(10000.0) ** (-np.arange(HALF, dtype=np.float32) / np.float32(HALF))
    for i in range(TT):
        ang = (np.arange(P, dtype=np.float32) + np.float32(P * i))[:, None] * inv[None, :]
        t[:, T_COS + i * HALF:T_COS + (i + 1) * HALF] = np.cos(ang)
        t[:, T_SIN + i * HALF:T_SIN + (i + 1) * HALF] = np.sin(ang)
    t[:, T_TRI:T_TRI + P] = p < np.arange(P)[None, :]
    t[:, T_ONE:T_ONE + P] = 1.0
    t[:, T_IOTA:T_IOTA + SLOTS] = np.arange(SLOTS)[None, :]
    t[:, T_THR:T_THR + PASSES] = np.arange(PASSES)[None, :] * SLOTS
    t[:, T_THR] = -1.0
    t[:, T_HOT:T_HOT + NE] = np.arange(NE)[None, :] == p % NE
    return t


def program(nc, x, wblk, wskv, wgate, cv, rows, brow, tab, wrout, be1, be2, gfin, wexp, out):
    with ExitStack() as ctx:
        def sb(name, shape, dt=F32):
            return ctx.enter_context(nc.sbuf_tensor(name, shape, dt))

        def sem(name):
            return ctx.enter_context(nc.semaphore(name))

        shapes = {"HT": [P, KT, SEQ], "GV": [P, TT, D], "GR": [P, TT, D], "SQ": [P, TT, D], "SQR": [P, TT, D]}
        with ExitStack() as rounded:
            slots_R = [rounded.enter_context(nc.sbuf_tensor(f"slot{n}_R", [P, SLOTW], F32R)) for n in range(NSLOT)]
            HT_R, GV_R, GR_R, SQ_R, SQR_R = [
                rounded.enter_context(nc.sbuf_tensor(name + "_R", shape, F32R)) for name, shape in shapes.items()]
        ring = sb("ring", [P, NSLOT * SLOTW])
        HT = sb("HT", shapes["HT"])
        GV = sb("GV", shapes["GV"])
        GR = sb("GR", shapes["GR"])
        SQ = sb("SQ", shapes["SQ"])
        SQR = sb("SQR", shapes["SQR"])
        X = sb("X", [P, TT, D])
        SIG = sb("SIG", [P, D])
        KVRAW = sb("KVRAW", [P, TT, KVW])
        KD = sb("KD", [P, TT, 4 * HD])
        KTT = sb("KTT", [P, 2, SEQ])
        PTG = sb("PTG", [P, GH, 3, P])
        BRW = sb("BRW", [P, 2, BW])
        CV = sb("CV", [P, NCV])
        ROW = sb("ROW", [P, NROW])
        TAB = sb("TAB", [P, NTAB])
        WR = sb("WR", [P, KT, NE])
        BE1 = sb("BE1", [3 * NE, 2 * D], BF16)
        SM = sb("SM", [P, 168])
        NBI = sb("NBI", [P, 1], I32)

        tail = [RING0 * SLOTW]

        def in_tail(n):
            tail[0] += n
            assert tail[0] <= NSLOT * SLOTW
            return ring[:, tail[0] - n:tail[0]]

        GQT, GKT, B, W0, W1, W2, TMP = [in_tail(GH * SEQ) for _ in range(7)]
        SS = in_tail(2 * HG * SEQ).rearrange("p (b h s) -> p b h s", b=2, h=HG)
        PTS = in_tail(2 * HG * SEQ).rearrange("p (b h s) -> p b h s", b=2, h=HG)
        WG = in_tail(GH * GDK)
        LRT = in_tail(SEQ)

        ident = TAB[:, T_ID:T_ID + P]

        def col(c, n=1, p=P):
            return CV[0:p, c:c + n]

        def small(a, n):
            return SM[:, a:a + n]
        S_SS, S_VAR, S_SD, S_RS = small(0, 2), small(2, 2), small(4, 2), small(6, 2)
        S_MX = [small(10 + 4 * b, 4) for b in range(2)]
        S_NM = [small(18 + 4 * b, 4) for b in range(2)]
        S_SUM = [small(26 + 4 * b, 4) for b in range(2)]
        S_DS = [small(34 + 4 * b, 4) for b in range(2)]
        S_ES = [small(42 + 4 * b, 4) for b in range(2)]
        S_DEN = [small(50 + 4 * b, 4) for b in range(2)]
        S_RD = [small(58 + 4 * b, 4) for b in range(2)]
        S_GS, S_GVAR, S_GSD, S_GRS = small(66, 8), small(74, 8), small(82, 8), small(90, 8)
        S_V8 = [small(98 + 8 * i, 8) for i in range(TT)]
        S_IF = [small(114 + 8 * i, 8) for i in range(TT)]
        S_NV = [small(130 + i, 1) for i in range(TT)]
        S_EG = [small(132 + 4 * i, 4) for i in range(TT)]
        S_ES4 = [small(140 + i, 1) for i in range(TT)]
        S_RG = [small(142 + i, 1) for i in range(TT)]
        S_GT = [small(144 + 4 * i, 4) for i in range(TT)]
        S_SQ = small(158, 4)
        S_PRE = small(162, 1)
        S_CNT, S_CMP, S_NP = small(152, 1), small(153, PASSES), small(157, 1)
        IDX = [sb(f"IDX{i}", [P, 8], U32) for i in range(TT)]

        RSR, DIAG = SIG[:, 0:SEQ], SIG[:, BW:BW + SEQ]

        def feature(t):
            return t[:].rearrange("p i d -> p (i d)").rearrange("p (k t) -> p k t", k=KT)

        def slot(s, rounded=False):
            return slots_R[s][:] if rounded else ring[:, s * SLOTW:(s + 1) * SLOTW]

        HTL, HTL_R = (slot(HTL_SLOT, r).rearrange("p (k t) -> p k t", k=KT) for r in (False, True))
        qT = feature(SQ)
        HT2 = (HT_R[:], HTL_R)
        OB2 = (feature(SQ_R), feature(SQR_R))
        OA2 = (feature(GV_R), feature(GR_R))
        MIX2 = OA2
        HTf = HT[:].rearrange("p k t -> p (k t)")
        xn = GV
        xnT = HT
        GRf = GR[:].rearrange("p i d -> p (i d)")
        RK = GRf[:, 0:TT * 129].rearrange("p (i e) -> p i e", i=TT)
        GT_ = GRf[:, 264:264 + TT * NE].rearrange("p (i e) -> p i e", i=TT)
        LG = GRf[:, 328:328 + TT * NE].rearrange("p (i e) -> p i e", i=TT)
        MK = GRf[:, 392:392 + TT * NE].rearrange("p (i e) -> p i e", i=TT)
        OH = GRf[:, 456:456 + TT * TOPK * NE].rearrange("p (i k e) -> p i k e", i=TT, k=TOPK)
        BIG = GRf[:, 712:712 + TT * NE].rearrange("p (i e) -> p i e", i=TT)
        KVf = KVRAW[:].rearrange("p i d -> p (i d)")
        OG = KVf[:, 0:TT * TOPK * NE].rearrange("p (i k e) -> p i k e", i=TT, k=TOPK)
        BE1R = HTf[0:NE, :]
        BE2R = HTf[NE:2 * NE, 0:D].rearrange("p (g w) -> p g w", g=2)
        BE2 = BRW[0:3 * NE, :, SEQ:2 * SEQ].bitcast(BF16)
        SQRf = SQR[:].rearrange("p i d -> p (i d)")
        SQf = SQ[:].rearrange("p i d -> p (i d)")
        XP = [a.bitcast(BF16).rearrange("p (i d) -> p i d", i=TT)
              for a in (SQRf[:, 0:D], SQRf[:, D:2 * D], GRf[:, D:2 * D])]
        REST = SQf.rearrange("p (i d) -> p i d", i=TT)
        XT = SQf[:, 0:512].rearrange("p (k c) -> p k c", k=KT)
        GLU, LIN, SGM = SQf[:, 512:1024], SQf[:, 1024:1536], SQf[:, 1536:2048]
        PTf = PTG[:].rearrange("p h b t -> p (h b t)")
        AT = PTf[:, 0:512]
        Y = PTf[:, 512:1024]
        SELG = PTf[:, 1024:1280].rearrange("p (i r c) -> p i r c", i=TT, r=2)
        SEL = PTf[:, 1280:1344].bitcast(BF16).rearrange("p (i c) -> p i c", i=TT)
        SELE = PTf[0:3 * NE, 1344:1376].bitcast(BF16)
        KDf = KD[:].rearrange("p i d -> p (i d)")
        KTf = KTT[:].rearrange("p g t -> p (g t)")
        MIX = [SIG[:, 0:BW], SIG[:, BW:D], KVf, KDf]
        GB = [PTf[:, 0:BW], PTf[:, BW:D], PTf[:, D:D + BW], KTf]
        SELT = BRW
        OUTB = GV

        PS = ctx.enter_context(nc.psum_tensor("PS", [P, 8, 512], F32))

        def bk(b, w=512, p=P):
            return PS[0:p, b, 0:w]

        x_in, ident_in, tab_in, cv_in, row_in = sem("x_in"), sem("ident_in"), sem("tab_in"), sem("cv_in"), sem("row_in")
        wg_in, wr_in, be1_in, be2_in, gfin_in = sem("wg_in"), sem("wr_in"), sem("be1_in"), sem("be2_in"), sem("gfin_in")
        unit_in = [sem(f"unit_in{q}") for q in range(len(W_SLOTS))]
        hi_ready = sem("hi_ready")
        lo_v, lo_p = sem("lo_v"), sem("lo_p")
        first_used = sem("first_used")
        bias_in = [sem(f"bias_in{q}") for q in range(2)]
        pj_full = [sem(f"pj_full{b}") for b in range(NPJ)]
        pj_free = [sem(f"pj_free{b}") for b in range(NPJ)]
        ssq0, var0, sd0 = sem("ssq0"), sem("var0"), sem("sd0")
        diag_ready, rsr_full, xt_full, ht_raw, ht_hi, ht_ready = (
            sem("diag_ready"), sem("rsr_full"), sem("xt_full"), sem("ht_raw"), sem("ht_hi"), sem("ht_ready"))
        lr_full, lr_ready, z_full, z_ready = sem("lr_full"), sem("lr_ready"), sem("z_full"), sem("z_ready")
        qrot_ready, qt_full, qt_ready = sem("qrot_ready"), sem("qt_full"), sem("qt_ready")
        krot_ready, kt_full, kt_ready = sem("krot_ready"), sem("kt_full"), sem("kt_ready")
        gate_neg, gate_sp, decay_in, decay_out = sem("gate_neg"), sem("gate_sp"), sem("decay_in"), sem("decay_out")
        gla_ops, gla_sc, gla_pt, gla_o, gla_sq, gla_var, gla_sd, gla_oa = (
            sem("gla_ops"), sem("gla_sc"), sem("gla_pt"), sem("gla_o"), sem("gla_sq"), sem("gla_var"), sem("gla_sd"), sem("gla_oa"))
        gla_zero = sem("gla_zero")
        gr_sig, gr_ready = sem("gr_sig"), sem("gr_ready")
        oat_full, oat_hi, oat_lo = sem("oat_full"), sem("oat_hi"), sem("oat_lo")
        obt_full, obt_hi, obt_lo = sem("obt_full"), sem("obt_hi"), sem("obt_lo")
        sw_s, sw_masked, sw_max, sw_exp = sem("sw_s"), sem("sw_masked"), sem("sw_max"), sem("sw_exp")
        sw_t, sw_ptA, sw_ptV, sw_o, sw_out = sem("sw_t"), sem("sw_ptA"), sem("sw_ptV"), sem("sw_o"), sem("sw_out")
        rsf, xg_ready, out_a = sem("rsf"), sem("xg_ready"), sem("out_a")
        ht_lo_p, gr_half, be2_ready, ssqh, rp1, rp2 = (
            sem("ht_lo_p"), sem("gr_half"), sem("be2_ready"), sem("ssqh"), sem("rp1"), sem("rp2"))
        mix_ready, mix_hi, mix_lo = sem("mix_ready"), sem("mix_hi"), sem("mix_lo")
        ssq1, var1, sd1, xn_ready, xnT_full, xnT_ready, lg_full = (
            sem("ssq1"), sem("var1"), sem("sd1"), sem("xn_ready"), sem("xnT_full"), sem("xnT_ready"), sem("lg_full"))
        top_ready, eg_ready, mask_ready, rank_full, gat_ready, gatT_full, gatT_ready, np_ready = (
            sem("top_ready"), sem("eg_ready"), sem("mask_ready"), sem("rank_full"), sem("gat_ready"), sem("gatT_full"), sem("gatT_ready"), sem("np_ready"))
        slot_in = [sem(f"slot_in{s}") for s in range(NSLOT)]
        chunk_used = sem("chunk_used")
        sel_ready, xg_full, xt_ready = sem("sel_ready"), sem("xg_full"), sem("xt_ready")
        u_read, glu_ready, sgm_ready, act_ready = sem("u_read"), sem("glu_ready"), sem("sgm_ready"), sem("act_ready")
        y_ready, at_full, at_ready = sem("y_ready"), sem("at_full"), sem("at_ready")
        selg_ready, selT_full, selT_a, selT_b = sem("selg_ready"), sem("selT_full"), sem("selT_a"), sem("selT_b")
        sele_ready, xp1, rest1, xp2, xp3, be1_ready = (
            sem("sele_ready"), sem("xp1"), sem("rest1"), sem("xp2"), sem("xp3"), sem("be1_ready"))
        moe_done, xf_ready, ssqf, varf, sdf, out_ready, out_done = (
            sem("moe_done"), sem("xf_ready"), sem("ssqf"), sem("varf"), sem("sdf"), sem("out_ready"), sem("out_done"))
        qt_cp, selg_raw, lin_ready = sem("qt_cp"), sem("selg_raw"), sem("lin_ready")
        dve_step, act_step = sem("dve_step"), sem("act_step")

        block = ctx.enter_context(nc.Block())

        def w_slot(u):
            return (u - (NU - len(W_SLOTS))) % len(W_SLOTS)

        def w_unit(u, rounded=False):
            return slot(W_SLOTS[w_slot(u)], rounded)[:, 0:unit_width(u)]

        def h_unit(u, rounded=False):
            return slot(H_SLOTS[(u - (NU - len(H_SLOTS))) % len(H_SLOTS)], rounded)[:, 0:unit_width(u)]

        def unit_width(u):
            return KH * (SKVW if BLOCKS[u // 2] == "skv" else BW)

        def by_pool(u):
            return u % 2 == 1 or u == 18

        def split_done(eng, u):
            n = sum(by_pool(m) == by_pool(u) for m in range(u + 1))
            eng.wait_ge(lo_p if by_pool(u) else lo_v, n)

        def landed(eng, u):
            fills = sum(w_slot(n) == w_slot(u) for n in range(u + 1))
            eng.wait_ge(unit_in[w_slot(u)], 16 * fills)

        def slot_of(c):
            s = (RING0 + c) % NSLOT
            return s, ring[:, s * SLOTW:(s + 1) * SLOTW]

        def multiplied(eng, u):
            if u % 2 == 0:
                eng.wait_ge(first_used, u // 2 + 1)
            elif BLOCKS[u // 2] == "skv":
                eng.wait_ge(lr_full, 1)
            else:
                eng.wait_ge(pj_full[u % NPJ], u // NPJ + 1)

        def evacuated(eng, u):
            eng.wait_ge(pj_free[u % NPJ], u // NPJ + 1)

        @block.sync
        def _(sp):
            for i in range(TT):
                sp.dma_start(X[:, i, :], x[i * P:(i + 1) * P, :]).then_inc(x_in, 16)

            def bias(n):
                sp.dma_start(BRW[:, n % 2, :], brow[n:n + 1, :].partition_broadcast(P)).then_inc(bias_in[n % 2], 16)

            def first_chunk(c):
                s, dst = slot_of(c)
                if c == 0:
                    sp.wait_ge(gla_o, GH)
                    sp.wait_ge(sw_out, NGRP)
                if RING0 + c >= NSLOT and c < NSLOT:
                    if s == HTL_SLOT:
                        multiplied(sp, GATES_DONE - 1)
                    elif s in W_SLOTS:
                        multiplied(sp, NU - len(W_SLOTS) + W_SLOTS.index(s))
                    else:
                        multiplied(sp, NU - len(H_SLOTS) + H_SLOTS.index(s))
                if c >= NSLOT:
                    sp.wait_ge(chunk_used, c - NSLOT + 1)
                sp.dma_start(dst, wexp[c]).then_inc(slot_in[s], 16)

            early = 0
            for u in range(NU):
                if u >= len(W_SLOTS):
                    multiplied(sp, u - len(W_SLOTS))
                if BLOCKS[u // 2] == "skv":
                    sp.dma_start(w_unit(u), wskv[u % 2]).then_inc(unit_in[w_slot(u)], 16)
                else:
                    sp.dma_start(w_unit(u), wblk[u - 2 * (u >= 6)]).then_inc(unit_in[w_slot(u)], 16)
                if u == 0:
                    sp.dma_start(TAB[:, P:NTAB], tab[:, P:NTAB]).then_inc(tab_in, 16)
                if u in (1, 2):
                    bias(u - 1)
                for n in range(2, len(BIAS_ROWS)):
                    last = BLOCKS.index(BIAS_ROWS[n - 2])
                    if u == 2 * last + 7:
                        evacuated(sp, 2 * last)
                        evacuated(sp, 2 * last + 1)
                        bias(n)
                if u >= GATES_DONE + 2 and (u - GATES_DONE - 2) % 4 < 3 and early < EARLY:
                    first_chunk(early)
                    early += 1
            assert early == EARLY

            def load_body(turn, e0):
                for c in range(UNROLL * CH):
                    s, dst = slot_of(c)
                    sp.wait_ge(chunk_used, turn * (UNROLL * CH) + c - NSLOT + 1)
                    sp.dma_start(dst, wexp[e0 * CH + c]).then_inc(slot_in[s], 16)

            for c in range(EARLY, UNROLL * CH):
                first_chunk(c)
            with sp.Fori(1, NE // UNROLL) as i:
                load_body(i, i * UNROLL)
            sp.wait_ge(np_ready, 1)
            passes = sp.value_load(NBI[0:1, 0:1], min_val=1, max_val=PASSES)
            with sp.If(passes > 1):
                with sp.Fori(1, passes) as b:
                    with sp.Fori(0, NE // UNROLL) as i:
                        load_body(b * (NE // UNROLL) + i, i * UNROLL)
            for i in range(TT):
                sp.wait_ge(out_ready, i + 1)
                sp.dma_start(out[i * P:(i + 1) * P, BW:D], OUTB[:, i, BW:D]).then_inc(out_done, 16)
            sp.wait_ge(out_done, 2 * 16 * TT)

        @block.gpsimd
        def _(pool):
            nc.gpsimd.memset(PTG[:], 0.0).then_inc(gla_zero, 1)
            for n in range(2):
                pool.wait_ge(ht_hi, n + 1)
                nc.gpsimd.tensor_tensor(HT2[1][:, 2 * n:2 * n + 2, :], HTL[:, 2 * n:2 * n + 2, :],
                                        HT_R[:, 2 * n:2 * n + 2, :].bitcast(F32), ALU.subtract).then_inc(ht_lo_p, 1)
            pool.dma_start(ROW[:], rows.partition_broadcast(P)).then_inc(row_in, 16)
            pool.dma_start(WG[0:RANK, :], wgate).then_inc(wg_in, 16)
            pool.dma_start(WR[:], wrout).then_inc(wr_in, 16)

            def gr_finish(u):
                n, m = (u - 14) // 2, u % 2
                part = GR[:, m, n * BW:(n + 1) * BW]
                pool.wait_ge(gr_sig, u - 13)
                nc.gpsimd.tensor_tensor(part, part, SIG[:, m * BW:(m + 1) * BW], ALU.mult).then_inc(gr_half, 1)
                pool.wait_ge(gr_half, u - 13)
                pv = part.rearrange("p (h d) -> p h d", h=2)
                nc.gpsimd.tensor_tensor(pv, pv, ROW[:, R_HEAD:R_HEAD + GDV].unsqueeze(1).broadcast_to([P, 2, GDV]),
                                        ALU.mult).then_inc(gr_ready, 1)

            for u in range(NU):
                if by_pool(u):
                    pool.wait_ge(hi_ready, u + 1)
                    nc.gpsimd.tensor_tensor(w_unit(u, True), w_unit(u), h_unit(u, True).bitcast(F32),
                                            ALU.subtract).then_inc(lo_p, 1)
                if u == 17:
                    pool.wait_ge(row_in, 16)
                if u in (19, 20):
                    gr_finish(u - 5)
                if u == 21:
                    gr_finish(16)
                    gr_finish(17)
                if u == 27:
                    multiplied(pool, GATES_DONE - 1)
                    pool.dma_start(BE1R, be1).then_inc(be1_in, 16)
                    pool.dma_start(BE2R, be2.rearrange("e (g w) -> e g w", g=2)).then_inc(be2_in, 16)
            pool.wait_ge(mix_lo, 4)
            pool.dma_start(SIG[:], gfin.partition_broadcast(P)).then_inc(gfin_in, 16)
            pool.wait_ge(xp1, 1)
            nc.gpsimd.tensor_tensor(REST[:, 1, :], xn[:, 1, :], XP[0][:, 1, :], ALU.subtract).then_inc(rp1, 1)
            pool.wait_ge(xp2, 1)
            nc.gpsimd.tensor_tensor(XP[2][:, 1, :], REST[:, 1, :], XP[1][:, 1, :], ALU.subtract).then_inc(rp2, 1)

        @block.tensor
        def _(pe):
            mm = nc.tensor.matmul

            pe.wait_ge(ident_in, 16)
            pe.wait_ge(x_in, 16 * TT)
            for a in range(4):
                for q in range(4):
                    k, i = 2 * a + q // 2, q % 2
                    last = nc.tensor.transpose(PS[:, 4 + a, q * P:(q + 1) * P], X[:, i, k * P:(k + 1) * P], ident)
                last.then_inc(xt_full, 1)
            pe.wait_ge(tab_in, 16)
            pe.wait_ge(diag_ready, TT)
            for i in range(TT):
                last = mm(PS[:, 3, i * P:(i + 1) * P], TAB[:, T_ONE:T_ONE + P], DIAG[:, i * P:(i + 1) * P],
                          start=True, stop=True)
            last.then_inc(rsr_full, 1)

            usage = [0]

            def pj_bank():
                b, n = usage[0] % NPJ, usage[0] // NPJ
                usage[0] += 1
                if n:
                    pe.wait_ge(pj_free[b], n)
                return b

            def dense(i, hooks={}):
                name = BLOCKS[i]
                token = name in TOKEN_MAJOR
                src = {"gl": OA2, "sw": OB2, "wo": MIX2}.get(name[:2], HT2)
                w = KVW if name == "skv" else BW
                width = SKVW if name == "skv" else BW
                banks = []
                for kh in range(2):
                    u = 2 * i + kh
                    split_done(pe, u)
                    ws = (h_unit(u, True), w_unit(u, True))
                    if name[:2] == "wo":
                        pe.wait_ge(mix_lo, 2 * (kh + 1))
                    if i == 0:
                        pe.wait_ge(ht_ready if kh else ht_lo_p, 2)

                    def chain(dst, left, right):
                        for k in range(KH):
                            for a, b in ((0, 0), (1, 0), (0, 1)):
                                last = mm(dst, left(k, a), right(k, b), start=(kh == 0 and k == 0 and a + b == 0 and first),
                                          stop=(kh == 1 and k == KH - 1 and b == 1), skip_group_check=True)
                        return last

                    for half in range(2):
                        if kh == 0:
                            banks.append(pj_bank())
                        b = banks[half]
                        first = True
                        if token:
                            last = chain(bk(b, w), lambda k, p: src[p][:, KH * kh + k, half * P:(half + 1) * P],
                                         lambda k, p: ws[p][:, k * width:k * width + w])
                        else:
                            for f in range(2):
                                first = f == 0
                                c = (2 * half + f) * P
                                last = chain(PS[:, b, f * SEQ:(f + 1) * SEQ], lambda k, p: ws[p][:, k * width + c:k * width + c + P],
                                             lambda k, p: src[p][:, KH * kh + k, :])
                        if kh == 1:
                            last.then_inc(pj_full[b], 1)
                        elif half == 1 and name != "skv":
                            last.then_inc(first_used, 1)
                        if half == 1 and name == "skv":
                            first = True
                            last = chain(PS[:, 3, 0:SEQ], lambda k, p: ws[p][:, k * width + KVW:(k + 1) * width],
                                         lambda k, p: src[p][:, KH * kh + k, :])
                            last.then_inc(lr_full if kh else first_used, 1)
                        for step in hooks.get((kh, half), ()):
                            step()

            def transpose16(get_src, full):
                for a in range(4):
                    for q in range(4):
                        k, i = 2 * a + q // 2, q % 2
                        last = nc.tensor.transpose(PS[:, 4 + a, q * P:(q + 1) * P], get_src(i, k), ident)
                    last.then_inc(full, 1)

            dense(0)
            dense(1)
            dense(2)
            def gate_input():
                pe.wait_ge(lr_ready, 1)
                pe.wait_ge(wg_in, 16)
                for h in range(GH):
                    last = mm(PS[:, 6 + h // 2, (h % 2) * SEQ:(h % 2 + 1) * SEQ], WG[0:RANK, h * GDK:(h + 1) * GDK],
                              LRT[0:RANK, :], start=True, stop=True)
                last.then_inc(z_full, 1)

            dense(3, {(0, 1): [gate_input]})
            dense(4)
            pe.wait_ge(krot_ready, TT)
            for g in range(2):
                for i in range(TT):
                    last = nc.tensor.transpose(PS[:, 3, (2 * g + i) * P:(2 * g + i + 1) * P],
                                               KD[:, i, g * P:(g + 1) * P], ident)
            last.then_inc(kt_full, 1)
            pe.wait_ge(qrot_ready, TT)
            pe.wait_ge(z_ready, GH)
            transpose16(lambda i, k: SQR[:, i, k * P:(k + 1) * P], qt_full)

            def scores(n):
                i, g4 = n // (NGRP // TT), n % (NGRP // TT)
                if n == 0:
                    pe.wait_ge(qt_ready, 2)
                    pe.wait_ge(qt_cp, 2)
                    pe.wait_ge(kt_ready, 1)
                else:
                    pe.wait_ge(sw_masked, 2 * n)
                ns = (i + 1) * P
                for hh in range(HG):
                    h = HG * g4 + hh
                    p0 = (h % 2) * HD
                    last = mm(PS[:, 4 + hh % 2, (hh // 2) * SEQ:(hh // 2) * SEQ + ns],
                              qT[p0:p0 + HD, h // 2, i * P:(i + 1) * P],
                              KTT[p0:p0 + HD, h // (QH // 2), 0:ns], start=True, stop=True)
                last.then_inc(sw_s, 1)

            def probs_t(n):
                i = n // (NGRP // TT)
                pe.wait_ge(sw_exp, n + 1)
                if n:
                    pe.wait_ge(sw_ptA, n)
                    pe.wait_ge(sw_ptV, n)
                for hh in range(HG):
                    for st in range(i + 1):
                        last = nc.tensor.transpose(PS[:, 6 + hh // 2, (2 * (hh % 2) + st) * P:(2 * (hh % 2) + st + 1) * P],
                                                   SS[:, n % 2, hh, st * P:(st + 1) * P], ident)
                last.then_inc(sw_t, 1)

            def values(n):
                i, g4 = n // (NGRP // TT), n % (NGRP // TT)
                pe.wait_ge(sw_ptA, n + 1)
                pe.wait_ge(sw_ptV, n + 1)
                if n:
                    pe.wait_ge(sw_out, n)
                kv = g4 // 2
                for hh in range(HG):
                    for st in range(i + 1):
                        last = mm(PS[:, 3, hh * HD:(hh + 1) * HD], PTS[:, n % 2, hh, st * P:(st + 1) * P],
                                  KVRAW[:, st, P + kv * HD:P + (kv + 1) * HD], start=(st == 0), stop=(st == i))
                last.then_inc(sw_o, 1)

            def swa_slot(n):
                def run(n=n):
                    if 0 <= n - 2 < NGRP:
                        values(n - 2)
                    if 0 <= n - 1 < NGRP:
                        probs_t(n - 1)
                    if n < NGRP:
                        scores(n)
                return run

            def attention_slots(i):
                n = 2 * (i - 5)
                return {(0, 1): [swa_slot(n)], (1, 1): [swa_slot(n + 1)]}

            for i in range(5, 10):
                dense(i, attention_slots(i))

            def attention_t():
                pe.wait_ge(sw_out, NGRP)
                transpose16(lambda i, k: SQR[:, i, k * P:(k + 1) * P], obt_full)

            def gla_scores():
                pe.wait_ge(obt_hi, 4)
                pe.wait_ge(obt_lo, 4)
                pe.wait_ge(gla_ops, 5)
                for h in range(GH):
                    w0, w1, w2 = (w[:, h * SEQ:(h + 1) * SEQ] for w in (W0, W1, W2))
                    gq, gk = GQT[:, h * SEQ:(h + 1) * SEQ], GKT[:, h * SEQ:(h + 1) * SEQ]
                    mm(PS[:, 4 + h, 0:P], w0[:, 0:P], w0[:, P:SEQ], start=True, stop=True)
                    for i in range(TT):
                        c = P + i * P
                        t0 = i * P
                        mm(PS[0:64, 4 + h, c:c + 64], w1[:, t0:t0 + 64], w1[:, t0 + 64:t0 + 128], start=True, stop=True)
                        for q in range(2):
                            s0 = t0 + 64 * q
                            mm(PS[64 * q:64 * q + 32, 4 + h, c + 64:c + 96], w2[:, s0:s0 + 32], w2[:, s0 + 32:s0 + 64],
                               start=True, stop=True)
                        for q in range(4):
                            s0 = t0 + 32 * q
                            last = mm(PS[32 * q:32 * q + 32, 4 + h, c + 96:c + 128], gk[:, s0:s0 + 32], gq[:, s0:s0 + 32],
                                      start=True, stop=True)
                last.then_inc(gla_sc, 1)

            def gla_output():
                pe.wait_ge(gla_pt, 1)
                for u in range(10, 14):
                    evacuated(pe, u)
                for h in range(GH):
                    v = slice(h * GDV, (h + 1) * GDV)
                    mm(PS[:, 4 + h, 0:GDV], PTG[:, h, 1, :], GV[:, 0, v], start=True, stop=True)
                    mm(PS[:, 4 + h, GDV:2 * GDV], PTG[:, h, 0, :], GV[:, 0, v], start=True, stop=False)
                    last = mm(PS[:, 4 + h, GDV:2 * GDV], PTG[:, h, 2, :], GV[:, 1, v], start=False, stop=True)
                    last.then_inc(gla_o, 1)

            def gla_t():
                pe.wait_ge(gla_oa, GH * TT)
                transpose16(lambda i, k: GR[:, i, k * P:(k + 1) * P], oat_full)

            dense(10, {(0, 1): [attention_t]})
            gla_scores()
            dense(11, {(0, 1): [gla_output]})
            dense(12, {(1, 0): [gla_t]})
            pe.wait_ge(oat_hi, 4)
            pe.wait_ge(oat_lo, 4)
            for i in range(13, NB - 1):
                dense(i)

            def new_x_t(n):
                for i in range(TT):
                    evacuated(pe, 2 * (NB - 2 + n) + i)
                    for k in range(KH * n, KH * (n + 1)):
                        q = 2 * (k % 2) + i
                        last = nc.tensor.transpose(PS[:, 4 + k // 2, q * P:(q + 1) * P], X[:, i, k * P:(k + 1) * P], ident)
                        if i == TT - 1 and k % 2 == 1:
                            last.then_inc(xnT_full, 1)

            def logits(n):
                for k in range(KH * n, KH * (n + 1)):
                    if k % 2 == 0:
                        pe.wait_ge(xnT_ready, k // 2 + 1)
                    for i in range(TT):
                        last = mm(PS[:, 3 - i, 0:NE], xnT[:, k, i * P:(i + 1) * P], WR[:, k, :],
                                  start=(k == 0), stop=(k == KT - 1))
                return last

            pe.wait_ge(wr_in, 16)
            dense(NB - 1, {(0, 1): [lambda: new_x_t(0)], (1, 0): [lambda: logits(0)]})
            new_x_t(1)
            logits(1).then_inc(lg_full, 1)
            tri, ones = TAB[:, T_TRI:T_TRI + P], TAB[:, T_ONE:T_ONE + P]
            pe.wait_ge(mask_ready, 1)
            mm(PS[:, 4, 0:NE], tri, MK[:, 0, :], start=True, stop=True)
            mm(PS[:, 4, NE:2 * NE], tri, MK[:, 1, :], start=True, stop=False)
            mm(PS[:, 4, NE:2 * NE], ones, MK[:, 0, :], start=False, stop=True)
            mm(PS[:, 4, 2 * NE:3 * NE], ones, MK[:, 0, :], start=True, stop=False)
            mm(PS[:, 4, 2 * NE:3 * NE], ones, MK[:, 1, :], start=False, stop=True).then_inc(rank_full, 1)
            pe.wait_ge(y_ready, 1)
            pe.wait_ge(selT_a, 1)
            for n in range(4):
                last = mm(bk(n), SELT[:, 0, 0:P // 2].bitcast(BF16), Y[:, 0:256].bitcast(BF16),
                          start=True, stop=True, skip_group_check=True)

            def gather():
                for k in range(KT):
                    for n in range(3 * TT):
                        last = mm(PS[:, 7, k * SLOTS:(k + 1) * SLOTS], XP[n // TT][:, n % TT, k * P:(k + 1) * P],
                                  SEL[:, n % TT, :], start=(n == 0), stop=(n == 3 * TT - 1))
                last.then_inc(xg_full, 1)

            def scatter(tiles=range(TT)):
                for i in tiles:
                    for n in range(2):
                        last = mm(bk(2 * i + n), SELT[:, n, i * P:(i + 1) * P], Y,
                                  start=False, stop=True, skip_group_check=True)
                return last

            def both_halves(b, lhsT, rhs, start, stop):
                for g in range(2):
                    last = mm(PS[g * SLOTS:(g + 1) * SLOTS, b, :], lhsT, rhs[:, g * 512:(g + 1) * 512],
                              start=start, stop=stop)
                return last

            pe.wait_ge(xp3, 1)
            pe.wait_ge(rp2, 1)
            pe.wait_ge(sel_ready, 1)
            gather()
            pe.wait_ge(be1_ready, 1)
            pe.wait_ge(be2_ready, 1)
            pe.wait_ge(np_ready, 1)
            passes = pe.value_load(NBI[0:1, 0:1], min_val=1, max_val=PASSES)
            with pe.Fori(0, passes) as b:
                with pe.Fori(0, NE // UNROLL) as it:
                    turn = b * (NE // UNROLL) + it
                    for j in range(UNROLL):
                        e = turn * UNROLL + j

                        def chunk(c):
                            s, data = slot_of(j * CH + c)
                            pe.wait_ge(slot_in[s], turn * 48 + 16 * ((j * CH + c) // NSLOT + 1))
                            return data

                        pe.wait_ge(sele_ready, e + 1)
                        pe.wait_ge(selT_a, e + 1)
                        pe.wait_ge(selT_b, e + 1)
                        for n in range(2):
                            both_halves(4 + n, SELE, BE1[:, n * D:(n + 1) * D], True, False)
                        pe.wait_ge(y_ready, e + 1)
                        for g in range(2):
                            mm(PS[g * SLOTS:(g + 1) * SLOTS, 6, :], SELE, BE2[:, g, :], start=True, stop=False)
                        pe.wait_ge(xt_ready, e + 1)
                        for c in range(CH1):
                            w = chunk(c)
                            for n in range(2):
                                last = both_halves(4 + n, XT[:, c, :], w[:, n * D:(n + 1) * D], False, c == CH1 - 1)
                            last.then_inc(chunk_used, 1)
                            if c == 1:
                                scatter()
                        pe.wait_ge(sel_ready, e + 2)
                        gather()
                        pe.wait_ge(selg_ready, e + 1)
                        pe.wait_ge(u_read, e + 1)
                        for i in range(TT):
                            last = nc.tensor.transpose(PS[:, 5, i * P:(i + 1) * P], SELG[:, i], ident)
                        last.then_inc(selT_full, 1)
                        pe.wait_ge(act_ready, e + 2)
                        for q in range(4):
                            last = nc.tensor.transpose(PS[:, 4, q * P:(q + 1) * P], LIN[:, q * P:(q + 1) * P], ident)
                        last.then_inc(at_full, 1)
                        pe.wait_ge(at_ready, e + 1)
                        for c in range(CH2):
                            w = chunk(CH1 + c)
                            for kk in range(2):
                                f = 2 * c + kk
                                o = (2 * (f % 4) + f // 4) * SLOTS
                                last = both_halves(6, AT[:, o:o + SLOTS], w[:, kk * D:(kk + 1) * D],
                                                   False, f == FT - 1)
                            last.then_inc(chunk_used, 1)
            total = passes * NE
            pe.wait_ge(y_ready, total + 1)
            pe.wait_ge(selT_a, total + 1)
            pe.wait_ge(selT_b, total + 1)
            for i in range(TT):
                scatter([i]).then_inc(moe_done, 1)

        @block.scalar
        def _(act):
            fn = nc.scalar.activation
            steps = [0]

            def link(ins):
                steps[0] += 1
                ins.then_inc(act_step, 1)
                act.wait_ge(act_step, steps[0])

            def split(u):
                landed(act, u)
                if u >= len(H_SLOTS):
                    multiplied(act, u - len(H_SLOTS))
                fn(h_unit(u, True), w_unit(u), ACT.Copy).then_inc(hi_ready, 1)

            act.dma_start(TAB[:, T_ID:T_ID + P], tab[:, T_ID:T_ID + P]).then_inc(ident_in, 16)
            act.dma_start(CV[:], cv).then_inc(cv_in, 16)

            def preload(func):
                fn(S_PRE, TAB[:, T_ID:T_ID + 1], func).then_inc(act_step, 1)
                steps[0] += 1
                act.wait_ge(act_step, steps[0])

            act.wait_ge(ident_in, 16)
            preload(ACT.Sqrt)
            for i in range(TT):
                act.wait_ge(x_in, 16 * TT)
                fn(SQ[:, i, :], X[:, i, :], ACT.Square, accum_out=S_SS[:, i:i + 1]).then_inc(ssq0, 1)
            act.wait_ge(var0, 1)
            fn(S_SD, S_VAR, ACT.Sqrt).then_inc(sd0, 1)
            split(0)
            for a in range(4):
                act.wait_ge(ht_raw, 2 * (a + 1))
                fn(HT_R[:, 2 * a:2 * a + 2, :], HTL[:, 2 * a:2 * a + 2, :], ACT.Copy).then_inc(ht_hi, 1)
                if a == 1:
                    split(1)
            for u in range(2, 10):
                split(u)
            act.wait_ge(lr_full, 1)
            act.wait_ge(cv_in, 16)
            fn(LRT[0:RANK, :], PS[0:RANK, 3, 0:SEQ], ACT.Identity, bias=col(C_BLR, p=RANK)).then_inc(lr_ready, 1)

            def feature_major(i, dst, c, func):
                for half in range(2):
                    u = 2 * i + half
                    act.wait_ge(pj_full[u % NPJ], u // NPJ + 1)
                    for f in range(2):
                        n = 2 * half + f
                        last = fn(dst[half][:, f * SEQ:(f + 1) * SEQ], PS[:, u % NPJ, f * SEQ:(f + 1) * SEQ], func,
                                  bias=col(c + n))
                    last.then_inc(pj_free[u % NPJ], 1)

            act.wait_ge(z_full, 1)
            for h in range(GH):
                fn(TMP[:, h * SEQ:(h + 1) * SEQ], PS[:, 6 + h // 2, (h % 2) * SEQ:(h % 2 + 1) * SEQ], ACT.Identity,
                   bias=col(C_BGATE + h)).then_inc(z_ready, 1)
            split(10)
            act.wait_ge(gate_neg, 1)
            link(fn(W1, W0, ACT.Exp))
            fn(W1, W1, ACT.Ln, bias=1.0).then_inc(gate_sp, 1)
            feature_major(3, [GQT[:, c * BW:(c + 1) * BW] for c in range(2)], C_BQ, ACT.Identity)
            split(11)
            split(12)
            feature_major(4, [GKT[:, c * BW:(c + 1) * BW] for c in range(2)], C_BK, ACT.Identity)
            for a in range(2):
                act.wait_ge(qt_full, a + 1)
                fn(qT[:, 2 * a:2 * a + 2, :], PS[:, 4 + a, :].rearrange("p (k t) -> p k t", k=2), ACT.Copy).then_inc(qt_cp, 1)

            split(13)

            def swa_exp(n):
                ns = (n // (NGRP // TT) + 1) * P
                q = n % 2
                act.wait_ge(sw_max, n + 1)
                for hh in range(HG):
                    fn(SS[:, q, hh, 0:ns], SS[:, q, hh, 0:ns], ACT.Exp, bias=S_NM[q][:, hh:hh + 1],
                       accum_out=S_SUM[q][:, hh:hh + 1])
                fn(S_ES[q], S_DS[q], ACT.Exp).then_inc(sw_exp, 1)

            def swa_pt(n):
                i = n // (NGRP // TT)
                act.wait_ge(sw_t, n + 1)
                fn(PTS[:, n % 2, 0:2, 0:(i + 1) * P],
                   PS[:, 6, :].rearrange("p (h s) -> p h s", h=2)[:, :, 0:(i + 1) * P], ACT.Copy).then_inc(sw_ptA, 1)

            def gr_sigmoid(u):
                n, m = (u - 14) // 2, u % 2
                evacuated(act, u)
                if u >= 16:
                    act.wait_ge(gr_ready, u - 15)
                fn(SIG[:, m * BW:(m + 1) * BW], GR[:, m, n * BW:(n + 1) * BW], ACT.Sigmoid).then_inc(gr_sig, 1)

            def decays():
                v0 = W0.rearrange("p (h t) -> p h t", h=GH)
                b0 = B.rearrange("p (h t) -> p h t", h=GH)
                act.wait_ge(decay_in, 1)
                fn(v0[:, :, 0:P], v0[:, :, 0:P], ACT.Exp, scale=1.0 / TAU)
                fn(v0[:, :, P:SEQ], b0[:, :, P:SEQ], ACT.Exp, scale=1.0 / TAU).then_inc(decay_out, 1)
                for n, w in ((2, W1), (3, W2)):
                    act.wait_ge(decay_in, n)
                    fn(w, w, ACT.Exp, scale=1.0 / TAU).then_inc(decay_out, 1)
                act.wait_ge(decay_in, 4)
                act.wait_ge(decay_out, 1)
                fn(B, TMP, ACT.Exp, scale=1.0 / TAU).then_inc(decay_out, 1)
                act.wait_ge(decay_out, 4)
                fn(TMP, TMP, ACT.Exp, scale=-1.0 / TAU).then_inc(decay_out, 1)

            for n in range(NGRP + 1):
                if 0 <= n - 1:
                    swa_pt(n - 1)
                if n < NGRP:
                    swa_exp(n)
                split(n + 14)
                if n == 1:
                    decays()
                if n >= 5:
                    gr_sigmoid(n + 9)

            def high_t(dst, full, done):
                for a in range(4):
                    act.wait_ge(full, a + 1)
                    fn(dst[:, 2 * a:2 * a + 2, :], PS[:, 4 + a, :].rearrange("p (k t) -> p k t", k=2), ACT.Copy).then_inc(done, 1)

            act.wait_ge(gr_ready, 4)
            feature_major(9, MIX[0:2], C_BGA, ACT.Sigmoid)
            split(23)
            high_t(OB2[0], obt_full, obt_hi)
            split(24)
            feature_major(10, MIX[2:4], C_BGA + 4, ACT.Sigmoid)
            split(25)
            for h in range(GH):
                act.wait_ge(gla_o, h + 1)
                act.wait_ge(gla_sq, TT * h)
                for i in range(TT):
                    fn(PS[:, 3, i * GDV:(i + 1) * GDV], PS[:, 4 + h, i * GDV:(i + 1) * GDV], ACT.Square,
                       accum_out=S_GS[:, TT * h + i:TT * h + i + 1]).then_inc(gla_sq, 1)
            act.wait_ge(gla_var, 1)
            fn(S_GSD, S_GVAR, ACT.Sqrt).then_inc(gla_sd, 1)
            split(26)
            feature_major(11, GB[0:2], C_BGB, ACT.Sigmoid)
            split(27)
            split(28)
            high_t(OA2[0], oat_full, oat_hi)
            feature_major(12, GB[2:4], C_BGB + 4, ACT.Sigmoid)
            for u in range(29, NU - 3):
                split(u)
            for c in range(2):
                act.wait_ge(mix_ready, c + 1)
                fn(MIX2[0][:, 2 * c:2 * c + 2, :].rearrange("p k t -> p (k t)"), MIX[c], ACT.Copy).then_inc(mix_hi, 1)
            split(NU - 3)
            split(NU - 2)
            for c in range(2, 4):
                act.wait_ge(mix_ready, c + 1)
                fn(MIX2[0][:, 2 * c:2 * c + 2, :].rearrange("p k t -> p (k t)"), MIX[c], ACT.Copy).then_inc(mix_hi, 1)
            split(NU - 1)
            preload(ACT.Sqrt)
            for u in range(2 * NB - 4, 2 * NB):
                n, i = (u - 2 * NB + 4) // 2, u % 2
                evacuated(act, u)
                fn(SQ[:, i, n * BW:(n + 1) * BW], X[:, i, n * BW:(n + 1) * BW], ACT.Square,
                   accum_out=S_SQ[:, 2 * i + n:2 * i + n + 1]).then_inc(ssq1, 1)
            act.wait_ge(var1, 1)
            fn(S_SD, S_VAR, ACT.Sqrt).then_inc(sd1, 1)
            for n, i in enumerate((1, 0)):
                act.wait_ge(xn_ready, n + 1)
                fn(XP[0][:, i, :], xn[:, i, :], ACT.Copy).then_inc(xp1, 1)
            act.wait_ge(rp1, 1)
            fn(XP[1][:, 1, :], REST[:, 1, :], ACT.Copy).then_inc(xp2, 1)
            act.wait_ge(rest1, 1)
            fn(XP[1][:, 0, :], REST[:, 0, :], ACT.Copy).then_inc(xp2, 1)
            for i in range(TT):
                act.wait_ge(top_ready, i + 1)
                fn(S_EG[i], S_V8[i][:, 0:TOPK], ACT.Exp, bias=S_NV[i], accum_out=S_ES4[i]).then_inc(eg_ready, 1)
            act.wait_ge(np_ready, 1)
            passes = act.value_load(NBI[0:1, 0:1], min_val=1, max_val=PASSES)
            with act.Fori(0, passes) as b:
                with act.Fori(0, NE) as e:
                    done = b * NE + e
                    act.wait_ge(glu_ready, done + 1)
                    fn(SGM, GLU, ACT.Sigmoid, scale=ALPHA).then_inc(sgm_ready, 1)
                    act.wait_ge(selT_full, done + 1)
                    fn(SELT[0:SLOTS, 0, 0:SEQ], PS[0:SLOTS, 5, 0:SEQ], ACT.Copy).then_inc(selT_a, 1)
                    act.wait_ge(at_full, done + 1)
                    fn(AT, bk(4), ACT.Copy).then_inc(at_ready, 1)
                    act.wait_ge(chunk_used, done * CH + CH)
                    fn(Y, bk(6), ACT.Copy).then_inc(y_ready, 1)
            preload(ACT.Sqrt)
            for i in range(TT):
                for n in range(2):
                    act.wait_ge(xf_ready, 2 * i + n + 1)
                    fn(OUTB[:, i, n * BW:(n + 1) * BW], X[:, i, n * BW:(n + 1) * BW], ACT.Square,
                       accum_out=S_SQ[:, 2 * i + n:2 * i + n + 1]).then_inc(ssqf, 1)
                act.wait_ge(varf, i + 1)
                fn(S_SD[:, i:i + 1], S_VAR[:, i:i + 1], ACT.Sqrt).then_inc(sdf, 1)
                act.wait_ge(rsf, i + 1)
                act.wait_ge(xg_ready, 2 * i + 1)
                fn(OUTB[:, i, 0:BW], X[:, i, 0:BW], ACT.Copy, scale=S_RS[:, i:i + 1]).then_inc(out_a, 1)
                act.wait_ge(out_a, i + 1)
                act.dma_start(out[i * P:(i + 1) * P, 0:BW], OUTB[:, i, 0:BW]).then_inc(out_done, 16)

        @block.vector
        def _(dve):
            v = nc.vector
            steps = [0]

            def link(ins):
                steps[0] += 1
                ins.then_inc(dve_step, 1)
                dve.wait_ge(dve_step, steps[0])

            def mean_eps(ssq, var, n, count_sem, count, done):
                dve.wait_ge(count_sem, count)
                v.tensor_scalar(var, ssq, 1.0 / n, EPS, ALU.mult, ALU.add).then_inc(done, 1)

            def rest(u):
                dve.wait_ge(hi_ready, u + 1)
                v.tensor_tensor(w_unit(u, True), w_unit(u), h_unit(u, True).bitcast(F32), ALU.subtract).then_inc(lo_v, 1)

            mean_eps(S_SS, S_VAR, D, ssq0, TT, var0)
            dve.wait_ge(sd0, 1)
            link(v.reciprocal(S_RS, S_SD))
            dve.wait_ge(ident_in, 16)
            for i in range(TT):
                v.tensor_scalar(DIAG[:, i * P:(i + 1) * P], ident, S_RS[:, i:i + 1], None, ALU.mult).then_inc(diag_ready, 1)
            dve.wait_ge(cv_in, 16)
            dve.wait_ge(rsr_full, 1)
            link(v.tensor_copy(RSR, PS[:, 3, 0:SEQ]))
            for a in range(4):
                dve.wait_ge(xt_full, a + 1)
                for k in range(2 * a, 2 * a + 2):
                    v.scalar_tensor_tensor(HTL[:, k, :], PS[:, 4 + a, (k % 2) * SEQ:(k % 2 + 1) * SEQ],
                                           col(C_GMIX + k), RSR, ALU.mult, ALU.mult).then_inc(ht_raw, 1)
                if a == 3:
                    for n in range(a - 1, a + 1):
                        dve.wait_ge(ht_hi, n + 1)
                        v.tensor_tensor(HT2[1][:, 2 * n:2 * n + 2, :], HTL[:, 2 * n:2 * n + 2, :],
                                        HT_R[:, 2 * n:2 * n + 2, :].bitcast(F32),
                                        ALU.subtract).then_inc(ht_ready, 1)
                if a == 1:
                    rest(0)
            rest(2)
            rest(4)

            def bias_part(part, dst, raw, base, done):
                places = [dst[(base + n) % 3 * NE:((base + n) % 3 + 1) * NE] for n in range(3)]
                if part == 2:
                    v.tensor_copy(places[0], raw).then_inc(done, 1)
                else:
                    link(v.tensor_copy(places[0], raw))
                    link(v.tensor_copy(places[2 - part], places[0]))
                    link(v.tensor_tensor(raw, raw, places[0], ALU.subtract))

            def biases(part):
                dve.wait_ge(be1_in, 16)
                bias_part(part, BE1, BE1R, 0, be1_ready)
                dve.wait_ge(be2_in, 16)
                bias_part(part, BE2, BE2R, 1, be2_ready)

            def token_major(u, dst, w, done=None):
                i = u // 2
                n = BIAS_ROWS.index(BLOCKS[i])
                dve.wait_ge(bias_in[n % 2], 16 * (n // 2 + 1))
                dve.wait_ge(pj_full[u % NPJ], u // NPJ + 1)
                v.tensor_tensor(dst, bk(u % NPJ, w), BRW[:, n % 2, 0:w], ALU.add).then_inc(pj_free[u % NPJ], 1)

            cos = TAB[:, T_COS:T_COS + TT * HALF].rearrange("p (i d) -> p i d", i=TT)
            sin = TAB[:, T_SIN:T_SIN + TT * HALF].rearrange("p (i d) -> p i d", i=TT)

            def rotate(src, dst, n, i, done):
                t1 = SIG[:, 0:n * HALF].rearrange("p (h d) -> p h d", h=n)
                t2 = SIG[:, BW:BW + n * HALF].rearrange("p (h d) -> p h d", h=n)
                c = cos[:, i, :].unsqueeze(1).broadcast_to([P, n, HALF])
                s = sin[:, i, :].unsqueeze(1).broadcast_to([P, n, HALF])
                v.tensor_tensor(t1, src[:, :, 0, :], c, ALU.mult)
                link(v.tensor_tensor(t2, src[:, :, 1, :], s, ALU.mult))
                for d in dst:
                    last = v.tensor_tensor(d[:, :, 0, :], t1, t2, ALU.subtract)
                link(last)
                v.tensor_tensor(t1, src[:, :, 1, :], c, ALU.mult)
                link(v.tensor_tensor(t2, src[:, :, 0, :], s, ALU.mult))
                for d in dst:
                    last = v.tensor_tensor(d[:, :, 1, :], t1, t2, ALU.add)
                last.then_inc(done, 1)
                dve.wait_ge(done, i + 1)

            def rotate_queries(i):
                evacuated(dve, i)
                evacuated(dve, 2 + i)
                rotate(SQ[:, i, :].rearrange("p (h x d) -> p h x d", h=QH, x=2),
                       [SQR[:, i, :].rearrange("p (h x d) -> p h x d", h=QH, x=2)], QH, i, qrot_ready)

            dve.wait_ge(tab_in, 16)
            for u in range(6):
                i, m = u // 2, u % 2
                if i < 2:
                    token_major(u, SQ[:, m, i * BW:(i + 1) * BW], BW)
                else:
                    token_major(u, KVRAW[:, m, :], KVW)
                if u == 3:
                    rotate_queries(0)
                if m and u < 5:
                    rest(u + 5)
            rotate_queries(1)

            def decay_sums():
                dve.wait_ge(gate_sp, 1)
                link(v.scalar_tensor_tensor(W2, TMP, 0.0, W1, ALU.min, ALU.subtract))
                link(v.memset(W0, 1.0))
                link(v.memset(W0.rearrange("p (n t) -> p n t", t=P)[:, :, 0:1], 0.0))
                link(v.tensor_tensor_scan(B, W0, W2, 0.0, ALU.mult, ALU.add))

            def decay_exponents():
                bh = B.rearrange("p (h t) -> p h t", h=GH)
                v.tensor_tensor(W0.rearrange("p (h t) -> p h t", h=GH)[:, :, 0:P],
                                bh[:, :, P - 1:P].broadcast_to([P, GH, P]), bh[:, :, 0:P], ALU.subtract).then_inc(decay_in, 1)
                for w, half in ((W1, 64), (W2, 32)):
                    n = GH * SEQ // (2 * half)
                    wv = w.rearrange("p (n s t) -> p n s t", s=2, t=half)
                    bv = B.rearrange("p (n s t) -> p n s t", s=2, t=half)
                    ref = bv[:, :, 0, half - 1:half].broadcast_to([P, n, half])
                    v.tensor_tensor(wv[:, :, 0, :], ref, bv[:, :, 0, :], ALU.subtract)
                    v.tensor_tensor(wv[:, :, 1, :], bv[:, :, 1, :], ref, ALU.subtract).then_inc(decay_in, 1)
                tv = TMP.rearrange("p (n t) -> p n t", t=32)
                bv = B.rearrange("p (n t) -> p n t", t=32)
                link(v.tensor_tensor(tv, bv, bv[:, :, 15:16].broadcast_to([P, GH * SEQ // 32, 32]), ALU.subtract))
                v.tensor_scalar(TMP, TMP, -CLAMP * TAU, CLAMP * TAU, ALU.max, ALU.min).then_inc(decay_in, 1)

            def decay_products(level):
                if level == 0:
                    for u in range(6, 10):
                        evacuated(dve, u)
                    dve.wait_ge(decay_out, 1)
                    a, q, k = (t.rearrange("p (h t) -> p h t", h=GH) for t in (W0, GQT, GKT))
                    v.tensor_tensor(a[:, :, 0:P], a[:, :, 0:P], k[:, :, 0:P], ALU.mult)
                    v.scalar_tensor_tensor(a[:, :, P:SEQ], a[:, :, P:SEQ], GSCALE, q[:, :, P:SEQ], ALU.mult, ALU.mult).then_inc(gla_ops, 1)
                elif level < 3:
                    w, half = ((W1, 64), (W2, 32))[level - 1]
                    dve.wait_ge(decay_out, level + 1)
                    a, q, k = (t.rearrange("p (n s t) -> p n s t", s=2, t=half) for t in (w, GQT, GKT))
                    v.tensor_tensor(a[:, :, 0, :], a[:, :, 0, :], k[:, :, 0, :], ALU.mult)
                    v.scalar_tensor_tensor(a[:, :, 1, :], a[:, :, 1, :], GSCALE, q[:, :, 1, :], ALU.mult, ALU.mult).then_inc(gla_ops, 1)
                else:
                    dve.wait_ge(decay_out, 5)
                    dve.wait_ge(gla_ops, 3)
                    v.scalar_tensor_tensor(GQT, B, GSCALE, GQT, ALU.mult, ALU.mult).then_inc(gla_ops, 1)
                    v.tensor_tensor(GKT, TMP, GKT, ALU.mult).then_inc(gla_ops, 1)

            for i in range(TT):
                evacuated(dve, 4 + i)
                kd = KD[:, i, :].rearrange("p (h c x d) -> p h c x d", h=2, c=2, x=2)
                rotate(KVRAW[:, i, 0:P].rearrange("p (h x d) -> p h x d", h=2, x=2),
                       [kd[:, :, c] for c in range(2)], 2, i, krot_ready)
            dve.wait_ge(z_ready, GH)
            v.scalar_tensor_tensor(W0, TMP, -1.0, TMP, ALU.mult, ALU.min).then_inc(gate_neg, 1)
            rest(10)
            decay_sums()
            rest(12)
            decay_exponents()
            dve.wait_ge(kt_full, 1)
            v.tensor_copy(KTT[:].rearrange("p g t -> p (g t)"), bk(3)).then_inc(kt_ready, 1)
            for a in range(2, 4):
                dve.wait_ge(qt_full, a + 1)
                v.tensor_copy(qT[:, 2 * a:2 * a + 2, :], PS[:, 4 + a, :].rearrange("p (k t) -> p k t", k=2)).then_inc(qt_ready, 1)

            mask = TAB[:, T_SWA:T_SWA + SEQ]

            def swa_mask(n):
                i, g4 = n // (NGRP // TT), n % (NGRP // TT)
                q, ns = n % 2, (i + 1) * P
                dve.wait_ge(sw_s, n + 1)
                m = (mask[:, P:SEQ] if i == 0 else mask).unsqueeze(1).broadcast_to([P, 2, ns])
                for a in range(2):
                    last = v.scalar_tensor_tensor(SS[:, q, 2 * a:2 * a + 2, 0:ns],
                                                  PS[:, 4 + a, :].rearrange("p (h s) -> p h s", h=2)[:, :, 0:ns],
                                                  QSCALE, m, ALU.mult, ALU.add)
                    last.then_inc(sw_masked, 1)
                dve.wait_ge(sw_masked, 2 * (n + 1))
                link(v.tensor_reduce(S_MX[q], SS[:, q, :, 0:ns], AX_X, ALU.max))
                sink = ROW[:, R_SINK + HG * g4:R_SINK + HG * (g4 + 1)]
                link(v.tensor_tensor(S_MX[q], S_MX[q], sink, ALU.max))
                v.tensor_scalar(S_NM[q], S_MX[q], -1.0, None, ALU.mult)
                v.tensor_tensor(S_DS[q], sink, S_MX[q], ALU.subtract).then_inc(sw_max, 1)

            def swa_pt(n):
                i = n // (NGRP // TT)
                dve.wait_ge(sw_t, n + 1)
                v.tensor_copy(PTS[:, n % 2, 2:4, 0:(i + 1) * P],
                              PS[:, 7, :].rearrange("p (h s) -> p h s", h=2)[:, :, 0:(i + 1) * P]).then_inc(sw_ptV, 1)

            def swa_out(n):
                i, g4 = n // (NGRP // TT), n % (NGRP // TT)
                q = n % 2
                dve.wait_ge(sw_exp, n + 1)
                if n >= 2:
                    dve.wait_ge(sw_out, n - 1)
                link(v.tensor_tensor(S_DEN[q], S_SUM[q], S_ES[q], ALU.add))
                link(v.reciprocal(S_RD[q], S_DEN[q]))
                dve.wait_ge(sw_o, n + 1)
                v.tensor_tensor(SQR[:, i, g4 * HG * HD:(g4 + 1) * HG * HD].rearrange("p (a b d) -> p b a d", a=2, b=2),
                                PS[:, 3, 0:HG * HD].rearrange("p (b a d) -> p b a d", a=2, b=2),
                                S_RD[q].rearrange("p (b a) -> p b a", a=2).unsqueeze(3).broadcast_to([P, 2, 2, HD]),
                                ALU.mult).then_inc(sw_out, 1)

            dve.wait_ge(row_in, 16)
            DECAY_SLOTS = [2, 3, 5, 7]
            for n in range(NGRP + 2):
                u = 10 + n
                evac = u % 2 == 1 and u < 18
                if evac:
                    dst, c = (GV, (u - 10) // 2 * BW) if u < 14 else (GR, (u - 14) // 2 * BW)
                    token_major(u - 1, dst[:, 0, c:c + BW], BW)
                if n - 2 >= 0:
                    swa_out(n - 2)
                if 0 <= n - 1 < NGRP:
                    swa_pt(n - 1)
                if n < NGRP:
                    swa_mask(n)
                if evac:
                    token_major(u, dst[:, 1, c:c + BW], BW)
                if not by_pool(n + 13):
                    rest(n + 13)
                if n in DECAY_SLOTS:
                    decay_products(DECAY_SLOTS.index(n))

            def rest_t(pair, full, done):
                dve.wait_ge(full, 4)
                for a in range(4):
                    hi = pair[0][:, 2 * a:2 * a + 2, :].bitcast(F32)
                    if done is obt_lo:
                        dve.wait_ge(obt_hi, a + 1)
                    else:
                        dve.wait_ge(oat_hi, a + 1)
                    v.tensor_tensor(pair[1][:, 2 * a:2 * a + 2, :], PS[:, 4 + a, :].rearrange("p (k t) -> p k t", k=2), hi,
                                    ALU.subtract).then_inc(done, 1)

            rest_t(OB2, obt_full, obt_lo)
            rest(24)

            dve.wait_ge(gla_zero, 1)
            dve.wait_ge(gla_sc, 1)
            sc = PS[:, 4:8, :]
            v.tensor_copy(PTG[:, :, 0, :], sc[:, :, 0:P])
            tiles = sc[:, :, P:P + SEQ].rearrange("p h (i c) -> p h i c", i=TT)
            v.tensor_copy(PTG[0:64, :, 1:3, 64:128], tiles[0:64, :, :, 0:64])
            for q in range(2):
                s = slice(64 * q, 64 * q + 32)
                v.tensor_copy(PTG[s, :, 1:3, 64 * q + 32:64 * q + 64], tiles[s, :, :, 64:96])
            for q in range(4):
                s = slice(32 * q, 32 * q + 32)
                last = v.tensor_tensor(PTG[s, :, 1:3, 32 * q:32 * q + 32], tiles[s, :, :, 96:128],
                                       TAB[s, T_DIAG:T_DIAG + 32].unsqueeze(1).unsqueeze(1).broadcast_to([32, GH, TT, 32]), ALU.mult)
            last.then_inc(gla_pt, 1)
            mean_eps(S_GS, S_GVAR, GDV, gla_sq, GH * TT, gla_var)
            dve.wait_ge(gla_sd, 1)
            link(v.reciprocal(S_GRS, S_GSD))
            dve.wait_ge(gr_ready, 4)
            for h in range(GH):
                for i in range(TT):
                    g = GR[:, i, h * GDV:(h + 1) * GDV]
                    n = TT * h + i
                    v.scalar_tensor_tensor(g, PS[:, 4 + h, i * GDV:(i + 1) * GDV], S_GRS[:, n:n + 1], g,
                                           ALU.mult, ALU.mult).then_inc(gla_oa, 1)
            rest(26)
            rest(28)
            rest_t(OA2, oat_full, oat_lo)
            rest(30)

            for i in (13, 14):
                for half in range(2):
                    u, c = 2 * i + half, 2 * (i - 13) + half
                    evacuated(dve, 2 * (9 + c // 2) + half)
                    dve.wait_ge(pj_full[u % NPJ], u // NPJ + 1)
                    v.tensor_tensor(MIX[c], bk(u % NPJ), MIX[c], ALU.mult).then_inc(pj_free[u % NPJ], 1)
                biases(i - 13)
                rest(2 * i + 6)

            def mix_rest(c):
                dve.wait_ge(mix_hi, c + 1)
                v.tensor_tensor(MIX2[1][:, 2 * c:2 * c + 2, :].rearrange("p k t -> p (k t)"), MIX[c],
                                MIX2[0][:, 2 * c:2 * c + 2, :].bitcast(F32).rearrange("p k t -> p (k t)"),
                                ALU.subtract).then_inc(mix_lo, 1)

            for i in (15, 16):
                for half in range(2):
                    u, c = 2 * i + half, 2 * (i - 15) + half
                    evacuated(dve, 2 * (11 + c // 2) + half)
                    dve.wait_ge(pj_full[u % NPJ], u // NPJ + 1)
                    v.tensor_tensor(GB[c], bk(u % NPJ), GB[c], ALU.mult).then_inc(pj_free[u % NPJ], 1)
                    evacuated(dve, u)
                    v.tensor_tensor(MIX[c], MIX[c], GB[c], ALU.add).then_inc(mix_ready, 1)
                for half in range(2):
                    mix_rest(2 * (i - 15) + half)
                if i == 15:
                    biases(2)
                    v.memset(Y, 0.0).then_inc(y_ready, 1)
                    rest(36)
            v.memset(SELT[:, 0, 0:SEQ], 0.0).then_inc(selT_a, 1)
            v.memset(SELT[:, 1, 0:SEQ], 0.0).then_inc(selT_b, 1)
            gffn = col(C_GFFN, KT)
            for i in (17, 18):
                for m in range(TT):
                    u = 2 * i + m
                    xs = X[:, m, (i - 17) * BW:(i - 16) * BW]
                    dve.wait_ge(pj_full[u % NPJ], u // NPJ + 1)
                    v.tensor_tensor(xs, bk(u % NPJ), xs, ALU.add).then_inc(pj_free[u % NPJ], 1)
                if i == 18:
                    dve.wait_ge(ssq1, 2 * TT)
                    link(v.tensor_reduce(S_SS, S_SQ.rearrange("p (i n) -> p i n", i=TT), AX_X, ALU.add))
                    v.tensor_scalar(S_VAR, S_SS, 1.0 / D, EPS, ALU.mult, ALU.add).then_inc(var1, 1)
                for a in range(2 * (i - 17), 2 * (i - 16)):
                    dve.wait_ge(xnT_full, a + 1)
                    v.tensor_tensor(xnT[:, 2 * a:2 * a + 2, :], PS[:, 4 + a, :].rearrange("p (k t) -> p k t", k=2),
                                    gffn[:, 2 * a:2 * a + 2].unsqueeze(2).broadcast_to([P, 2, SEQ]), ALU.mult).then_inc(xnT_ready, 1)
            dve.wait_ge(sd1, 1)
            link(v.reciprocal(S_RS, S_SD))

            def norm(i):
                v.tensor_scalar(xn[:, i, :], X[:, i, :], S_RS[:, i:i + 1], None, ALU.mult).then_inc(xn_ready, 1)

            norm(1)
            dve.wait_ge(lg_full, 1)
            for i in range(TT):
                last = v.scalar_tensor_tensor(LG[:, i, :], PS[:, 3 - i, 0:NE], S_RS[:, i:i + 1],
                                              ROW[:, R_ROUTER:R_ROUTER + NE], ALU.mult, ALU.add)
            norm(0)
            link(last)
            for i in range(TT):
                last = v.max(S_V8[i], LG[:, i, :])
            link(last)
            for i in range(TT):
                v.tensor_scalar(S_NV[i], S_V8[i][:, 0:1], -1.0, None, ALU.mult).then_inc(top_ready, 1)
                last = v.max_index(IDX[i][:], S_V8[i], LG[:, i, :])
            link(last)
            for i in range(TT):
                last = v.tensor_copy(S_IF[i], IDX[i][:])
            link(last)
            top = [P, TT, TOPK, NE]
            experts = TAB[:, T_IOTA:T_IOTA + NE].unsqueeze(1).unsqueeze(1).broadcast_to(top)
            indices = SM[:, 114:114 + 8 * TT].rearrange("p (i k) -> p i k", i=TT)[:, :, 0:TOPK]
            link(v.tensor_tensor(OH, experts, indices.unsqueeze(3).broadcast_to(top), ALU.is_equal))
            v.tensor_reduce(MK, OH.rearrange("p i k e -> p i e k"), AX_X, ALU.add).then_inc(mask_ready, 1)
            dve.wait_ge(xp1, 2)
            v.tensor_tensor(REST[:, 0, :], xn[:, 0, :], XP[0][:, 0, :], ALU.subtract).then_inc(rest1, 1)
            dve.wait_ge(mask_ready, 1)
            link(v.tensor_scalar(BIG, MK, -1e6, 1e6, ALU.mult, ALU.add))
            dve.wait_ge(xp2, 2)
            v.tensor_tensor(XP[2][:, 0, :], REST[:, 0, :], XP[1][:, 0, :], ALU.subtract).then_inc(xp3, 1)
            dve.wait_ge(rank_full, 1)
            link(v.tensor_tensor(BIG, BIG, PS[:, 4, 0:TT * NE].rearrange("p (i e) -> p i e", i=TT), ALU.add))
            v.memset(RK[:, :, PASSES * NE:PASSES * NE + 1], 1e6)
            for b in range(PASSES):
                last = v.tensor_scalar(RK[:, :, b * NE:(b + 1) * NE], BIG, float(-b * SLOTS), None, ALU.add)
            link(last)
            iota = TAB[:, T_IOTA:T_IOTA + SLOTS].unsqueeze(1).broadcast_to([P, TT, SLOTS])
            iota2 = TAB[:, T_IOTA:T_IOTA + SLOTS].unsqueeze(1).unsqueeze(1).broadcast_to([P, TT, 2, SLOTS])

            def spread(a):
                return a.broadcast_to([P, a.shape[1], SLOTS])

            def spread2(a):
                return a.unsqueeze(3).broadcast_to([P, TT, 2, SLOTS])

            def hot(a):
                return TAB[0:3 * NE, a].broadcast_to([3 * NE, SLOTS])

            v.tensor_tensor(SEL, iota, spread(RK[:, :, 0:1]), ALU.is_equal).then_inc(sel_ready, 1)
            v.tensor_copy(SELE, hot(slice(T_HOT, T_HOT + 1))).then_inc(sele_ready, 1)
            link(v.tensor_reduce(S_CNT, PS[:, 4, 2 * NE:3 * NE], AX_X, ALU.max))
            link(v.tensor_scalar(S_CMP, TAB[:, T_THR:T_THR + PASSES], S_CNT, None, ALU.is_lt))
            link(v.tensor_reduce(S_NP, S_CMP, AX_X, ALU.add))
            v.tensor_copy(NBI[:], S_NP).then_inc(np_ready, 1)
            x_bank = PS[:, 7, :].rearrange("p (k c) -> p k c", k=KT)
            dve.wait_ge(xg_full, 1)
            v.tensor_tensor(XT, x_bank, spread(gffn.unsqueeze(2)), ALU.mult).then_inc(xt_ready, 1)
            dve.wait_ge(eg_ready, TT)
            for i in range(TT):
                last = v.reciprocal(S_RG[i], S_ES4[i])
            link(last)
            for i in range(TT):
                last = v.tensor_scalar(S_GT[i], S_EG[i], S_RG[i], None, ALU.mult)
            link(last)
            gates = SM[:, 144:144 + 4 * TT].rearrange("p (i k) -> p i k", i=TT)
            link(v.tensor_tensor(OG, OH, gates.unsqueeze(3).broadcast_to(top), ALU.mult))
            link(v.tensor_reduce(GT_, OG.rearrange("p i k e -> p i e k"), AX_X, ALU.add))
            dve.wait_ge(xp3, 1)
            dve.wait_ge(rp2, 1)
            v.memset(LIN, 0.0).then_inc(act_ready, 1)
            dve.wait_ge(np_ready, 1)
            passes = dve.value_load(NBI[0:1, 0:1], min_val=1, max_val=PASSES)
            with dve.Fori(0, passes) as b:
                with dve.Fori(0, NE) as e:
                    done = b * NE + e
                    dve.wait_ge(chunk_used, done * CH + 1)
                    v.tensor_tensor(SEL, iota, spread(RK[:, :, bass.ds(done + 1, 1)]), ALU.is_equal).then_inc(sel_ready, 1)
                    v.tensor_tensor(SELG, iota2, spread2(RK[:, :, bass.ds(done, 1)]), ALU.is_equal).then_inc(selg_raw, 1)
                    v.tensor_copy(SELE, hot(bass.ds(T_HOT + (e + 1) % NE, 1))).then_inc(sele_ready, 1)
                    dve.wait_ge(selg_raw, done + 1)
                    v.tensor_tensor(SELG, SELG, spread2(GT_[:, :, bass.ds(e, 1)]), ALU.mult).then_inc(selg_ready, 1)
                    dve.wait_ge(chunk_used, done * CH + CH1)
                    dve.wait_ge(act_ready, done + 1)
                    v.tensor_scalar(GLU, bk(4), LIMIT, None, ALU.min).then_inc(glu_ready, 1)
                    v.tensor_scalar(LIN, bk(5), -LIMIT, LIMIT, ALU.max, ALU.min).then_inc(u_read, 1)
                    dve.wait_ge(glu_ready, done + 1)
                    dve.wait_ge(u_read, done + 1)
                    v.scalar_tensor_tensor(LIN, LIN, 1.0, GLU, ALU.add, ALU.mult).then_inc(lin_ready, 1)
                    dve.wait_ge(lin_ready, done + 1)
                    dve.wait_ge(sgm_ready, done + 1)
                    v.tensor_tensor(LIN, LIN, SGM, ALU.mult).then_inc(act_ready, 1)
                    dve.wait_ge(xg_full, done + 2)
                    v.tensor_tensor(XT, x_bank, spread(gffn.unsqueeze(2)), ALU.mult).then_inc(xt_ready, 1)
                    dve.wait_ge(selT_full, done + 1)
                    v.tensor_copy(SELT[SLOTS:P, 1, 0:SEQ], PS[SLOTS:P, 5, 0:SEQ]).then_inc(selT_b, 1)
            dve.wait_ge(gfin_in, 16)
            for i in range(TT):
                dve.wait_ge(moe_done, i + 1)
                for n in range(2):
                    xs = X[:, i, n * BW:(n + 1) * BW]
                    v.tensor_tensor(xs, bk(2 * i + n), xs, ALU.add).then_inc(xf_ready, 1)
                for n in range(2):
                    dve.wait_ge(ssqf, 2 * i + n + 1)
                    xs = X[:, i, n * BW:(n + 1) * BW]
                    if n == 1:
                        link(v.tensor_tensor(S_SS[:, i:i + 1], S_SQ[:, 2 * i:2 * i + 1], S_SQ[:, 2 * i + 1:2 * i + 2], ALU.add))
                        v.tensor_scalar(S_VAR[:, i:i + 1], S_SS[:, i:i + 1], 1.0 / D, EPS, ALU.mult, ALU.add).then_inc(varf, 1)
                    v.tensor_tensor(xs, xs, SIG[:, n * BW:(n + 1) * BW], ALU.mult).then_inc(xg_ready, 1)
                dve.wait_ge(sdf, i + 1)
                v.reciprocal(S_RS[:, i:i + 1], S_SD[:, i:i + 1]).then_inc(rsf, 1)
                dve.wait_ge(rsf, i + 1)
                dve.wait_ge(xg_ready, 2 * i + 2)
                v.tensor_scalar(OUTB[:, i, BW:D], X[:, i, BW:D], S_RS[:, i:i + 1], None, ALU.mult).then_inc(out_ready, 1)


def kernel(**inputs):
    import concourse.bacc as bacc
    from concourse.bass_utils import run_bass_kernel_spmd

    f = {k: np.asarray(a) for k, a in inputs.items()}
    x = f["x"].reshape(SEQ, D)
    w_in, b_in = f["w_in"][0], f["b_in"][0]
    at = {}
    off = 0
    for name, size in (("gq", 512), ("gk", 512), ("gv", 1024), ("gr", 1024), ("lr", 16), ("sq", 1024),
                       ("sk", 128), ("sv", 128), ("ga", 1024), ("gb", 1024)):
        at[name] = off
        off += size

    def units(w):
        return w.reshape(2, KH, P, -1).transpose(0, 2, 1, 3).reshape(2, P, -1)

    def columns(name):
        if name[:2] in ("gl", "sw", "wo"):
            w = f[{"gl": "w_gla_out", "sw": "w_swa_out", "wo": "w_out"}[name[:2]]][0]
            n = int(name[-1]) * BW
            return w[:, n:n + BW]
        n = at[name[:2]] + (int(name[2]) * BW if len(name) > 2 else 0)
        return w_in[:, n:n + BW]

    def feature_columns(a):
        return a.reshape(-1, P).T

    s0 = at["sk"]
    lr0 = at["lr"]
    cv = np.zeros((P, NCV), np.float32)
    for c, a in ((C_GMIX, f["g_mix"][0]), (C_BQ, b_in[at["gq"]:at["gq"] + 512]), (C_BK, b_in[at["gk"]:at["gk"] + 512]),
                 (C_BGA, b_in[at["ga"]:at["ga"] + D]), (C_BGB, b_in[at["gb"]:at["gb"] + D]),
                 (C_BGATE, f["b_gla_gate"][0]), (C_GFFN, f["g_ffn"][0])):
        cv[:, c:c + a.size // P] = feature_columns(a)
    cv[0:RANK, C_BLR] = b_in[lr0:lr0 + RANK]
    brow = np.zeros((len(BIAS_ROWS), BW), np.float32)
    for n, name in enumerate(BIAS_ROWS):
        if name == "skv":
            brow[n, 0:KVW] = b_in[s0:s0 + KVW]
        else:
            c = at[name[:2]] + int(name[2]) * BW
            brow[n] = b_in[c:c + BW]
    sinks = f["sinks"][0].reshape(QH // HG, 2, 2).transpose(0, 2, 1).reshape(-1)
    rows = np.concatenate([sinks, f["g_gla_head"][0], f["b_router"][0]])[None, :]
    w1 = f["w_e1"][0].reshape(NE, KT, P, D, 2).transpose(0, 1, 2, 4, 3).reshape(NE, CH1, P, SLOTW)
    w2 = f["w_e2"][0].reshape(NE, CH2, 2, P, D).transpose(0, 1, 3, 2, 4).reshape(NE, CH2, P, SLOTW)
    arrays = {
        "x": x,
        "wblk": np.concatenate([units(columns(n)) for n in BLOCKS if n != "skv"]),
        "wskv": units(np.concatenate([w_in[:, s0:s0 + KVW], w_in[:, lr0:lr0 + RANK],
                                      np.zeros((D, SKVW - KVW - RANK), np.float32)], axis=1)),
        "wgate": f["w_gla_gate"][0],
        "cv": cv,
        "rows": rows,
        "brow": brow,
        "tab": tables(),
        "wrout": f["w_router"][0].reshape(KT, P, NE).transpose(1, 0, 2),
        "be1": f["b_e1"][0].reshape(NE, D, 2).transpose(0, 2, 1).reshape(NE, 2 * D),
        "be2": f["b_e2"][0],
        "gfin": f["g_final"][None, :],
        "wexp": np.concatenate([w1, w2], axis=1).reshape(NE * CH, P, SLOTW),
    }
    arrays = {k: np.ascontiguousarray(a) for k, a in arrays.items()}
    nc = bacc.Bacc("TRN2", target_bir_lowering=False, num_devices=1)
    args = [nc.dram_tensor(k, a.shape, F32, kind="ExternalInput").ap() for k, a in arrays.items()]
    out = nc.dram_tensor("out", (SEQ, D), F32, kind="ExternalOutput").ap()
    program(nc, *args, out)
    res = run_bass_kernel_spmd(nc, [arrays], core_ids=[0])
    return res.results[0]["out"].reshape(1, SEQ, D)
```
